# Optimizing a Trainium2 kernel written in Bass

```python
import jax, jax.numpy as jnp
from jax import lax
import numpy as np

D_MODEL = 1024
BATCH = 1
SEQ = 128
DEPTH = 2
DEC_BATCH = 1
DEC_SEQ = 512
PAST_LEN = 128

GRID_W = 64
N_HEADS = 8
N_KV_HEADS = 2
HEAD_DIM = 64
ATTN_WIDTH = N_HEADS * HEAD_DIM
KV_WIDTH = N_KV_HEADS * HEAD_DIM
ROPE_AXIS_DIM = HEAD_DIM // 2
ROPE_BASE = 10000.0
Q_BLOCK = 128
POOL_WINDOWS = (2, 4, 8, 16)
N_POOL_GROUPS = 4
POOL_GROUP_DIM = 64
POOL_WIDTH = N_POOL_GROUPS * POOL_GROUP_DIM
N_FOURIER_GROUPS = 4
FOURIER_GROUP_DIM = 64
FOURIER_WIDTH = N_FOURIER_GROUPS * FOURIER_GROUP_DIM
N_BRANCHES = 3
SPLIT_POINTS = (ATTN_WIDTH,
                ATTN_WIDTH + KV_WIDTH,
                ATTN_WIDTH + 2 * KV_WIDTH,
                ATTN_WIDTH + 2 * KV_WIDTH + POOL_WIDTH,
                ATTN_WIDTH + 2 * KV_WIDTH + POOL_WIDTH + FOURIER_WIDTH)
IN_WIDTH = SPLIT_POINTS[-1] + N_BRANCHES * D_MODEL
N_EXPERT_GROUPS = 4
EXPERTS_PER_GROUP = 8
N_EXPERTS = N_EXPERT_GROUPS * EXPERTS_PER_GROUP
TOP_K = 2
EXPERT_FF = 256
MOE_BLOCK = 128
N_MOD = 6
RMS_EPS = 1e-6

kernel_name = "hybrid_diffusion_prefix_trunk_step"

def rmsnorm(x, g):
    xf = x.astype(jnp.float32)
    y = xf * lax.rsqrt(jnp.mean(xf * xf, axis=-1, keepdims=True) + RMS_EPS)
    return (y * g.astype(jnp.float32)).astype(x.dtype)

def grid_rope(L):
    rows = L // GRID_W
    row = jnp.repeat(jnp.arange(rows), GRID_W).astype(jnp.float32)
    col = jnp.tile(jnp.arange(GRID_W), rows).astype(jnp.float32)
    n_freq = ROPE_AXIS_DIM // 2
    inv = ROPE_BASE ** (-jnp.arange(n_freq, dtype=jnp.float32) * 2.0 / ROPE_AXIS_DIM)
    ang = jnp.stack([row[:, None] * inv, col[:, None] * inv], axis=1)
    return jnp.cos(ang), jnp.sin(ang)

def apply_rope(x, cos, sin):
    B, L, H, hd = x.shape
    xr = x.astype(jnp.float32).reshape(B, L, H, 2, 2, ROPE_AXIS_DIM // 2)
    x1 = xr[..., 0, :]
    x2 = xr[..., 1, :]
    c = cos[None, :, None]
    s = sin[None, :, None]
    out = jnp.stack([x1 * c - x2 * s, x2 * c + x1 * s], axis=-2)
    return out.reshape(B, L, H, hd).astype(x.dtype)

def attend(q, k, v):
    B, Lq, H, hd = q.shape
    KV = k.shape[2]
    G = H // KV
    nb = Lq // Q_BLOCK
    qb = q.reshape(B, nb, Q_BLOCK, KV, G, hd).transpose(1, 0, 2, 3, 4, 5)
    scale = hd ** -0.5

    def one_block(q_blk):
        s = jnp.einsum('bqkgd,bskd->bkgqs', q_blk, k,
                       preferred_element_type=jnp.float32) * scale
        p = jax.nn.softmax(s, axis=-1)
        return jnp.einsum('bkgqs,bskd->bqkgd', p.astype(v.dtype), v)

    o = lax.map(one_block, qb)
    return o.transpose(1, 0, 2, 3, 4, 5).reshape(B, Lq, H * hd)

def multiscale_pool(xp, w_group, scale):
    B, L, _ = xp.shape
    xg = xp.reshape(B, L, N_POOL_GROUPS, POOL_GROUP_DIM).astype(jnp.float32)
    csum = jnp.concatenate([jnp.zeros((B, 1, N_POOL_GROUPS, POOL_GROUP_DIM), jnp.float32),
                            jnp.cumsum(xg, axis=1)], axis=1)
    t = jnp.arange(L)
    outs = []
    for g, w in enumerate(POOL_WINDOWS):
        lo = jnp.clip(t - w // 2, 0, L)
        hi = jnp.clip(t + w // 2, 0, L)
        cnt = (hi - lo).astype(jnp.float32)
        window_sum = csum[:, hi, g] - csum[:, lo, g]
        outs.append(window_sum / cnt[None, :, None] - xg[:, :, g])
    pooled = jnp.stack(outs, axis=2).astype(xp.dtype)
    mixed = jnp.einsum('blgc,gcd->blgd', pooled, w_group)
    return mixed.reshape(B, L, POOL_WIDTH) * scale

def fourier_mix(xf):
    B, L, _ = xf.shape
    xg = xf.reshape(B, L, N_FOURIER_GROUPS, FOURIER_GROUP_DIM).astype(jnp.float32)
    y = jnp.fft.fft2(xg, axes=(1, 3), norm="ortho").real
    return y.reshape(B, L, FOURIER_WIDTH).astype(xf.dtype)

def mixing(h, lp, latent_ctx):
    B, L, _ = h.shape
    proj = h @ lp["w_in"]
    q, k, v, xp, xf, gts = jnp.split(proj, SPLIT_POINTS, axis=-1)
    q = rmsnorm(q.reshape(B, L, N_HEADS, HEAD_DIM), lp["q_norm"])
    k = rmsnorm(k.reshape(B, L, N_KV_HEADS, HEAD_DIM), lp["k_norm"])
    v = v.reshape(B, L, N_KV_HEADS, HEAD_DIM)
    if latent_ctx is None:
        k_all, v_all = k, v
    else:
        ctx_k, ctx_v, cos, sin = latent_ctx
        q = apply_rope(q, cos, sin)
        k_all = jnp.concatenate([ctx_k.astype(k.dtype), apply_rope(k, cos, sin)], axis=1)
        v_all = jnp.concatenate([ctx_v.astype(v.dtype), v], axis=1)
    attn = attend(q, k_all, v_all) @ lp["w_attn_out"]
    pool = multiscale_pool(xp, lp["w_pool_group"], lp["pool_scale"]) @ lp["w_pool_out"]
    four = fourier_mix(xf) @ lp["w_fourier_out"]
    g = jax.nn.sigmoid(gts.reshape(B, L, N_BRANCHES, D_MODEL))
    merged = g[:, :, 0] * attn + g[:, :, 1] * pool + g[:, :, 2] * four
    return merged @ lp["w_out"], k, v

def hierarchical_moe(h, lp):
    N, D = h.shape
    lg = (h @ lp["w_router_group"]).astype(jnp.float32) + lp["b_router_group"].astype(jnp.float32)
    p_group = jax.nn.softmax(lg, axis=-1)
    g_sel = jnp.argmax(lg, axis=-1)
    p_g_sel = jnp.take_along_axis(p_group, g_sel[:, None], axis=-1)
    le = ((h @ lp["w_router_expert"]).astype(jnp.float32)
          + lp["b_router_expert"].astype(jnp.float32)).reshape(N, N_EXPERT_GROUPS, EXPERTS_PER_GROUP)
    le_sel = jnp.take_along_axis(le, g_sel[:, None, None], axis=1)[:, 0]
    top_v, top_i = lax.top_k(le_sel, TOP_K)
    expert_idx = g_sel[:, None] * EXPERTS_PER_GROUP + top_i
    expert_w = p_g_sel * jax.nn.softmax(top_v, axis=-1)

    A = N * TOP_K
    flat_e = expert_idx.reshape(-1).astype(jnp.int32)
    flat_w = expert_w.reshape(-1)
    flat_tok = jnp.repeat(jnp.arange(N, dtype=jnp.int32), TOP_K)
    order = jnp.argsort(flat_e)
    sorted_e = flat_e[order]
    counts = jnp.bincount(flat_e, length=N_EXPERTS)
    padded = ((counts + MOE_BLOCK - 1) // MOE_BLOCK) * MOE_BLOCK
    pad_end = jnp.cumsum(padded)
    pad_start = pad_end - padded
    start = jnp.cumsum(counts) - counts
    dest = pad_start[sorted_e] + (jnp.arange(A) - start[sorted_e])
    n_blocks = (A + N_EXPERTS * (MOE_BLOCK - 1) + MOE_BLOCK - 1) // MOE_BLOCK
    rows = n_blocks * MOE_BLOCK
    row_tok = jnp.full((rows,), N, jnp.int32).at[dest].set(flat_tok[order])
    row_w = jnp.zeros((rows,), jnp.float32).at[dest].set(flat_w[order]).astype(h.dtype)
    block_expert = jnp.minimum(
        jnp.searchsorted(pad_end, jnp.arange(n_blocks) * MOE_BLOCK, side='right'), N_EXPERTS - 1)
    h_pad = jnp.concatenate([h, jnp.zeros((1, D), h.dtype)], axis=0)
    xs = h_pad[row_tok].reshape(n_blocks, MOE_BLOCK, D)
    w_gate, w_up, w_down = lp["w_expert_gate"], lp["w_expert_up"], lp["w_expert_down"]

    def expert_block(args):
        xb, e = args
        return (jax.nn.silu(xb @ w_gate[e]) * (xb @ w_up[e])) @ w_down[e]

    y = lax.map(expert_block, (xs, block_expert)).reshape(rows, D) * row_w[:, None]
    return jax.ops.segment_sum(y, row_tok, num_segments=N + 1)[:N]

def trunk_layer(x, mod, lp, latent_ctx):
    sh1, sc1, g1, sh2, sc2, g2 = jnp.split(mod.astype(x.dtype), N_MOD, axis=-1)
    h = rmsnorm(x, lp["norm_mix_pre"]) * (1 + sc1) + sh1
    mix, k, v = mixing(h, lp, latent_ctx)
    x = x + g1 * rmsnorm(mix, lp["norm_mix_post"])
    B, L, D = x.shape
    h = rmsnorm(x, lp["norm_ffn_pre"]) * (1 + sc2) + sh2
    ffn = hierarchical_moe(h.reshape(B * L, D), lp).reshape(B, L, D)
    x = x + g2 * rmsnorm(ffn, lp["norm_ffn_post"])
    return x, k, v

def setup_inputs(seed: int = 0) -> dict:
    key = jax.random.key(seed)
    ks = iter(jax.random.split(key, 40))
    f32 = jnp.float32

    def nrm(shape, s):
        return jax.random.normal(next(ks), shape, f32) * s

    def gain(shape):
        return 1.0 + 0.1 * jax.random.normal(next(ks), shape, f32)

    D = D_MODEL
    return {
        "x_prompt": nrm((BATCH, SEQ, D), 1.0),
        "x_sample": nrm((DEC_BATCH, DEC_SEQ, D), 1.0),
        "cache_k": nrm((DEC_BATCH, DEPTH, PAST_LEN, N_KV_HEADS, HEAD_DIM), 1.0),
        "cache_v": nrm((DEC_BATCH, DEPTH, PAST_LEN, N_KV_HEADS, HEAD_DIM), 1.0),
        "c": nrm((DEC_BATCH, D), 1.0),
        "c_ctx": nrm((D,), 1.0),
        "w_ada": nrm((DEPTH, D, N_MOD * D), 0.2 * D ** -0.5),
        "b_ada": nrm((DEPTH, N_MOD * D), 0.02),
        "norm_mix_pre": gain((DEPTH, D)),
        "norm_mix_post": gain((DEPTH, D)),
        "norm_ffn_pre": gain((DEPTH, D)),
        "norm_ffn_post": gain((DEPTH, D)),
        "w_in": nrm((DEPTH, D, IN_WIDTH), D ** -0.5),
        "q_norm": gain((DEPTH, HEAD_DIM)),
        "k_norm": gain((DEPTH, HEAD_DIM)),
        "w_attn_out": nrm((DEPTH, ATTN_WIDTH, D), ATTN_WIDTH ** -0.5),
        "w_pool_group": nrm((DEPTH, N_POOL_GROUPS, POOL_GROUP_DIM, POOL_GROUP_DIM), POOL_GROUP_DIM ** -0.5),
        "pool_scale": gain((DEPTH, POOL_WIDTH)),
        "w_pool_out": nrm((DEPTH, POOL_WIDTH, D), POOL_WIDTH ** -0.5),
        "w_fourier_out": nrm((DEPTH, FOURIER_WIDTH, D), FOURIER_WIDTH ** -0.5),
        "w_out": nrm((DEPTH, D, D), D ** -0.5),
        "w_router_group": nrm((DEPTH, D, N_EXPERT_GROUPS), D ** -0.5),
        "b_router_group": nrm((DEPTH, N_EXPERT_GROUPS), 0.01),
        "w_router_expert": nrm((DEPTH, D, N_EXPERTS), D ** -0.5),
        "b_router_expert": nrm((DEPTH, N_EXPERTS), 0.01),
        "w_expert_gate": nrm((DEPTH, N_EXPERTS, D, EXPERT_FF), D ** -0.5),
        "w_expert_up": nrm((DEPTH, N_EXPERTS, D, EXPERT_FF), D ** -0.5),
        "w_expert_down": nrm((DEPTH, N_EXPERTS, EXPERT_FF, D), EXPERT_FF ** -0.5),
    }

def reference(x_prompt, x_sample, cache_k, cache_v, c, c_ctx, w_ada, b_ada,
              norm_mix_pre, norm_mix_post, norm_ffn_pre, norm_ffn_post, w_in, q_norm, k_norm,
              w_attn_out, w_pool_group, pool_scale, w_pool_out, w_fourier_out, w_out,
              w_router_group, b_router_group, w_router_expert, b_router_expert,
              w_expert_gate, w_expert_up, w_expert_down):
    cos, sin = grid_rope(x_sample.shape[1])
    silu_ctx = jax.nn.silu(c_ctx)
    silu_c = jax.nn.silu(c)
    xp_stream = x_prompt
    xs_stream = x_sample
    new_k, new_v = [], []
    for l in range(DEPTH):
        lp = dict(w_in=w_in[l], q_norm=q_norm[l], k_norm=k_norm[l], w_attn_out=w_attn_out[l],
                  w_pool_group=w_pool_group[l], pool_scale=pool_scale[l], w_pool_out=w_pool_out[l],
                  w_fourier_out=w_fourier_out[l], w_out=w_out[l],
                  norm_mix_pre=norm_mix_pre[l], norm_mix_post=norm_mix_post[l],
                  norm_ffn_pre=norm_ffn_pre[l], norm_ffn_post=norm_ffn_post[l],
                  w_router_group=w_router_group[l], b_router_group=b_router_group[l],
                  w_router_expert=w_router_expert[l], b_router_expert=b_router_expert[l],
                  w_expert_gate=w_expert_gate[l], w_expert_up=w_expert_up[l],
                  w_expert_down=w_expert_down[l])
        mod_ctx = (silu_ctx @ w_ada[l] + b_ada[l])[None, None, :]
        xp_stream, k_ctx, v_ctx = trunk_layer(xp_stream, mod_ctx, lp, None)
        new_k.append(k_ctx)
        new_v.append(v_ctx)
        mod_lat = (silu_c @ w_ada[l] + b_ada[l])[:, None, :]
        xs_stream, _, _ = trunk_layer(xs_stream, mod_lat, lp,
                                      (cache_k[:, l], cache_v[:, l], cos, sin))
    new_cache_k = jnp.stack(new_k, axis=1)
    new_cache_v = jnp.stack(new_v, axis=1)
    return (xp_stream, xs_stream, new_cache_k, new_cache_v)


_drawn_inputs = setup_inputs


def setup_inputs(seed=0):
    import zlib

    import numpy as np

    out = dict(_drawn_inputs(seed))
    spreads = {}
    factors = {'cache_k': 5.846,
     'cache_v': 4.248,
     'q_norm': 8.0,
     'pool_scale': 2.81,
     'b_router_group': 3.622,
     'b_router_expert': 5.188}
    for name, (base, spread) in spreads.items():
        noise = np.random.default_rng([zlib.crc32(name.encode()), seed]).standard_normal(out[name].shape)
        drawn = base * np.exp(spread * noise) if base else spread * noise
        out[name] = __import__('jax').numpy.asarray(drawn.astype(out[name].dtype))
    for name, factor in factors.items():
        out[name] = (out[name] * factor).astype(out[name].dtype)
    return out
```

```python
import concourse.bass as bass
from concourse import mybir
from contextlib import ExitStack

F32 = mybir.dt.float32
I32 = mybir.dt.int32
ALU = mybir.AluOpType
ACT = mybir.ActivationFunctionType
AX = mybir.AxisListType

P = 128
D = 1024
DK = D // P
DEPTH = 2
CTX, LAT = 128, 512
TOK = CTX + LAT
NT = TOK // P
LT = LAT // P
NH, NKV, HD = 8, 2, 64
QW, KW = NH * HD, NKV * HD
NHEADS = NH + NKV
POOLW = FOURW = 256
IN_W = QW + 2 * KW + POOLW + FOURW + 3 * D
KEYS = P + LAT
KALL = KEYS + CTX
SCALE = float(HD) ** -0.5
NG, EPG = 4, 8
NE = NG * EPG
NR = NG + NE
FF = 256
BLK = 64
XBLK = TOK // BLK - 1
EPS = 1e-6
BIG = 1e30
POOL_PAD = 8

C_ID, C_ONE, C_TRI, C_CC, C_CS, C_XC, C_XS = (i * P for i in range(7))
C_EDGE = 7 * P
C_WINV = C_EDGE + 32
C_EID = C_WINV + 2
C_REV = C_EID + NE
C_SEL = C_REV + NE
C_HALF = C_SEL + 2
NCONST = C_HALF + 1
V_BADA, V_MPRE, V_MPOST, V_FPRE, V_FPOST, V_PS = 0, 48, 56, 64, 72, 80
NVEC = 82

CHUNKS = ([("ada", c, 1) for c in range(12)] + [("q", 0, 1), ("kvx", 0, 2), ("xp", 0, 1),
          ("cos", 0, 1), ("sin", 0, 1)] + [("gate", c, 1) for c in range(6)] +
          [("ao", 0, 2), ("pf", 0, 2), ("wo", 0, 1), ("wo", 1, 1)])
WSLOTS = 3
assert len(CHUNKS) % WSLOTS == 0
CHUNK_AT = {(n, i): c for c, (n, i, _) in enumerate(CHUNKS)}

USES = []
for _s in range(6):
    USES.append(("ada", _s, _s % 2, 1))
USES.append(("adacol", 0, 2, 1))
USES += [("hT", k, k % 4, 1) for k in range(DK)]
for _i in range(NT):
    USES.append(("qkv", _i, _i % 2, 1))
    if _i:
        USES.append(("qkT", _i - 1, 2 + (_i - 1) % 2, 1))
USES.append(("qkT", NT - 1, 2, 1))
USES.append(("qkT", NT, 3, 1))
USES += [("xp", c, c, 1) for c in range(2)]
USES += [("dft", j, (2 + j) % 4, 1) for j in range(4)]
USES += [("plin", c, 2 + c, 1) for c in range(2)]
USES += [("four", c, c, 1) for c in range(2)]
USES.append(("ctxS", 0, 2, 1))
NGATE = 3 * DK


def attention_steps():
    steps = [("ctxS", 0), ("gates", 0)]
    steps += [("ctxT", 0), ("gates", 1), ("ctxO", 0)]
    g = 2
    for h in range(NH):
        for t in range(LT):
            steps.append(("S", (h, t)))
            if g < NGATE:
                steps.append(("gates", g))
                g += 1
        steps.append(("PV", h))
    return steps


STEPS = attention_steps()
USES = [u for u in USES if u[0] != "ctxS"]
for _n, _x in STEPS:
    if _n == "gates":
        USES.append(("gate", _x, _x % 2, 1))
    elif _n == "S":
        USES.append(("S", _x, 2, 1))
    elif _n == "ctxS":
        USES.append(("ctxS", 0, 2, 1))
    elif _n == "ctxT":
        USES.append(("ctxT", 0, 3, 1))
    elif _n == "ctxO":
        USES.append(("ctxO", 0, 2, 1))
for _d in range(DK):
    USES += [(b, _d, (3 * _d + j) % 4, 1) for j, b in enumerate(("mattn", "mpool", "mfour"))]
USES += [("bc", v, v % 4, 1) for v in range(8)]
for _i in range(NT):
    USES.append(("mix", _i, _i % 2, 1))
    if _i:
        USES.append(("h2T", _i - 1, 2 + (_i - 1) % 2, 1))
USES += [("h2T", NT - 1, 2, 1), ("lg", 0, 3, 1), ("pos", 0, 0, 1)]


class Pairs:

    def __init__(self):
        self.at, self.full, self.free = {}, [0] * 4, [0] * 4
        for name, i, p, drains in USES:
            self.at[name, i] = (p, self.full[p], self.free[p])
            self.full[p] += 1
            self.free[p] += drains


PAIRS = Pairs()

PER = dict(
    dve_step=0, act_step=0, pool_step=0, ada_half=6, ada_cols=6, affine_ready=1, x_sumsq=NT,
    rstd1=1, xn_ready=1, qk_raw=NT, qk_sq=NT, qk_rstd=NT, qk_rot=NT, pooled=2, cprob=1, cpn=1,
    smax=LT * NH, pnorm=LT * NH, tr_full=5 * NH, ptT=5 * NH, pv_full=NH, o_ready=NH, merged=DK,
    mix_sq=NT, mix_rstd=NT, x_mid=NT, x2_sq=NT, x2_rstd=NT, h_a=NT, h_b=NT, h_sent0=48, h_sent1=32, wr_in=16,
    sel_in=1, sel_exp=1, mask_ready=1, slots_ready=1, table_clear=16, table_set=16 * 2 * NT,
    table_read=32, ids_step=4, y_scaled=NT, y_sum=NT, y_sq=NT, y_rstd=NT, x_end=NT, layer_in=160, kv_out=32,
    xg_zero=1,
)


def trunk_kernel(nc, A, CH):
    ctx = ExitStack()
    with ctx:
        def sb(name, shape, dt=F32):
            return ctx.enter_context(nc.sbuf_tensor(name, shape, dt))

        def sem(name):
            return ctx.enter_context(nc.semaphore(name))

        X = sb("x_rows", [P, NT, D])
        HT = sb("h_T", [P, DK * TOK])
        G = sb("gates_mem", [P, NGATE * TOK])
        W = sb("w_ring", [P, WSLOTS, 4096])
        R = sb("attn_mem", [P, 13568])
        CON = sb("consts", [P, NCONST])
        VEC = sb("vectors", [P, NVEC])
        SILU = sb("silu_c", [P, DK, 32])
        MOD = sb("mod", [P, 6, DK, 2])
        AFF = sb("affine", [P, 4, DK, 2])
        ST = sb("stats", [P, 6, NT])

        hT = HT[:, :].rearrange("p (k t) -> p k t", k=DK)

        def cut(t, at, shape):
            n = 1
            for s in shape:
                n *= s
            v = t[:, at:at + n]
            if len(shape) == 1:
                return v
            names = "abcd"[:len(shape)]
            spec = " ".join(names)
            return v.rearrange(f"p ({spec}) -> p {spec}", **{c: s for c, s in zip(names[1:], shape[1:])})

        xn = cut(G, 0, (NT, D))
        AB = cut(G, 0, (4, TOK))
        PL = LAT + CTX + 4 * POOL_PAD
        pS = [cut(G, 4 * TOK + i * PL, (PL,)) for i in range(3)]
        XF = cut(G, 5120, (NT, FOURW))
        xpT = cut(G, 6400, (2, PL))
        qraw = cut(G, 7744, (2, 640))
        qsq = cut(G, 9024, (640,))
        qa = cut(G, 9664, (640,))
        qb = cut(G, 10304, (640,))
        qrot = cut(G, 10944, (2, 640))
        ROPE = cut(G, 12224, (2, LT, HD))
        GAIN = cut(G, 12736, (640,))
        pooled = cut(G, 9664, (2, TOK))
        qst = cut(G, 13376, (4, NHEADS))
        kc = cut(G, 13416, (KW,))
        WPG = cut(G, 13544, (2, P))
        TG = cut(G, 0, (3, DK, TOK))
        EW = [cut(G, e * 6144, (6144,)) for e in range(2)]
        wgu = [EW[e][:, 0:4096].rearrange("p (u k f) -> p u k f", u=2, k=DK) for e in range(2)]
        wdn = [EW[e][:, 4096:6144].rearrange("p (c n) -> p c n", c=2) for e in range(2)]
        qT = cut(R, 0, (4, TOK))
        kT = cut(R, 2560, (2, KALL))
        V = cut(R, 4096, (NT + 1, KW))
        PR = cut(R, 4864, (LT, KEYS))
        PT = cut(R, 7424, (2, 512))
        OT = cut(R, 8448, (4, TOK))
        PM = cut(R, 11008, (2, TOK))
        FM = cut(R, 12288, (2, TOK))
        part = cut(R, 0, (2, D))
        cP = cut(R, 4864, (NH, P))
        cPT = cut(R, 7424, (NH, P))
        aST = sb("attn_stats", [P, 3, 8])
        ROW = cut(R, 0, (8, D))
        hrow = cut(R, 8192, (2, D))
        tmix = cut(R, 10240, (2, D))
        rt = [cut(R, 10240 + 160 * i, (NT, NE)) for i in range(10)]
        WR = cut(G, 12288, (DK, NR))
        junk = cut(R, 12288, (D,))
        yg = cut(R, 8192, (2, 2, D))
        xg = cut(HT, 0, (2, D))
        xT = cut(HT, 2048, (2, DK, BLK))
        GU = cut(HT, 3072, (2, FF))
        th = cut(HT, 3584, (2, BLK))
        hE = cut(HT, 3712, (2, 2, BLK))
        yb = cut(HT, 3968, (2, 512))
        RS = sb("router_small", [P, 8, NT])
        SLOT = sb("slots", [P, 2, NT], I32)
        TID = sb("assignment_ids", [P, 2, NT], I32)
        IDX = cut(G, 13000, (3, NE + 2)).bitcast(I32)
        RB = sb("router_bias", [P, NR])
        MOST = sb("largest_count", [P, 1], I32)
        HALF = sb("minus_half", [P, NHEADS])
        IDC = sb("row_ids_now", [P, 4], I32)
        EX = cut(R, 11840, (2, NT, 5))
        sg = cut(HT, 4992, (2, BLK))

        PS = ctx.enter_context(nc.psum_tensor("ps", [P, 8, 512], F32))

        def bank(b):
            return PS[:, b, :]

        def pair(p):
            return PS[:, 2 * p:2 * p + 2, :].rearrange("p b n -> p (b n)")

        S = {name: sem(name) for name in PER}
        per = dict(PER)
        per.update(CH)
        full = [sem(f"psum_full{p}") for p in range(4)]
        free = [sem(f"psum_free{p}") for p in range(4)]
        loaded = [sem(f"chunk_loaded{s}") for s in range(WSLOTS)]
        const_in = sem("const_in")
        aside = sem("aside")
        f_turn = sem("more_turns")
        silu_a, silu_b = sem("silu_tanh"), sem("silu_ready")
        setup = sem("setup_done")
        done = sem("outputs_stored")
        ex_loaded = [sem(f"expert_loaded{e}") for e in range(2)]
        rows_in = [sem(f"expert_rows{e}") for e in range(2)]
        idc = [sem(f"gather_ids_copied{e}") for e in range(2)]
        idy = [sem(f"scatter_ids_copied{e}") for e in range(2)]
        yg_in = [sem(f"y_gathered{i}") for i in range(2)]
        xT_full, xT_out = sem("ex_xT_full"), sem("ex_xT_out")
        gu_full, gu_out, gt_full = sem("ex_gu_full"), sem("ex_gu_out"), sem("ex_gt_full")
        th_out, sg_out, h_out = sem("ex_tanh"), sem("ex_silu"), sem("ex_h")
        dn_full, y_out = sem("ex_down_full"), sem("ex_y_out")
        y_sent = [sem(f"ex_y_sent{e}") for e in range(2)]
        f_ids, f_step, f_gathered, f_sent = sem("more_ids"), sem("more_ids_step"), sem("more_gathered"), sem("more_sent")
        f_rows, f_loaded, f_done = sem("more_rows_in"), sem("more_weights_in"), sem("more_block_done")
        f_xT, f_xo, f_gu, f_go, f_gt = sem("more_xT"), sem("more_xT_out"), sem("more_gu"), sem("more_gu_out"), sem("more_gt")
        f_th, f_sg, f_h, f_dn, f_y = sem("more_tanh"), sem("more_silu"), sem("more_h"), sem("more_down"), sem("more_y_out")
        count = {"dve_step": 0, "act_step": 0, "pool_step": 0}

        def upto(name, l, n):
            return l * per[name] + n

        chunk_dmas = [[0] for _ in range(WSLOTS)]
        for c, (_, _, n) in enumerate(CHUNKS):
            chunk_dmas[c % WSLOTS].append(chunk_dmas[c % WSLOTS][-1] + 16 * n)

        def chunk(name, i=0):
            c = CHUNK_AT[name, i]
            return c % WSLOTS, chunk_dmas[c % WSLOTS][c // WSLOTS + 1]

        def loaded_at(l, name, i=0):
            s, n = chunk(name, i)
            return loaded[s], l * chunk_dmas[s][-1] + n

        def used_at(l, c):
            name, i, _ = CHUNKS[c]
            if name == "ada" and i % 2 == 0:
                return S["ada_half"], upto("ada_half", l, i // 2 + 1)
            return filled_at(l, *{"ada": ("ada", i // 2), "q": ("qkv", NT - 1), "kvx": ("qkv", NT - 1), "xp": ("xp", 1),
                                  "cos": ("dft", 1), "sin": ("dft", 3), "gate": ("gate", 4 * i + 3),
                                  "ao": ("mattn", DK - 1), "pf": ("mfour", DK - 1), "wo": ("mix", NT - 1)}[name])

        def freed_at(l, name, i):
            p, _, n = PAIRS.at[name, i]
            return free[p], l * PAIRS.free[p] + n + 1

        def filled_at(l, name, i):
            p, n, _ = PAIRS.at[name, i]
            return full[p], l * PAIRS.full[p] + n + 1

        def drained_at(l, name, i):
            p, _, n = PAIRS.at[name, i]
            return free[p], l * PAIRS.free[p] + n + 2

        def pair_of(name, i):
            return PAIRS.at[name, i][0]

        def cols(base):
            return CON[:, base:base + P]

        ident, ones, tri = cols(C_ID), cols(C_ONE), cols(C_TRI)

        def stream(n):
            return slice(0, LAT) if n == 0 else slice(LAT, TOK)

        def further_blocks(eng, l, body, mine):
            eng.wait_ge(S["slots_ready"], upto("slots_ready", l, 1))
            eng.sem_inc(aside, 1)
            most = eng.value_load(MOST[0:1, 0:1], min_val=0, max_val=TOK)
            with eng.Fori(1, XBLK + 1) as b:
                with eng.If(most > b * BLK):
                    with eng.Fori(0, NE) as e:
                        body(b, e, (l * XBLK + b - 1) * NE + e)
                with eng.Else():
                    for s, n in mine:
                        eng.sem_inc(s, n * NE)
                if eng.engine == nc.gpsimd.engine:
                    eng.sem_inc(f_turn, 1)
                else:
                    eng.wait_ge(f_turn, l * XBLK + b)
                    eng.sem_inc(aside, 1)

        block = ctx.enter_context(nc.Block())

        @block.sync
        def _(sp):
            with sp.Fori(0, DEPTH) as l:
                for c, (name, i, _) in enumerate(CHUNKS):
                    s = c % WSLOTS
                    slot = W[:, s, :]
                    if c >= WSLOTS:
                        sp.wait_ge(*used_at(l, c - WSLOTS))
                    k8 = slot.rearrange("p (k n) -> p k n", k=DK)

                    def w_cols(w, a, b):
                        return w[bass.ds(l, 1), :, a:b].rearrange("a (k p) n -> p (a k) n", p=P)

                    if name == "ada":
                        sp.dma_start(k8, w_cols(A["w_ada"], 512 * i, 512 * i + 512)).then_inc(loaded[s], 16)
                    elif name == "q":
                        sp.dma_start(k8, w_cols(A["w_in"], 0, QW)).then_inc(loaded[s], 16)
                    elif name == "kvx":
                        sp.dma_start(k8[:, :, 0:256], w_cols(A["w_in"], QW, QW + 256)).then_inc(loaded[s], 16)
                        sp.dma_start(k8[:, :, 256:512], w_cols(A["w_in"], 1024, 1280)).then_inc(loaded[s], 16)
                    elif name == "xp":
                        sp.dma_start(slot[:, 0:2048].rearrange("p (k n) -> p k n", k=DK),
                                     w_cols(A["w_in"], 768, 1024)).then_inc(loaded[s], 16)
                    elif name in ("cos", "sin"):
                        src = A["dft"][0 if name == "cos" else 1].rearrange("(k p) n -> p k n", p=P)
                        sp.dma_start(slot[:, 0:2048].rearrange("p (k n) -> p k n", k=LT), src).then_inc(loaded[s], 16)
                    elif name == "gate":
                        sp.dma_start(k8, w_cols(A["w_in"], 1280 + 512 * i, 1792 + 512 * i)).then_inc(loaded[s], 16)
                    elif name == "ao":
                        v = A["w_attn_out"][bass.ds(l, 1)].rearrange("a (s j p) n -> s p (a j) n", s=2, p=HD)
                        for h in range(2):
                            sp.dma_start(slot[HD * h:HD * h + HD, :].rearrange("p (j n) -> p j n", j=4),
                                         v[h]).then_inc(loaded[s], 16)
                    elif name == "pf":
                        for h, w in enumerate(("w_pool_out", "w_fourier_out")):
                            sp.dma_start(slot[:, 2048 * h:2048 * h + 2048].rearrange("p (k n) -> p k n", k=2),
                                         w_cols(A[w], 0, D)).then_inc(loaded[s], 16)
                    else:
                        sp.dma_start(k8, w_cols(A["w_out"], 512 * i, 512 * i + 512)).then_inc(loaded[s], 16)
                sp.wait_ge(S["merged"], upto("merged", l, DK))
                sp.sem_inc(aside, 1)
                with sp.Fori(0, NE // 2) as it:
                    for e in range(2):
                        sp.wait_ge(dn_full, (l * (NE // 2) + it) * 2 + e + 1)
                        sp.sem_inc(aside, 1)
                        ex = bass.ds(it * 2 + e, 1)
                        for u, w in enumerate(("w_expert_gate", "w_expert_up")):
                            sp.dma_start(wgu[e][:, u], A[w][bass.ds(l, 1), ex].rearrange("a b (p k) f -> p (a b k) f", p=P))\
                              .then_inc(ex_loaded[e], 16)
                        sp.dma_start(wdn[e], A["w_expert_down"][bass.ds(l, 1), ex].rearrange("a b (p c) n -> p (a b c) n", p=P))\
                          .then_inc(ex_loaded[e], 16)

                def weights_again(b, e, n):
                    sp.wait_ge(f_rows, n + 1)
                    sp.sem_inc(aside, 1)
                    ex = bass.ds(e, 1)
                    for u, w in enumerate(("w_expert_gate", "w_expert_up")):
                        sp.dma_start(wgu[0][:, u], A[w][bass.ds(l, 1), ex].rearrange("a b (p k) f -> p (a b k) f", p=P))\
                          .then_inc(f_loaded, 16)
                    sp.dma_start(wdn[0], A["w_expert_down"][bass.ds(l, 1), ex].rearrange("a b (p c) n -> p (a b c) n", p=P))\
                      .then_inc(f_loaded, 16)
                    sp.wait_ge(f_loaded, 48 * n + 48)
                    sp.sem_inc(aside, 1)

                further_blocks(sp, l, weights_again, [(f_loaded, 48)])

        @block.gpsimd
        def _(pool):
            def hold(s, value):
                pool.wait_ge(s, value)
                pool.sem_inc(aside, 1)

            def link(l, ins):
                count["pool_step"] += 1
                ins.then_inc(S["pool_step"], 1)
                hold(S["pool_step"], upto("pool_step", l, count["pool_step"]))

            pool.dma_start(CON[:, :], A["consts"]).then_inc(const_in, 16)
            pool.dma_start(SILU[:, :, 0:2], A["c_cols"]).then_inc(const_in, 16)
            for k in range(2):
                pool.dma_start(TID[:, k, :], A["token_ids"][:, k, :]).then_inc(y_sent[k], 16)
            for i in range(NT):
                src = A["x_sample"][0, P * i:P * i + P, :] if i < LT else A["x_prompt"][0]
                pool.dma_start(X[:, i, :], src).then_inc(const_in, 16)

            def rstd(l, wait, n, src, dst, inc):
                hold(S[wait], upto(wait, l, n))
                link(l, pool.tensor_scalar(dst, src, 1.0 / D, EPS, ALU.mult, ALU.add))
                w = dst.shape[1]
                pool.tensor_tensor(dst, dst, HALF[:, 0:w], ALU.pow).then_inc(S[inc], 1)

            for k in range(2):
                pool.wait_ge(y_sent[k], 16)
            pool.memset(HALF[:, :], -0.5).then_inc(setup, 1)
            pool.wait_ge(setup, 1)
            blocks16 = pool.alloc_register("blocks16")
            pool.reg_mov(blocks16, 0)
            with pool.Fori(0, DEPTH) as l:
                count["pool_step"] = 0
                hold(S["x_end"], l * per["x_end"] + 1)
                def small(dst, src):
                    pool.dma_start(dst, src).then_inc(S["layer_in"], 16)

                small(VEC[:, :], A["vecs"][bass.ds(l, 1)].rearrange("a p n -> p (a n)"))
                small(RB[:, :], A["router_b"][bass.ds(l, 1)].rearrange("a p n -> p (a n)"))
                small(GAIN, A["gains"][bass.ds(l, 1)].rearrange("a p n -> p (a n)"))
                small(ROPE.rearrange("p a b c -> p (a b c)"), A["rope"])
                small(kc, A["cache_k"][0, bass.ds(l, 1)].rearrange("a p h d -> p (a h d)"))
                small(V[:, 0, :], A["cache_v"][0, bass.ds(l, 1)].rearrange("a p h d -> p (a h d)"))
                pool.memset(WPG, 0.0).then_inc(setup, 1)
                hold(setup, l + 2)
                for g in range(4):
                    h = g % 2
                    small(WPG[HD * h:HD * h + HD, g // 2, HD * h:HD * h + HD],
                          A["w_pool_group"][bass.ds(l, 1), g].rearrange("a c d -> c (a d)"))
                pool.dma_start(A["table"].rearrange("(p n) a -> p (n a)", p=P), A["table_init"])\
                    .then_inc(S["table_clear"], 16)

                rstd(l, "x_sumsq", NT, ST[:, 0, :], ST[:, 1, :], "rstd1")
                for i in range(NT):
                    hold(S["qk_sq"], upto("qk_sq", l, i + 1))
                    a, b = qst[:, (i % 2) * 2, :], qst[:, (i % 2) * 2 + 1, :]
                    link(l, pool.tensor_scalar(b, a, 1.0 / HD, EPS, ALU.mult, ALU.add))
                    pool.tensor_tensor(b, b, HALF[:, 0:NHEADS], ALU.pow).then_inc(S["qk_rstd"], 1)
                hold(S["merged"], upto("merged", l, DK))
                hold(*filled_at(l, "bc", 0))
                pool.dma_start(WR, A["w_router"][bass.ds(l, 1)].rearrange("a (k p) n -> p (a k) n", p=P))\
                    .then_inc(S["wr_in"], 16)
                for i in range(NT + 1):
                    if i < NT:
                        rstd(l, "mix_sq", i + 1, ST[:, 2, i:i + 1], ST[:, 3, i:i + 1], "mix_rstd")
                    if i:
                        j = i - 1
                        rstd(l, "x2_sq", j + 1, ST[:, 4, j:j + 1], ST[:, 5, j:j + 1], "x2_rstd")
                        s = 0 if j < LT else 1
                        hold(S["h_a"], upto("h_a", l, j + 1))
                        pool.tensor_tensor(hrow[:, j % 2, :], hrow[:, j % 2, :], ROW[:, 4 + s, :], ALU.add)\
                            .then_inc(S["h_b"], 1)
                        hold(S["h_b"], upto("h_b", l, j + 1))
                        pool.dma_start(A["h_rows"][P * j:P * j + P, :], hrow[:, j % 2, :])\
                            .then_inc(S[f"h_sent{j % 2}"], 16)
                hold(S["slots_ready"], upto("slots_ready", l, 1))
                hold(S["table_clear"], upto("table_clear", l, 16))
                for k in range(2):
                    for i in range(NT):
                        pool.indirect_dma_start(
                            out=A["table"], out_offset=bass.IndirectOffsetOnAxis(ap=SLOT[:, k, i:i + 1], axis=0),
                            in_=TID[:, k, i:i + 1], in_offset=None).then_inc(S["table_set"], 16)
                hold(S["table_set"], upto("table_set", l, 16 * 2 * NT))
                pool.memset(IDX[:, 0, NE:NE + 2], 2 * TOK).then_inc(S["ids_step"], 1)
                for h in range(2):
                    pool.dma_start(IDX[BLK * h:BLK * h + BLK, 0, 0:NE],
                                   A["table"][0:BLK * NE].rearrange("(p e) a -> p (e a)", e=NE))\
                        .then_inc(S["table_read"], 16)
                hold(S["table_read"], upto("table_read", l, 32))
                hold(S["ids_step"], upto("ids_step", l, 1))
                pool.tensor_scalar(IDX[:, 1, :], IDX[:, 0, :], float(TOK), -float(TOK), ALU.is_ge, ALU.mult)\
                    .then_inc(S["ids_step"], 1)
                pool.tensor_scalar(IDX[:, 2, :], IDX[:, 0, :], 2.0, CON[:, C_HALF:C_HALF + 1], ALU.mult, ALU.add)\
                    .then_inc(S["ids_step"], 1)
                hold(S["ids_step"], upto("ids_step", l, 3))
                pool.tensor_tensor(IDX[:, 1, :], IDX[:, 1, :], IDX[:, 0, :], ALU.add).then_inc(S["ids_step"], 1)
                hold(S["ids_step"], upto("ids_step", l, 4))
                for e in range(2):
                    hold(S[f"h_sent{e}"], upto(f"h_sent{e}", l, per[f"h_sent{e}"]))
                hold(*filled_at(l, "pos", 0))
                pool.memset(HT[0:BLK, 0:2 * D], 0.0).then_inc(S["xg_zero"], 1)
                hold(S["xg_zero"], upto("xg_zero", l, 1))

                def gather(e, nth, col):
                    pool.tensor_copy(IDC[0:BLK, e:e + 1], IDX[0:BLK, 1, bass.ds(col, 1)]).then_inc(idc[e], 1)
                    hold(idc[e], nth)
                    pool.indirect_dma_start(
                        out=xg[0:BLK, e, :], out_offset=None, in_=A["h_rows"],
                        in_offset=bass.IndirectOffsetOnAxis(ap=IDC[0:BLK, e:e + 1], axis=0),
                        bounds_check=TOK - 1, oob_is_err=False).then_inc(rows_in[e], 16)

                for e in range(2):
                    gather(e, l * (NE // 2 + 1) + 1, e)
                with pool.Fori(0, NE // 2) as it:
                    q = l * (NE // 2) + it
                    for e in range(2):
                        hold(xT_full, q * 2 + e + 3)
                        hold(rows_in[e], (q + l) * 16 + 16)
                        gather(e, q + l + 2, it * 2 + 2 + e)
                    for e in range(2):
                        hold(y_out, q * 2 + e + 3)
                        pool.tensor_copy(IDC[:, 2 + e:3 + e], IDX[:, 2, bass.ds(it * 2 + e, 1)]).then_inc(idy[e], 1)
                        hold(idy[e], q + 1)
                        pool.indirect_dma_start(
                            out=A["y_half_rows"], out_offset=bass.IndirectOffsetOnAxis(ap=IDC[:, 2 + e:3 + e], axis=0),
                            in_=yb[:, e, :], in_offset=None,
                            bounds_check=4 * TOK - 1, oob_is_err=False).then_inc(y_sent[e], 16)
                for e in range(2):
                    hold(y_sent[e], (l + 1) * (NE // 2) * 16 + 16)

                def more_rows(b, e, n):
                    pool.reg_add(blocks16, blocks16, 16)
                    in_all = pool.snap(blocks16)
                    ids = A["table"].rearrange("(b p x) a -> b p (x a)", p=BLK, x=NE)[bass.ds(b, 1)]
                    for h in range(2):
                        pool.dma_start(IDX[BLK * h:BLK * h + BLK, 0, 0:NE], ids.rearrange("b p x -> p (b x)"))\
                            .then_inc(f_ids, 16)
                    hold(f_ids, in_all * 2)
                    now, token, half = IDC[:, 3:4], IDX[:, 1, 0:1], IDX[:, 2, 0:1]
                    pool.tensor_copy(now, IDX[:, 0, bass.ds(e, 1)]).then_inc(f_step, 1)
                    hold(f_step, 4 * n + 1)
                    pool.tensor_scalar(token, now, float(TOK), -float(TOK), ALU.is_ge, ALU.mult).then_inc(f_step, 1)
                    pool.tensor_scalar(half, now, 2.0, CON[:, C_HALF:C_HALF + 1], ALU.mult, ALU.add).then_inc(f_step, 1)
                    hold(f_step, 4 * n + 3)
                    pool.tensor_tensor(IDC[0:BLK, 0:1], token[0:BLK], now[0:BLK], ALU.add).then_inc(f_step, 1)
                    hold(f_step, 4 * n + 4)
                    pool.indirect_dma_start(
                        out=xg[0:BLK, 0, :], out_offset=None, in_=A["h_rows"],
                        in_offset=bass.IndirectOffsetOnAxis(ap=IDC[0:BLK, 0:1], axis=0),
                        bounds_check=TOK - 1, oob_is_err=False).then_inc(f_gathered, 16)
                    hold(f_gathered, in_all)
                    pool.sem_inc(f_rows, 1)
                    hold(f_y, n + 1)
                    pool.tensor_copy(IDC[:, 2:3], half).then_inc(f_done, 1)
                    hold(f_done, n + 1)
                    pool.indirect_dma_start(
                        out=A["y_half_rows"], out_offset=bass.IndirectOffsetOnAxis(ap=IDC[:, 2:3], axis=0),
                        in_=yb[:, 0, :], in_offset=None,
                        bounds_check=4 * TOK - 1, oob_is_err=False).then_inc(f_sent, 16)
                    hold(f_sent, in_all)

                for e in range(2):
                    hold(rows_in[e], (l + 1) * (NE // 2 + 1) * 16)
                further_blocks(pool, l, more_rows, [(f_step, 4), (f_rows, 1), (f_done, 1)])
                for i in range(NT):
                    if i >= 2:
                        hold(S["x_end"], upto("x_end", l, i - 1) + 1)
                    pool.dma_start(yg[:, i % 2].rearrange("p k (h n) -> p k h n", h=2),
                                   A["y_half_rows"].rearrange("(k t h) n -> t k h n", k=2, h=2)[P * i:P * i + P])\
                        .then_inc(yg_in[i % 2], 16)
                    if i:
                        rstd(l, "y_sq", i, ST[:, 2, i - 1:i], ST[:, 3, i - 1:i], "y_rstd")
                rstd(l, "y_sq", NT, ST[:, 2, NT - 1:NT], ST[:, 3, NT - 1:NT], "y_rstd")

        @block.scalar
        def _(act):
            def link(l, ins):
                count["act_step"] += 1
                ins.then_inc(S["act_step"], 1)
                act.wait_ge(S["act_step"], upto("act_step", l, count["act_step"]))

            act.wait_ge(const_in, 16 * (2 + NT))
            act.activation(SILU[:, :, 2:4], SILU[:, :, 0:2], ACT.Tanh, scale=0.5).then_inc(silu_a, 1)
            with act.Fori(0, DEPTH) as l:
                count["act_step"] = 0
                act.wait_ge(S["x_end"], upto("x_end", l, 1))
                for i in range(NT):
                    act.activation(junk, X[:, i, :], ACT.Square, accum_out=ST[:, 0, i:i + 1])\
                       .then_inc(S["x_sumsq"], 1)
                    act.wait_ge(S["x_sumsq"], upto("x_sumsq", l, i + 1))
                for s in range(6):
                    act.wait_ge(*filled_at(l, "ada", s))
                    if s >= 2:
                        act.wait_ge(S["ada_cols"], upto("ada_cols", l, s - 1))
                    act.activation(part[:, s % 2, :], pair(pair_of("ada", s)), ACT.Copy)\
                        .then_inc(free[pair_of("ada", s)], 1)
                act.wait_ge(S["affine_ready"], upto("affine_ready", l, 1))
                for k in range(0, DK, 2):
                    act.wait_ge(*filled_at(l, "hT", k))
                    for s in range(2):
                        ins = act.activation(hT[:, k, stream(s)], pair(pair_of("hT", k))[:, stream(s)], ACT.Identity,
                                             bias=MOD[:, 0, k, s:s + 1], scale=AFF[:, 0, k, s:s + 1])
                    ins.then_inc(free[pair_of("hT", k)], 1)
                def qkT(i):
                    act.wait_ge(*filled_at(l, "qkT", i))
                    p = pair_of("qkT", i)
                    to = slice(P * i, P * i + P)
                    if i < NT:
                        act.activation(qT[:, :, to], bank(2 * p).rearrange("p (j t) -> p j t", j=4), ACT.Copy)
                        to = slice(P + P * i, 2 * P + P * i)
                    else:
                        to = slice(0, P)
                    for s in range(2):
                        h = slice(HD * s, HD * s + HD)
                        ins = act.activation(kT[h, s, to], PS[h, 2 * p + 1, 0:P], ACT.Copy)
                    ins.then_inc(free[p], 1)

                for i in range(NT):
                    act.wait_ge(*filled_at(l, "qkv", i))
                    p = pair(pair_of("qkv", i))
                    if i >= 2:
                        act.wait_ge(S["qk_rot"], upto("qk_rot", l, i - 1))
                    act.activation(qraw[:, i % 2, :], p[:, 0:640], ACT.Copy).then_inc(S["qk_raw"], 1)
                    if i == NT - 1:
                        link(l, act.activation(V[:, 1 + i, :], p[:, 640:768], ACT.Copy))
                        act.dma_start(A["out_v"][0, bass.ds(l, 1)].rearrange("a p h d -> p (a h d)"), V[:, 1 + i, :])\
                           .then_inc(S["kv_out"], 16)
                    else:
                        act.activation(V[:, 1 + i, :], p[:, 640:768], ACT.Copy)
                    act.activation(XF[:, i, :], p[:, 768:1024], ACT.Copy).then_inc(free[pair_of("qkv", i)], 1)
                    if i:
                        qkT(i - 1)
                act.wait_ge(S["qk_rot"], upto("qk_rot", l, NT))
                act.dma_start(A["out_k"][0, bass.ds(l, 1)].rearrange("a p h d -> p (a h d)"),
                              qrot[:, (NT - 1) % 2, QW:640]).then_inc(S["kv_out"], 16)
                qkT(NT - 1)
                qkT(NT)
                for c in range(2):
                    act.wait_ge(*filled_at(l, "xp", c))
                    p = pair(c)
                    act.activation(xpT[:, c, POOL_PAD:POOL_PAD + LAT], p[:, 0:LAT], ACT.Copy)
                    act.activation(xpT[:, c, 3 * POOL_PAD + LAT:3 * POOL_PAD + TOK], p[:, LAT:TOK], ACT.Copy)\
                       .then_inc(free[c], 1)
                for j in range(4):
                    act.wait_ge(*filled_at(l, "dft", j))
                    act.activation(AB[:, j, :], pair(pair_of("dft", j))[:, 0:TOK], ACT.Copy)\
                       .then_inc(free[pair_of("dft", j)], 1)
                for c in range(2):
                    act.wait_ge(*filled_at(l, "plin", c))
                    act.activation(PM[:, c, :], pair(pair_of("plin", c))[:, 0:TOK], ACT.Copy,
                                   scale=VEC[:, V_PS + c:V_PS + c + 1]).then_inc(free[pair_of("plin", c)], 1)
                for c in range(2):
                    act.wait_ge(*filled_at(l, "four", c))
                    act.activation(FM[:, c, :], pair(pair_of("four", c))[:, 0:TOK], ACT.Copy)\
                       .then_inc(free[pair_of("four", c)], 1)
                act.wait_ge(S["kv_out"], upto("kv_out", l, 32))
                n_s = 0
                for what, x in STEPS:
                    if what == "ctxS":
                        act.wait_ge(*drained_at(l, "ctxS", 0))
                        act.activation(cP.rearrange("p h t -> p (h t)"), cP.rearrange("p h t -> p (h t)"), ACT.Exp,
                                       scale=SCALE).then_inc(S["cprob"], 1)
                    elif what == "ctxT":
                        act.wait_ge(*filled_at(l, "ctxT", 0))
                        act.activation(cPT.rearrange("p h t -> p (h t)"), pair(3), ACT.Copy).then_inc(free[3], 1)
                    elif what == "gates":
                        act.wait_ge(*filled_at(l, "gate", x))
                        act.activation(TG[:, x // DK, x % DK, :], pair(x % 2)[:, 0:TOK], ACT.Tanh, scale=0.5)\
                           .then_inc(free[x % 2], 1)
                    elif what == "S":
                        h, t = x
                        n_s += 1
                        act.wait_ge(S["smax"], upto("smax", l, n_s))
                        if h:
                            act.wait_ge(S["tr_full"], upto("tr_full", l, 5 * h))
                        act.activation(PR[:, t, :], pair(2)[:, 0:KEYS], ACT.Exp, scale=SCALE,
                                       bias=aST[:, 0, t:t + 1], accum_out=aST[:, 1, t:t + 1]).then_inc(free[2], 1)
                    elif what == "PV":
                        for kt in range(5):
                            n = 5 * x + kt
                            if n % 2:
                                act.wait_ge(S["tr_full"], upto("tr_full", l, n + 1))
                                act.activation(PT[:, 1, :], bank(6), ACT.Copy).then_inc(S["ptT"], 1)
                for v in range(8):
                    act.wait_ge(*filled_at(l, "bc", v))
                    act.activation(ROW[:, v, :], pair(v % 4), ACT.Copy).then_inc(free[v % 4], 1)
                for i in range(NT + 2):
                    if i < NT:
                        act.wait_ge(*filled_at(l, "mix", i))
                        act.activation(junk, pair(i % 2), ACT.Square, scale=0.5, accum_out=ST[:, 2, i:i + 1])\
                           .then_inc(S["mix_sq"], 1)
                        act.wait_ge(S["mix_sq"], upto("mix_sq", l, i + 1))
                    if 1 <= i <= NT:
                        act.wait_ge(S["x_mid"], upto("x_mid", l, i))
                        act.activation(junk, X[:, i - 1, :], ACT.Square, accum_out=ST[:, 4, i - 1:i])\
                           .then_inc(S["x2_sq"], 1)
                        act.wait_ge(S["x2_sq"], upto("x2_sq", l, i))
                    if i >= 2:
                        j = i - 2
                        act.wait_ge(*filled_at(l, "h2T", j))
                        p = pair_of("h2T", j)
                        act.activation(hT[:, :, P * j:P * j + P], pair(p).rearrange("p (k t) -> p k t", k=DK),
                                       ACT.Copy).then_inc(free[p], 1)
                act.wait_ge(S["sel_in"], upto("sel_in", l, 1))
                act.activation(EX[:, 1], EX[:, 0], ACT.Exp).then_inc(S["sel_exp"], 1)
                with act.Fori(0, NE // 2) as it:
                    n = (l * (NE // 2) + it) * 2

                    def x_out(e):
                        act.wait_ge(xT_full, n + e + 3)
                        act.wait_ge(gu_full, n + e + 1)
                        act.activation(xT[:, e].rearrange("p k t -> p (k t)"), bank(e), ACT.Copy).then_inc(xT_out, 1)

                    def tanh(e):
                        act.wait_ge(gt_full, n + e + 3)
                        act.wait_ge(h_out, n + e + 2)
                        act.activation(th, bank(4 + e)[:, 0:256].rearrange("p (c t) -> p c t", c=2)[:, :, 0:BLK],
                                       ACT.Tanh, scale=0.5).then_inc(th_out, 1)

                    def y_rows(e):
                        act.wait_ge(dn_full, n + e + 3)
                        act.wait_ge(y_sent[e], (l * (NE // 2) + it) * 16 + 16)
                        act.activation(yb[:, e, :], bank(6 + e), ACT.Copy, scale=0.5).then_inc(y_out, 1)

                    x_out(0)
                    x_out(1)
                    tanh(0)
                    y_rows(0)
                    tanh(1)
                    y_rows(1)

                def more_act(b, e, n):
                    act.wait_ge(f_xT, n + 1)
                    act.activation(xT[:, 0].rearrange("p k t -> p (k t)"), bank(0), ACT.Copy).then_inc(f_xo, 1)
                    act.wait_ge(f_gt, n + 1)
                    act.activation(th, bank(4)[:, 0:256].rearrange("p (c t) -> p c t", c=2)[:, :, 0:BLK],
                                   ACT.Tanh, scale=0.5).then_inc(f_th, 1)
                    act.wait_ge(f_dn, n + 1)
                    act.activation(yb[:, 0, :], bank(6), ACT.Copy, scale=0.5).then_inc(f_y, 1)

                further_blocks(act, l, more_act, [(f_xo, 1), (f_th, 1), (f_y, 1)])
                seen = [0, 0]
                for i in range(NT + 1):
                    if i < NT:
                        seen[i % 2] += 16
                        act.wait_ge(yg_in[i % 2], l * (48 if i % 2 == 0 else 32) + seen[i % 2])
                        act.activation(yg[:, i % 2, 0, :], yg[:, i % 2, 0, :], ACT.Copy, scale=RS[:, 5, i:i + 1])\
                           .then_inc(S["y_scaled"], 1)
                    if i:
                        j = i - 1
                        act.wait_ge(S["y_sum"], upto("y_sum", l, i))
                        act.activation(junk, yg[:, j % 2, 0, :], ACT.Square, accum_out=ST[:, 2, j:j + 1])\
                           .then_inc(S["y_sq"], 1)
                        act.wait_ge(S["y_sq"], upto("y_sq", l, i))
            act.wait_ge(S["x_end"], DEPTH * per["x_end"] + 1)
            act.dma_start(A["out_s"][0].rearrange("(i p) n -> p i n", p=P), X[:, 0:LT, :]).then_inc(done, 16)
            act.dma_start(A["out_p"][0], X[:, LT, :]).then_inc(done, 16)
            act.wait_ge(done, 32)
            act.wait_ge(S["kv_out"], DEPTH * 32)

        @block.vector
        def _(dve):
            def link(l, ins):
                count["dve_step"] += 1
                ins.then_inc(S["dve_step"], 1)
                dve.wait_ge(S["dve_step"], upto("dve_step", l, count["dve_step"]))

            def bc(ap, axis, shape):
                return ap.unsqueeze(axis).broadcast_to([P] + list(shape))

            for p in range(4):
                dve.sem_inc(free[p], 1)
            dve.sem_inc(S["x_end"], 1)
            for s in (xT_full, xT_out, gu_full, gu_out, gt_full, h_out, dn_full, y_out):
                dve.sem_inc(s, 2)
            dve.wait_ge(const_in, 16 * (2 + NT))
            dve.wait_ge(silu_a, 1)
            dve.scalar_tensor_tensor(SILU[:, :, 0:2], SILU[:, :, 2:4], 1.0, SILU[:, :, 0:2], ALU.add, ALU.mult)\
               .then_inc(silu_b, 1)
            dve.wait_ge(silu_b, 1)
            dve.tensor_scalar(SILU[:, :, 0:2], SILU[:, :, 0:2], 0.5, None, ALU.mult).then_inc(silu_b, 1)
            dve.memset(SILU[:, :, 2:32], 0.0).then_inc(silu_b, 1)

            with dve.Fori(0, DEPTH) as l:
                count["dve_step"] = 0
                dve.wait_ge(S["x_end"], upto("x_end", l, 1))
                dve.memset(kT[HD:P, 0, :], 0.0)
                dve.memset(kT[0:HD, 1, :], 0.0)
                for a, b in ((0, POOL_PAD), (POOL_PAD + LAT, 3 * POOL_PAD + LAT), (PL - POOL_PAD, PL)):
                    dve.memset(xpT[:, :, a:b], 0.0)
                dve.wait_ge(S["rstd1"], upto("rstd1", l, 1))
                for i in range(NT):
                    ins = dve.tensor_scalar(xn[:, i, :], X[:, i, :], ST[:, 1, i:i + 1], None, ALU.mult)
                ins.then_inc(S["xn_ready"], 1)
                dve.wait_ge(*filled_at(l, "adacol", 0))
                dve.wait_ge(S["layer_in"], upto("layer_in", l, per["layer_in"]))
                dve.tensor_tensor(MOD[:, :, :, :].rearrange("p s k t -> p (s k) t"),
                                  PS[:, 4, 0:96].rearrange("p (s t) -> p s t", t=2),
                                  bc(VEC[:, V_BADA:V_BADA + 48], 2, (48, 2)), ALU.add).then_inc(free[2], 1)
                dve.wait_ge(*drained_at(l, "adacol", 0))
                for n, (sec, add, mul, gain) in enumerate(((1, 1.0, None, V_MPRE), (2, None, 0.5, V_MPOST),
                                                           (4, 1.0, None, V_FPRE), (5, None, 1.0, V_FPOST))):
                    ins = dve.scalar_tensor_tensor(AFF[:, n], MOD[:, sec], add if mul is None else mul,
                                                   bc(VEC[:, gain:gain + DK], 2, (DK, 2)),
                                                   ALU.add if mul is None else ALU.mult, ALU.mult)
                ins.then_inc(S["affine_ready"], 1)
                dve.wait_ge(S["affine_ready"], upto("affine_ready", l, 1))
                for k in range(1, DK, 2):
                    dve.wait_ge(*filled_at(l, "hT", k))
                    for s in range(2):
                        ins = dve.tensor_scalar(hT[:, k, stream(s)], pair(pair_of("hT", k))[:, stream(s)],
                                                AFF[:, 0, k, s:s + 1], MOD[:, 0, k, s:s + 1], ALU.mult, ALU.add)
                    ins.then_inc(free[pair_of("hT", k)], 1)
                for i in range(NT):
                    raw, st = qraw[:, i % 2, :], (i % 2) * 2
                    dve.wait_ge(S["qk_raw"], upto("qk_raw", l, i + 1))
                    if i:
                        dve.wait_ge(S["qk_rot"], upto("qk_rot", l, i))
                    link(l, dve.tensor_tensor(qsq, raw, raw, ALU.mult))
                    dve.tensor_reduce(qst[:, st, :], qsq.rearrange("p (h d) -> p h d", d=HD), AX.X, ALU.add)\
                       .then_inc(S["qk_sq"], 1)
                    dve.wait_ge(S["qk_rstd"], upto("qk_rstd", l, i + 1))
                    link(l, dve.tensor_tensor(qa.rearrange("p (h d) -> p h d", d=HD), raw.rearrange("p (h d) -> p h d", d=HD),
                                              bc(qst[:, st + 1, :], 2, (NHEADS, HD)), ALU.mult))
                    if i >= 2:
                        dve.wait_ge(*filled_at(l, "qkT", i - 2))
                    out_q = qrot[:, i % 2, 0:QW].rearrange("p (j s d) -> p s j d", j=4, s=2)
                    out_k = qrot[:, i % 2, QW:640]
                    if i < LT:
                        link(l, dve.tensor_tensor(qb, qa, GAIN, ALU.mult))
                        x5 = qb.rearrange("p (h a f c) -> p h a f c", a=2, f=2, c=16)
                        y5 = qsq.rearrange("p (h a f c) -> p h a f c", a=2, f=2, c=16)
                        r5 = ROPE[:, 1, i, :].rearrange("p (a f c) -> p a f c", a=2, f=2)
                        dve.tensor_tensor(qa.rearrange("p (h d) -> p h d", d=HD), qb.rearrange("p (h d) -> p h d", d=HD),
                                          bc(ROPE[:, 0, i, :], 1, (NHEADS, HD)), ALU.mult)
                        for f in range(2):
                            ins = dve.tensor_tensor(y5[:, :, :, f, :], x5[:, :, :, 1 - f, :],
                                                    bc(r5[:, :, f, :], 1, (NHEADS, 2, 16)), ALU.mult)
                        link(l, ins)
                        a, b, op = qa, qsq, ALU.add
                    else:
                        a, b, op = qa, GAIN, ALU.mult
                    dve.tensor_tensor(out_q, a[:, 0:QW].rearrange("p (s j d) -> p s j d", s=2, j=4),
                                      b[:, 0:QW].rearrange("p (s j d) -> p s j d", s=2, j=4), op)
                    dve.tensor_tensor(out_k, a[:, QW:640], b[:, QW:640], op).then_inc(S["qk_rot"], 1)
                for c in range(2):
                    dve.wait_ge(*drained_at(l, "xp", c))
                    x = xpT[:, c, :]

                    def double(to, of, half, lo, part=slice(0, P)):
                        a, b = lo, PL - lo
                        up = half if half else 0
                        dn = half if half else 1
                        link(l, dve.tensor_tensor(to[part, a:b], of[part, a - dn:b - dn], of[part, a + up:b + up], ALU.add))

                    double(pS[0], x, 0, 1)
                    if c == 0:
                        low, high, half, lo = pS[0], pS[1], 1, 2
                    else:
                        double(pS[1], pS[0], 1, 2)
                        double(pS[2], pS[1], 2, 4)
                        low, high, half, lo = pS[2], pS[0], 4, 8
                    dve.tensor_copy(high[0:HD, POOL_PAD:PL - POOL_PAD], low[0:HD, POOL_PAD:PL - POOL_PAD])
                    double(high, low, half, lo, slice(HD, P))
                    for side, at, step in ((0, POOL_PAD, LAT + 2 * POOL_PAD), (1, LAT, CTX + 2 * POOL_PAD)):
                        e = C_EDGE + (2 * side + c) * 8
                        for n in range(2):
                            v = high[:, at + n * step:at + n * step + 8]
                            ins = dve.tensor_tensor(v, v, CON[:, e:e + 8], ALU.mult)
                    link(l, ins)
                    for s, at in ((0, POOL_PAD), (1, 3 * POOL_PAD + LAT)):
                        n = LAT if s == 0 else CTX
                        ins = dve.scalar_tensor_tensor(pooled[:, c, stream(s)], high[:, at:at + n],
                                                       CON[:, C_WINV + c:C_WINV + c + 1], x[:, at:at + n],
                                                       ALU.mult, ALU.subtract)
                    ins.then_inc(S["pooled"], 1)
                    dve.wait_ge(S["pooled"], upto("pooled", l, c + 1))
                dve.wait_ge(*filled_at(l, "ctxS", 0))
                sc = pair(2).rearrange("p (h t) -> p h t", h=NH)
                link(l, dve.tensor_reduce(aST[:, 0, :], sc, AX.X, ALU.max))
                dve.tensor_tensor(cP, sc, bc(aST[:, 0, :], 2, (NH, P)), ALU.subtract).then_inc(free[2], 1)
                dve.wait_ge(S["cprob"], upto("cprob", l, 1))
                link(l, dve.tensor_reduce(aST[:, 1, :], cP, AX.X, ALU.add))
                link(l, dve.reciprocal(aST[:, 2, :], aST[:, 1, :]))
                dve.tensor_tensor(cP, cP, bc(aST[:, 2, :], 2, (NH, P)), ALU.mult).then_inc(S["cpn"], 1)
                dve.wait_ge(*filled_at(l, "ctxO", 0))
                dve.tensor_copy(OT[:, :, LAT:TOK], bank(4).rearrange("p (j t) -> p j t", j=4)).then_inc(free[2], 1)

                def normalise(h, t):
                    dve.wait_ge(*drained_at(l, "S", (h, t)))
                    link(l, dve.reciprocal(aST[:, 2, t:t + 1], aST[:, 1, t:t + 1]))
                    dve.tensor_scalar(PR[:, t, :], PR[:, t, :], aST[:, 2, t:t + 1], None, ALU.mult)\
                       .then_inc(S["pnorm"], 1)

                for h in range(NH):
                    for t in range(LT):
                        dve.wait_ge(*filled_at(l, "S", (h, t)))
                        link(l, dve.tensor_reduce(aST[:, 0, t:t + 1], pair(2)[:, 0:KEYS], AX.X, ALU.max))
                        dve.tensor_scalar(aST[:, 0, t:t + 1], aST[:, 0, t:t + 1], -SCALE, None, ALU.mult)\
                           .then_inc(S["smax"], 1)
                        if t:
                            normalise(h, t - 1)
                    normalise(h, LT - 1)
                    for kt in range(5):
                        n = 5 * h + kt
                        if n % 2 == 0:
                            dve.wait_ge(S["tr_full"], upto("tr_full", l, n + 1))
                            dve.tensor_copy(PT[:, 0, :], bank(6)).then_inc(S["ptT"], 1)
                    s, j = h // 4, h % 4
                    dve.wait_ge(S["pv_full"], upto("pv_full", l, h + 1))
                    dve.tensor_copy(OT[HD * s:HD * s + HD, j, 0:LAT], PS[HD * s:HD * s + HD, 7, :])\
                       .then_inc(S["o_ready"], 1)
                for d in range(DK):
                    for b, name in enumerate(("mattn", "mpool", "mfour")):
                        dve.wait_ge(*filled_at(l, name, d))
                        p = pair_of(name, d)
                        to = hT[:, d, :] if b == 0 else TG[:, b, d, :]
                        dve.scalar_tensor_tensor(to, TG[:, b, d, :], 1.0, pair(p)[:, 0:TOK], ALU.add, ALU.mult)\
                           .then_inc(free[p], 1)
                        if b:
                            dve.wait_ge(*drained_at(l, name, d))
                            ins = dve.tensor_tensor(hT[:, d, :], hT[:, d, :], TG[:, b, d, :], ALU.add)
                            if b == 1:
                                link(l, ins)
                    ins.then_inc(S["merged"], 1)

                def mixed(i):
                    s = 0 if i < LT else 1
                    dve.wait_ge(*filled_at(l, "mix", i))
                    dve.wait_ge(S["mix_rstd"], upto("mix_rstd", l, i + 1))
                    dve.scalar_tensor_tensor(tmix[:, i % 2, :], pair(i % 2), ST[:, 3, i:i + 1], ROW[:, s, :],
                                             ALU.mult, ALU.mult).then_inc(free[i % 2], 1)
                    dve.wait_ge(*drained_at(l, "mix", i))
                    dve.tensor_tensor(X[:, i, :], X[:, i, :], tmix[:, i % 2, :], ALU.add).then_inc(S["x_mid"], 1)

                def h_rows(i):
                    s = 0 if i < LT else 1
                    dve.wait_ge(S["x2_rstd"], upto("x2_rstd", l, i + 1))
                    if i >= 2:
                        dve.wait_ge(*filled_at(l, "h2T", i - 2))
                        dve.wait_ge(S[f"h_sent{i % 2}"], upto(f"h_sent{i % 2}", l, 16 * (i // 2)))
                    dve.scalar_tensor_tensor(hrow[:, i % 2, :], X[:, i, :], ST[:, 5, i:i + 1], ROW[:, 2 + s, :],
                                             ALU.mult, ALU.mult).then_inc(S["h_a"], 1)

                for v in range(4, 8):
                    dve.wait_ge(*drained_at(l, "bc", v))
                mixed(0)
                for i in range(NT):
                    if i + 1 < NT:
                        mixed(i + 1)
                    h_rows(i)
                L = cut(R, 10240, (NT, NR))
                sc1, mask, m1, m2, oh1, oh2 = rt[2], rt[3], rt[4], rt[5], rt[6], rt[7]
                CUM = cut(R, 10240 + 160 * 8, (NT + 1, NE))
                rev, eid = CON[:, C_REV:C_REV + NE], CON[:, C_EID:C_EID + NE]
                dve.wait_ge(*filled_at(l, "lg", 0))
                dve.tensor_tensor(L, PS[:, 6, 0:NT * NR].rearrange("p (t n) -> p t n", n=NR),
                                  bc(RB[:, :], 1, (NT, NR)), ALU.add).then_inc(free[3], 1)
                dve.wait_ge(*drained_at(l, "lg", 0))

                def first_best(vals, best, n, out, tmp):
                    link(l, dve.tensor_reduce(best, vals, AX.X, ALU.max))
                    link(l, dve.tensor_tensor(tmp, vals, bc(best, 2, (NT, n)), ALU.is_equal))
                    link(l, dve.tensor_tensor(tmp, tmp, bc(rev[:, 0:n], 1, (NT, n)), ALU.mult))
                    link(l, dve.tensor_reduce(RS[:, 7, :], tmp, AX.X, ALU.max))
                    link(l, dve.tensor_tensor(out, tmp, bc(RS[:, 7, :], 2, (NT, n)), ALU.is_equal))

                g_oh, g_tmp = mask[:, :, 0:NG], sc1[:, :, 0:NG]
                first_best(L[:, :, 0:NG], RS[:, 0, :], NG, g_oh, g_tmp)
                dve.tensor_tensor(EX[:, 0, :, 0:NG], L[:, :, 0:NG], bc(RS[:, 0, :], 2, (NT, NG)), ALU.subtract)
                link(l, dve.tensor_scalar(g_tmp, g_oh, 1.0, BIG, ALU.subtract, ALU.mult))
                for i in range(NT):
                    ins = dve.tensor_tensor(m1[:, i, :].rearrange("p (g e) -> p g e", g=NG),
                                            L[:, i, NG:NR].rearrange("p (g e) -> p g e", g=NG),
                                            bc(g_tmp[:, i, :], 2, (NG, EPG)), ALU.add)
                link(l, ins)
                first_best(m1, RS[:, 2, :], NE, oh1, sc1)
                link(l, dve.scalar_tensor_tensor(m2, oh1, -2 * BIG, m1, ALU.mult, ALU.add))
                first_best(m2, RS[:, 3, :], NE, oh2, sc1)
                dve.tensor_tensor(EX[:, 0, :, 4], RS[:, 3, :], RS[:, 2, :], ALU.subtract).then_inc(S["sel_in"], 1)
                dve.memset(CUM[:, 0, :], 0.0)
                link(l, dve.tensor_tensor(mask, oh1, oh2, ALU.add))
                for i in range(NT):
                    ins = dve.tensor_tensor(CUM[:, i + 1, :], CUM[:, i, :], mask[:, i, :], ALU.add)
                    if i < NT - 1:
                        link(l, ins)
                ins.then_inc(S["mask_ready"], 1)
                dve.wait_ge(S["sel_exp"], upto("sel_exp", l, 1))
                link(l, dve.tensor_reduce(RS[:, 1, :], EX[:, 1, :, 0:NG], AX.X, ALU.add))
                link(l, dve.scalar_tensor_tensor(RS[:, 4, :], EX[:, 1, :, 4], 1.0, RS[:, 1, :], ALU.add, ALU.mult))
                link(l, dve.reciprocal(RS[:, 5, :], RS[:, 4, :]))
                link(l, dve.tensor_tensor(RS[:, 6, :], RS[:, 5, :], EX[:, 1, :, 4], ALU.mult))
                dve.wait_ge(*filled_at(l, "pos", 0))
                link(l, dve.tensor_reduce(RS[:, 0, 0:1], PS[:, 1, 0:NE], AX.X, ALU.max))
                dve.tensor_copy(MOST[:, :], RS[:, 0, 0:1])
                dve.scalar_tensor_tensor(m1, PS[:, 0, 0:NT * NE].rearrange("p (t n) -> p t n", n=NE), float(NE),
                                         bc(eid, 1, (NT, NE)), ALU.mult, ALU.add).then_inc(free[0], 1)
                dve.wait_ge(*drained_at(l, "pos", 0))
                for k, oh in enumerate((oh1, oh2)):
                    link(l, dve.tensor_tensor(oh, oh, m1, ALU.mult))
                    link(l, dve.tensor_reduce(RS[:, 2 + k, :], oh, AX.X, ALU.add))
                    ins = dve.tensor_copy(SLOT[:, k, :], RS[:, 2 + k, :])
                ins.then_inc(S["slots_ready"], 1)
                with dve.Fori(0, NE // 2) as it:
                    n = (l * (NE // 2) + it) * 2
                    for e in range(2):
                        dve.wait_ge(gu_full, n + e + 3)
                        dve.wait_ge(gt_full, n + e + 1)
                        dve.tensor_copy(GU[:, e, :], PS[:, 2 + e, 0:FF]).then_inc(gu_out, 1)
                        dve.wait_ge(th_out, n + e + 1)
                        gt = bank(4 + e)[:, 0:256].rearrange("p (c t) -> p c t", c=2)
                        dve.scalar_tensor_tensor(sg, th, 1.0, gt[:, :, 0:BLK], ALU.add, ALU.mult).then_inc(sg_out, 1)
                        dve.wait_ge(sg_out, n + e + 1)
                        dve.wait_ge(dn_full, n + e + 1)
                        dve.tensor_tensor(hE[:, e], sg, gt[:, :, BLK:P], ALU.mult).then_inc(h_out, 1)

                def more_dve(b, e, n):
                    dve.wait_ge(f_gu, n + 1)
                    dve.tensor_copy(GU[:, 0, :], PS[:, 2, 0:FF]).then_inc(f_go, 1)
                    dve.wait_ge(f_th, n + 1)
                    gt = bank(4)[:, 0:256].rearrange("p (c t) -> p c t", c=2)
                    dve.scalar_tensor_tensor(sg, th, 1.0, gt[:, :, 0:BLK], ALU.add, ALU.mult).then_inc(f_sg, 1)
                    dve.wait_ge(f_sg, n + 1)
                    dve.tensor_tensor(hE[:, 0], sg, gt[:, :, BLK:P], ALU.mult).then_inc(f_h, 1)

                further_blocks(dve, l, more_dve, [(f_go, 1), (f_sg, 1), (f_h, 1)])
                for i in range(NT + 1):
                    if i < NT:
                        dve.wait_ge(S["y_scaled"], upto("y_scaled", l, i + 1))
                        y = yg[:, i % 2]
                        dve.scalar_tensor_tensor(y[:, 0, :], y[:, 1, :], RS[:, 6, i:i + 1], y[:, 0, :], ALU.mult, ALU.add)\
                           .then_inc(S["y_sum"], 1)
                        dve.wait_ge(S["y_sum"], upto("y_sum", l, i + 1))
                    if i:
                        j = i - 1
                        s = 0 if j < LT else 1
                        y = yg[:, j % 2]
                        dve.wait_ge(S["y_rstd"], upto("y_rstd", l, i))
                        link(l, dve.scalar_tensor_tensor(y[:, 1, :], y[:, 0, :], ST[:, 3, j:j + 1], ROW[:, 6 + s, :],
                                                         ALU.mult, ALU.mult))
                        dve.tensor_tensor(X[:, j, :], X[:, j, :], y[:, 1, :], ALU.add).then_inc(S["x_end"], 1)

        @block.tensor
        def _(pe):
            pe.wait_ge(const_in, 16 * (2 + NT))
            pe.wait_ge(silu_b, 3)
            mm, tp = nc.tensor.matmul, nc.tensor.transpose

            with pe.Fori(0, DEPTH) as l:

                def slot(name, i, k=DK):
                    s, _ = chunk(name, i)
                    return W[:, s, :].rearrange("p (k n) -> p k n", k=k)

                def both_streams(p, lhsT, rhs, start, stop):
                    mm(pair(p)[:, 0:LAT], lhsT, rhs[:, 0:LAT], start=start, stop=stop)
                    return mm(pair(p)[:, LAT:TOK], lhsT, rhs[:, LAT:TOK], start=start, stop=stop)

                def ada_cols(s):
                    pe.wait_ge(*drained_at(l, "ada", s))
                    if s == 0:
                        pe.wait_ge(*freed_at(l, "adacol", 0))
                    for k in range(DK):
                        ins = mm(PS[:, 4, s * 16 + 2 * k:s * 16 + 2 * k + 2], part[:, s % 2, P * k:P * k + P],
                                 CON[:, C_SEL:C_SEL + 2], start=True, stop=True)
                    ins.then_inc(S["ada_cols"], 1)

                for s in range(6):
                    pe.wait_ge(*freed_at(l, "ada", s))
                    for n in range(2):
                        pe.wait_ge(*loaded_at(l, "ada", 2 * s + n))
                        w = slot("ada", 2 * s + n)
                        for k in range(DK):
                            j = k % 4
                            ins = mm(PS[32 * j:32 * j + 32, 2 * (s % 2) + n, :], SILU[:, k, :], w[:, k, :],
                                     start=k < 4, stop=k >= 4)
                        ins.then_inc(*((S["ada_half"], 1) if n == 0 else (full[s % 2], 1)))
                    if s:
                        ada_cols(s - 1)
                ada_cols(5)
                pe.wait_ge(S["ada_cols"], upto("ada_cols", l, 6))
                pe.sem_inc(full[2], 1)
                pe.wait_ge(S["xn_ready"], upto("xn_ready", l, 1))
                for k in range(DK):
                    p = pair_of("hT", k)
                    pe.wait_ge(*freed_at(l, "hT", k))
                    for i in range(NT):
                        ins = tp(pair(p)[:, P * i:P * i + P], xn[:, i, P * k:P * k + P], ident)
                    ins.then_inc(full[p], 1)
                for k in range(4, DK):
                    pe.wait_ge(*drained_at(l, "hT", k))

                def qkT(i):
                    p = pair_of("qkT", i)
                    pe.wait_ge(*freed_at(l, "qkT", i))
                    if i < NT:
                        pe.wait_ge(S["qk_rot"], upto("qk_rot", l, i + 1))
                        for j in range(5):
                            ins = tp(pair(p)[:, P * j:P * j + P], qrot[:, i % 2, P * j:P * j + P], ident)
                    else:
                        pe.wait_ge(S["layer_in"], upto("layer_in", l, per["layer_in"]))
                        ins = tp(PS[:, 2 * p + 1, 0:P], kc, ident)
                    ins.then_inc(full[p], 1)

                for i in range(NT):
                    p = pair_of("qkv", i)
                    pe.wait_ge(*freed_at(l, "qkv", i))
                    for n, name in enumerate(("q", "kvx")):
                        pe.wait_ge(*loaded_at(l, name))
                        for k in range(DK):
                            ins = mm(bank(2 * p + n), hT[:, k, P * i:P * i + P], slot(name, 0)[:, k, :],
                                     start=k == 0, stop=k == DK - 1)
                    ins.then_inc(full[p], 1)
                    if i:
                        qkT(i - 1)
                for c in range(2):
                    pe.wait_ge(*freed_at(l, "xp", c))
                    pe.wait_ge(*loaded_at(l, "xp"))
                    w = W[:, chunk("xp")[0], 0:2048].rearrange("p (k n) -> p k n", k=DK)
                    for k in range(DK):
                        ins = both_streams(c, w[:, k, P * c:P * c + P], hT[:, k, :], k == 0, k == DK - 1)
                    ins.then_inc(full[c], 1)
                    if c == 0:
                        qkT(NT - 1)
                        qkT(NT)
                pe.wait_ge(*drained_at(l, "qkv", NT - 1))
                pe.wait_ge(*drained_at(l, "qkv", NT - 2))
                for j in range(4):
                    c, f = j % 2, j // 2
                    p = pair_of("dft", j)
                    pe.wait_ge(*freed_at(l, "dft", j))
                    name = ("cos", "sin")[f]
                    pe.wait_ge(*loaded_at(l, name))
                    w = W[:, chunk(name)[0], 0:2048].rearrange("p (k n) -> p k n", k=LT)
                    for k in range(LT):
                        ins = mm(bank(2 * p), XF[:, k, P * c:P * c + P], w[:, k, :], start=k == 0, stop=k == LT - 1)
                    mm(PS[:, 2 * p + 1, 0:P], XF[:, LT, P * c:P * c + P], cols(C_XC if f == 0 else C_XS),
                       start=True, stop=True).then_inc(full[p], 1)
                for c in range(2):
                    p = pair_of("plin", c)
                    pe.wait_ge(*freed_at(l, "plin", c))
                    pe.wait_ge(S["pooled"], upto("pooled", l, c + 1))
                    both_streams(p, WPG[:, c, :], pooled[:, c, :], True, True).then_inc(full[p], 1)
                for c in range(2):
                    p = pair_of("four", c)
                    pe.wait_ge(*freed_at(l, "four", c))
                    pe.wait_ge(*drained_at(l, "dft", c))
                    both_streams(p, cols(C_CC), AB[:, c, :], True, False)
                    pe.wait_ge(*drained_at(l, "dft", 2 + c))
                    both_streams(p, cols(C_CS), AB[:, 2 + c, :], False, True).then_inc(full[p], 1)

                pe.wait_ge(*drained_at(l, "qkT", NT - 1))
                pe.wait_ge(*drained_at(l, "qkT", NT))
                for what, x in STEPS:
                    if what == "gates":
                        pe.wait_ge(*freed_at(l, "gate", x))
                        pe.wait_ge(*loaded_at(l, "gate", x // 4))
                        w = slot("gate", x // 4)
                        for k in range(DK):
                            ins = both_streams(x % 2, w[:, k, P * (x % 4):P * (x % 4) + P], hT[:, k, :], k == 0, k == DK - 1)
                        ins.then_inc(full[x % 2], 1)
                    elif what == "ctxS":
                        pe.wait_ge(*freed_at(l, "ctxS", 0))
                        for h in range(NH):
                            ins = mm(pair(2)[:, P * h:P * h + P], qT[:, h % 4, LAT:TOK], kT[:, h // 4, KEYS:KALL],
                                     start=True, stop=True)
                        ins.then_inc(full[2], 1)
                    elif what == "ctxT":
                        pe.wait_ge(*freed_at(l, "ctxT", 0))
                        pe.wait_ge(S["cpn"], upto("cpn", l, 1))
                        for h in range(NH):
                            ins = tp(pair(3)[:, P * h:P * h + P], cP[:, h, :], ident)
                        ins.then_inc(full[3], 1)
                    elif what == "ctxO":
                        pe.wait_ge(*freed_at(l, "ctxO", 0))
                        pe.wait_ge(*drained_at(l, "ctxT", 0))
                        for h in range(NH):
                            s, j = h // 4, h % 4
                            ins = mm(PS[HD * s:HD * s + HD, 4, P * j:P * j + P], V[:, NT, HD * s:HD * s + HD], cPT[:, h, :],
                                     start=True, stop=True)
                        ins.then_inc(full[2], 1)
                    elif what == "S":
                        h, t = x
                        pe.wait_ge(*freed_at(l, "S", x))
                        q = qT[:, h % 4, P * t:P * t + P]
                        mm(bank(4), q, kT[:, h // 4, 0:512], start=True, stop=True)
                        mm(PS[:, 5, 0:P], q, kT[:, h // 4, 512:KEYS], start=True, stop=True).then_inc(full[2], 1)
                    elif what == "PV":
                        s, j = x // 4, x % 4
                        pe.wait_ge(S["pnorm"], upto("pnorm", l, LT * (x + 1)))
                        for kt in range(5):
                            n = 5 * x + kt
                            if n:
                                pe.wait_ge(S["ptT"], upto("ptT", l, n))
                            for t in range(LT):
                                ins = tp(bank(6)[:, P * t:P * t + P], PR[:, t, P * kt:P * kt + P], ident)
                            ins.then_inc(S["tr_full"], 1)
                            if kt == 0 and x:
                                pe.wait_ge(S["o_ready"], upto("o_ready", l, x))
                            pe.wait_ge(S["ptT"], upto("ptT", l, n + 1))
                            ins = mm(PS[HD * s:HD * s + HD, 7, :], V[:, kt, HD * s:HD * s + HD], PT[:, n % 2, :],
                                     start=kt == 0, stop=kt == 4)
                        ins.then_inc(S["pv_full"], 1)
                pe.wait_ge(S["o_ready"], upto("o_ready", l, NH))
                pe.wait_ge(*drained_at(l, "plin", 1))
                pe.wait_ge(*drained_at(l, "four", 1))
                for d in range(DK):
                    at = slice(P * d, P * d + P)
                    pf = W[:, chunk("pf")[0], :].rearrange("p (w k n) -> p w k n", w=2, k=2)
                    for name, src, n in (("mattn", OT, 4), ("mpool", PM, 2), ("mfour", FM, 2)):
                        p = pair_of(name, d)
                        pe.wait_ge(*freed_at(l, name, d))
                        pe.wait_ge(*loaded_at(l, "ao" if n == 4 else "pf"))
                        w = slot("ao", 0, 4) if n == 4 else pf[:, 0 if name == "mpool" else 1]
                        for k in range(n):
                            ins = both_streams(p, w[:, k, at], src[:, k, :], k == 0, k == n - 1)
                        ins.then_inc(full[p], 1)
                for v in range(8):
                    p, s = v % 4, v % 2
                    pe.wait_ge(*freed_at(l, "bc", v))
                    vec = (AFF[:, 1], AFF[:, 2], MOD[:, 3], AFF[:, 3])[v // 2]
                    for k in range(DK):
                        ins = mm(pair(p)[:, P * k:P * k + P], vec[:, k, s:s + 1].broadcast_to([P, P]), ident,
                                 start=True, stop=True)
                    ins.then_inc(full[p], 1)

                def h2T(i):
                    p = pair_of("h2T", i)
                    pe.wait_ge(*freed_at(l, "h2T", i))
                    pe.wait_ge(S["h_b"], upto("h_b", l, i + 1))
                    for k in range(DK):
                        ins = tp(pair(p)[:, P * k:P * k + P], hrow[:, i % 2, P * k:P * k + P], ident)
                    ins.then_inc(full[p], 1)

                pe.wait_ge(S["merged"], upto("merged", l, DK))
                for i in range(NT):
                    p = i % 2
                    pe.wait_ge(*freed_at(l, "mix", i))
                    for n in range(2):
                        pe.wait_ge(*loaded_at(l, "wo", n))
                        for k in range(DK):
                            ins = mm(bank(2 * p + n), hT[:, k, P * i:P * i + P], slot("wo", n)[:, k, :],
                                     start=k == 0, stop=k == DK - 1)
                    ins.then_inc(full[p], 1)
                    if i:
                        h2T(i - 1)
                h2T(NT - 1)
                pe.wait_ge(*freed_at(l, "lg", 0))
                pe.wait_ge(S["wr_in"], upto("wr_in", l, 16))
                pe.wait_ge(*drained_at(l, "h2T", NT - 1))
                pe.wait_ge(*drained_at(l, "h2T", NT - 2))
                for i in range(NT):
                    for k in range(DK):
                        ins = mm(PS[:, 6, NR * i:NR * i + NR], hT[:, k, P * i:P * i + P], WR[:, k, :],
                                 start=k == 0, stop=k == DK - 1)
                ins.then_inc(full[3], 1)
                pe.wait_ge(*freed_at(l, "pos", 0))
                pe.wait_ge(S["mask_ready"], upto("mask_ready", l, 1))
                flat = slice(0, NT * NE)
                cum = cut(R, 10240 + 160 * 8, (NT * NE + NE,))
                mm(PS[:, 0, flat], tri, rt[3].rearrange("p t n -> p (t n)"), start=True, stop=False)
                mm(PS[:, 0, flat], ones, cum[:, flat], start=False, stop=True)
                mm(PS[:, 1, 0:NE], ones, cum[:, NT * NE:], start=True, stop=True).then_inc(full[0], 1)

                def transpose_rows(e):
                    rows = xg[0:BLK, e, :].rearrange("p (f k) -> p k f", k=DK)
                    for k in range(DK):
                        ins = tp(bank(e)[:, BLK * k:BLK * k + BLK], rows[:, k, :], ident[0:BLK, 0:BLK])
                    return ins

                def gate_up_products(e):
                    for k in range(DK):
                        for u in range(2):
                            ins = mm(PS[BLK * u:BLK * u + BLK, 2 + e, 0:FF], xT[:, e, k, :], wgu[e][:, u, k, :],
                                     start=k == 0, stop=k == DK - 1)
                    return ins

                def transpose_gate_up(e):
                    v = GU[:, e, :].rearrange("p (f c) -> p c f", c=2)
                    for c in range(2):
                        ins = tp(bank(4 + e)[:, P * c:P * c + P], v[:, c, :], ident)
                    return ins

                def down_products(e):
                    for c in range(2):
                        for h in range(2):
                            ins = mm(PS[BLK * h:BLK * h + BLK, 6 + e, :], hE[:, e, c, :],
                                     wdn[e][:, c, 512 * h:512 * h + 512], start=c == 0, stop=c == 1)
                    return ins

                for p in range(4):
                    pe.wait_ge(free[p], (l + 1) * PAIRS.free[p] + 1)
                pe.sem_inc(aside, 1)
                with pe.Fori(0, NE // 2) as it:
                    q = l * (NE // 2) + it
                    n = q * 2

                    def rows_T(e):
                        pe.wait_ge(rows_in[e], (q + l) * 16 + 16)
                        pe.wait_ge(xT_out, n + e + 1)
                        pe.sem_inc(aside, 1)
                        transpose_rows(e).then_inc(xT_full, 1)

                    def gate_up(e):
                        pe.wait_ge(xT_out, n + e + 3)
                        pe.wait_ge(ex_loaded[e], q * 48 + 48)
                        pe.wait_ge(gu_out, n + e + 1)
                        gate_up_products(e).then_inc(gu_full, 1)

                    def gu_T(e):
                        pe.wait_ge(gu_out, n + e + 3)
                        pe.wait_ge(h_out, n + e + 1)
                        transpose_gate_up(e).then_inc(gt_full, 1)

                    def down(e):
                        pe.wait_ge(h_out, n + e + 3)
                        pe.wait_ge(y_out, n + e + 1)
                        down_products(e).then_inc(dn_full, 1)

                    rows_T(0)
                    gate_up(0)
                    rows_T(1)
                    gu_T(0)
                    gate_up(1)
                    down(0)
                    gu_T(1)
                    down(1)
                for s in (xT_out, gu_out, h_out, y_out):
                    pe.wait_ge(s, (l + 1) * NE + 2)

                def more_pe(b, e, n):
                    pe.wait_ge(f_rows, n + 1)
                    pe.sem_inc(aside, 1)
                    transpose_rows(0).then_inc(f_xT, 1)
                    pe.wait_ge(f_xo, n + 1)
                    pe.wait_ge(f_loaded, 48 * n + 48)
                    gate_up_products(0).then_inc(f_gu, 1)
                    pe.wait_ge(f_go, n + 1)
                    transpose_gate_up(0).then_inc(f_gt, 1)
                    pe.wait_ge(f_h, n + 1)
                    down_products(0).then_inc(f_dn, 1)

                further_blocks(pe, l, more_pe, [(f_xT, 1), (f_gu, 1), (f_gt, 1), (f_dn, 1)])
                pe.wait_ge(f_y, (l + 1) * XBLK * NE)

        for name, n in count.items():
            assert n == per[name], (name, n)


STEPS_PER_LAYER = dict(dve_step=138, act_step=1, pool_step=21)


def host_constants(np):
    con = np.zeros((P, NCONST), np.float64)
    con[:, C_ID:C_ID + P] = np.eye(P)
    con[:, C_ONE:C_ONE + P] = 1
    con[:, C_TRI:C_TRI + P] = np.triu(np.ones((P, P)), 1)

    def dft(n):
        a = 2 * np.pi * (np.outer(np.arange(n), np.arange(n)) % n) / n
        return np.cos(a) / np.sqrt(n), np.sin(a) / np.sqrt(n)

    cc, cs = dft(HD)
    for h in range(2):
        at = slice(HD * h, HD * h + HD)
        con[at, C_CC + HD * h:C_CC + HD * h + HD] = cc
        con[at, C_CS + HD * h:C_CS + HD * h + HD] = -cs
    con[:, C_XC:C_XC + P], con[:, C_XS:C_XS + P] = dft(CTX)
    for c in range(2):
        for h in range(2):
            w = (2, 4, 8, 16)[2 * c + h]
            at = slice(HD * h, HD * h + HD)
            con[at, C_WINV + c] = 1 / w
            t = np.arange(8)
            con[at, C_EDGE + c * 8:C_EDGE + c * 8 + 8] = w / np.minimum(w, t + w // 2)
            con[at, C_EDGE + (2 + c) * 8:C_EDGE + (2 + c) * 8 + 8] = w / np.minimum(w, 8 - t + w // 2)
    con[:, C_EID:C_EID + NE] = np.arange(NE)
    con[BLK:, C_HALF] = 1
    con[:, C_REV:C_REV + NE] = NE - np.arange(NE)
    for j in range(4):
        for s in range(2):
            con[32 * j + s, C_SEL + s] = 1
    f = np.float32
    t = np.arange(LAT)
    inv = (f(10000.0) ** (-np.arange(16, dtype=f) * f(2.0) / f(32))).astype(f)
    rope = np.zeros((P, 2, LT, HD), f)
    for a, pos in enumerate((t // 64, t % 64)):
        ang = (pos.astype(f)[:, None] * inv).astype(f)
        c, s = (np.cos(ang.astype(np.float64)).reshape(LT, P, 16).transpose(1, 0, 2),
                np.sin(ang.astype(np.float64)).reshape(LT, P, 16).transpose(1, 0, 2))
        for h in range(2):
            rope[:, 0, :, 32 * a + 16 * h:32 * a + 16 * h + 16] = c
            rope[:, 1, :, 32 * a + 16 * h:32 * a + 16 * h + 16] = s if h else -s
    return {
        "consts": con.astype(f), "rope": rope.reshape(P, -1), "dft": np.stack(dft(LAT)).astype(f),
        "token_ids": np.arange(2 * TOK, dtype=np.int32).reshape(2, NT, P).transpose(2, 0, 1).copy(),
        "table_init": np.full((P, TOK * NE // P), 2 * TOK, np.int32),
    }


def kernel(**inputs):
    import numpy as np
    import concourse.bacc as _bacc
    from concourse.bass_utils import run_bass_kernel_spmd as _run

    x = {k: np.asarray(v) for k, v in inputs.items()}

    def columns(v):
        return v.reshape(DEPTH, -1, P).transpose(0, 2, 1)

    arrays = host_constants(np)
    for k in ("x_prompt", "x_sample", "cache_k", "cache_v", "w_ada", "w_in", "w_attn_out", "w_pool_group",
              "w_pool_out", "w_fourier_out", "w_out", "w_expert_gate", "w_expert_up", "w_expert_down"):
        arrays[k] = np.ascontiguousarray(x[k])
    arrays["vecs"] = np.ascontiguousarray(np.concatenate([columns(x[k]) for k in (
        "b_ada", "norm_mix_pre", "norm_mix_post", "norm_ffn_pre", "norm_ffn_post", "pool_scale")], axis=2))
    arrays["c_cols"] = np.ascontiguousarray(np.stack([x["c"][0].reshape(DK, P).T, x["c_ctx"].reshape(DK, P).T], axis=2))
    arrays["gains"] = np.ascontiguousarray(np.broadcast_to(np.concatenate(
        [x["q_norm"]] * NH + [x["k_norm"]] * NKV, axis=1)[:, None, :], (DEPTH, P, NHEADS * HD)))
    arrays["router_b"] = np.ascontiguousarray(np.broadcast_to(np.concatenate(
        [x["b_router_group"], x["b_router_expert"]], axis=1)[:, None, :], (DEPTH, P, NR)))
    arrays["w_router"] = np.ascontiguousarray(np.concatenate([x["w_router_group"], x["w_router_expert"]], axis=2))

    nc = _bacc.Bacc("TRN2", target_bir_lowering=False, num_devices=1)
    A = {}
    for k, v in arrays.items():
        A[k] = nc.dram_tensor("in_" + k, v.shape, mybir.dt.from_np(v.dtype), kind="ExternalInput").ap()
    outs = [("out_p", (1, CTX, D)), ("out_s", (1, LAT, D)), ("out_k", (1, DEPTH, CTX, NKV, HD)),
            ("out_v", (1, DEPTH, CTX, NKV, HD))]
    for k, shape in outs:
        A[k] = nc.dram_tensor(k, shape, F32, kind="ExternalOutput").ap()
    A["h_rows"] = nc.dram_tensor("h_rows", (TOK, D), F32, kind="Internal").ap()
    A["y_half_rows"] = nc.dram_tensor("y_half_rows", (4 * TOK, D // 2), F32, kind="Internal").ap()
    A["table"] = nc.dram_tensor("table", (TOK * NE, 1), I32, kind="Internal").ap()
    trunk_kernel(nc, A, STEPS_PER_LAYER)
    r = _run(nc, [{"in_" + k: v for k, v in arrays.items()}], core_ids=[0])
    return tuple(r.results[0][k] for k, _ in outs)
```

```python
import concourse.bass as bass
from concourse import mybir
from contextlib import ExitStack

F32 = mybir.dt.float32
I32 = mybir.dt.int32
ALU = mybir.AluOpType
ACT = mybir.ActivationFunctionType
AX = mybir.AxisListType

P = 128
D = 1024
DK = D // P
DEPTH = 2
CTX, LAT = 128, 512
TOK = CTX + LAT
NT = TOK // P
LT = LAT // P
NH, NKV, HD = 8, 2, 64
QW, KW = NH * HD, NKV * HD
NHEADS = NH + NKV
POOLW = FOURW = 256
IN_W = QW + 2 * KW + POOLW + FOURW + 3 * D
KEYS = P + LAT
KALL = KEYS + CTX
SCALE = float(HD) ** -0.5
NG, EPG = 4, 8
NE = NG * EPG
NR = NG + NE
FF = 256
BLK = 64
XBLK = TOK // BLK - 1
EPS = 1e-6
BIG = 1e30
POOL_PAD = 8

C_ID, C_ONE, C_TRI, C_CC, C_CS, C_XC, C_XS = (i * P for i in range(7))
C_EDGE = 7 * P
C_WINV = C_EDGE + 32
C_EID = C_WINV + 2
C_REV = C_EID + NE
C_SEL = C_REV + NE
C_HALF = C_SEL + 2
NCONST = C_HALF + 1
V_BADA, V_MPRE, V_MPOST, V_FPRE, V_FPOST, V_PS = 0, 48, 56, 64, 72, 80
NVEC = 82

CHUNKS = ([("ada", 0, 1, 0), ("ada", 1, 1, 1), ("ada", 2, 1, 2), ("ada", 3, 1, 0), ("q", 0, 1, 1), ("kvx", 0, 2, 2),
           ("xp", 0, 1, 0), ("cos", 0, 1, 1), ("sin", 0, 1, 2), ("gate", 0, 1, 1), ("ada", 4, 1, 0), ("gate", 1, 1, 2)] +
          [("ada", 5, 1, 0), ("ada", 6, 1, 0), ("gate", 2, 1, 1), ("ada", 7, 1, 0), ("ada", 8, 1, 0), ("gate", 3, 1, 2),
           ("ada", 9, 1, 0), ("ada", 10, 1, 0), ("gate", 4, 1, 1), ("ada", 11, 1, 0), ("gate", 5, 1, 2)] +
          [("ao", 0, 2, 0), ("pf", 0, 2, 1), ("wo", 0, 1, 2), ("wo", 1, 1, 0)])
WSLOTS = 3
CHUNK_AT = {(name, i): c for c, (name, i, _, _) in enumerate(CHUNKS)}
EARLY = 4

USES = [("ada", c, c % 4, 2) for c in range(EARLY)]
USES += [("hT", k, k % 4, 1) for k in range(DK)]
for _i in range(NT):
    USES.append(("qkv", _i, _i % 2, 1))
    if _i:
        USES.append(("qkT", _i - 1, 2 + (_i - 1) % 2, 1))
USES.append(("qkT", NT - 1, 2, 1))
USES.append(("qkT", NT, 3, 1))
USES += [("xp", c, c, 1) for c in range(2)]
USES += [("dft", j, (2 + j) % 4, 1) for j in range(4)]
USES += [("plin", c, 2 + c, 1) for c in range(2)]
USES += [("four", c, c, 1) for c in range(2)]
NGATE = 3 * DK
FILL = ((2, 1, 1, 1), (2, 1, 1, 2))


def attention_steps():
    after_gate = {2: 5, 4: 6, 6: 7, 8: 8, 10: 9, 12: 10, 14: 11}
    halves = [("gates", (x, half)) for x in range(NGATE) for half in range(2)]
    steps = [("ada", 4), ("ctxS", 0)] + halves[0:2] + [("adacol", 4), ("ctxT", 0)] + halves[2:4] + [("ctxO", 0)]
    at, cols_due = 4, None
    for h in range(NH):
        for t in range(LT):
            steps.append(("S", (h, t)))
            if cols_due is not None:
                steps.append(("adacol", cols_due))
                cols_due = None
            n = FILL[h % 2][t]
            for step in halves[at:at + n]:
                steps.append(step)
                x, half = step[1]
                if half and x in after_gate:
                    assert cols_due is None
                    cols_due = after_gate[x]
                    steps.append(("ada", cols_due))
            at += n
        if cols_due is not None:
            steps.append(("adacol", cols_due))
            cols_due = None
        steps.append(("PV", h))
    assert at >= len(halves)
    return steps


STEPS = attention_steps()
_turn = 0
for _n, _x in STEPS:
    if _n == "ada":
        USES.append(("ada", _x, _turn, 2))
        _turn = 1 - _turn
    elif _n == "gates" and _x[1] == 0:
        USES.append(("gate", _x[0], _turn, 1))
        _turn = 1 - _turn
    elif _n == "S":
        USES.append(("S", _x, 2, 1))
    elif _n == "ctxS":
        USES.append(("ctxS", 0, 2, 1))
    elif _n == "ctxT":
        USES.append(("ctxT", 0, 3, 1))
    elif _n == "ctxO":
        USES.append(("ctxO", 0, 2, 1))
for _d in range(DK):
    USES += [(b, _d, (3 * _d + j) % 4, 1) for j, b in enumerate(("mattn", "mpool", "mfour"))]
USES += [("bc", v, v % 4, 1) for v in range(8)]
USES += [("mix", i, i % 2, 1) for i in range(NT)]
USES += [("h2T", i, 2, 1) for i in range(NT)]
USES += [("lg", 0, 3, 1), ("pos", 0, 0, 1)]


class Pairs:

    def __init__(self):
        self.at, self.full, self.free = {}, [0] * 4, [0] * 4
        for name, i, p, drains in USES:
            self.at[name, i] = (p, self.full[p], self.free[p])
            self.full[p] += 1
            self.free[p] += drains


PAIRS = Pairs()

PER = dict(
    dve_step=0, act_step=0, pool_step=0, ada_cols=12, affine_ready=1, rows_ready=1, x_sumsq=NT,
    rstd1=1, xn_ready=1, qk_raw=NT, qk_sq=NT, qk_rstd=NT, qk_rot=NT, pooled=2, cprob=1, cpn=1,
    smax=LT * NH, pnorm=LT * NH, tr_full=5 * NH, ptT0=5 * NH // 2, ptT1=5 * NH // 2, pv_full=NH, o_ready=NH, merged=DK,
    mix_sq=NT, mix_rstd=NT, x_mid=NT, x2_sq=NT, x2_rstd=NT, h_a=NT, h_b=NT, h_sent0=48, h_sent1=32, wr_in=16,
    sel_in=1, sel_exp=1, mask_ready=1, slots_ready=1, table_clear=16, table_set=16 * 2 * NT,
    table_read=32, ids_step=4, y_scaled=NT, y_sum=NT, y_sq=NT, y_rstd=NT, x_end=NT, layer_in=160, kv_out=32,
    xg_zero=1,
)


def trunk_kernel(nc, A, CH):
    ctx = ExitStack()
    with ctx:
        def sb(name, shape, dt=F32):
            return ctx.enter_context(nc.sbuf_tensor(name, shape, dt))

        def sem(name):
            return ctx.enter_context(nc.semaphore(name))

        X = sb("x_rows", [P, NT, D])
        HT = sb("h_T", [P, DK * TOK])
        G = sb("gates_mem", [P, NGATE * TOK])
        W = sb("w_ring", [P, WSLOTS, 4096])
        R = sb("attn_mem", [P, 13568])
        CON = sb("consts", [P, NCONST])
        VEC = sb("vectors", [P, NVEC])
        SILU = sb("silu_c", [P, DK, 32])
        MOD = sb("mod", [P, 6, DK, 2])
        AFF = sb("affine", [P, 4, DK, 2])
        ST = sb("stats", [P, 6, NT])

        hT = HT[:, :].rearrange("p (k t) -> p k t", k=DK)

        def cut(t, at, shape):
            n = 1
            for s in shape:
                n *= s
            v = t[:, at:at + n]
            if len(shape) == 1:
                return v
            names = "abcd"[:len(shape)]
            spec = " ".join(names)
            return v.rearrange(f"p ({spec}) -> p {spec}", **{c: s for c, s in zip(names[1:], shape[1:])})

        xn = cut(G, 0, (NT, D))
        AB = cut(G, 0, (4, TOK))
        PL = LAT + CTX + 4 * POOL_PAD
        pS = [cut(G, 4 * TOK + i * PL, (PL,)) for i in range(3)]
        XF = cut(G, 5120, (NT, FOURW))
        xpT = cut(G, 6400, (2, PL))
        qraw = cut(G, 7744, (2, 640))
        qsq = cut(G, 9024, (640,))
        qa = cut(G, 9664, (640,))
        qb = cut(G, 10304, (640,))
        qrot = cut(G, 10944, (2, 640))
        ROPE = cut(G, 12224, (2, LT, HD))
        GAIN = cut(G, 12736, (640,))
        pooled = cut(G, 9664, (2, TOK))
        qst = cut(G, 13376, (4, NHEADS))
        kc = cut(G, 13416, (KW,))
        WPG = cut(G, 13544, (2, P))
        TG = cut(G, 0, (3, DK, TOK))
        EW = [cut(G, e * 6144, (6144,)) for e in range(2)]
        wgu = [EW[e][:, 0:4096].rearrange("p (u k f) -> p u k f", u=2, k=DK) for e in range(2)]
        wdn = [EW[e][:, 4096:6144].rearrange("p (c n) -> p c n", c=2) for e in range(2)]
        qT = cut(R, 0, (4, TOK))
        kT = cut(R, 2560, (2, KALL))
        V = cut(R, 4096, (NT + 1, KW))
        PR = cut(R, 4864, (LT, KEYS))
        PT = cut(R, 7424, (2, 512))
        OT = cut(R, 8448, (4, TOK))
        PM = cut(R, 11008, (2, TOK))
        FM = cut(R, 12288, (2, TOK))
        part = cut(G, 14080, (2, 512))
        cP = cut(R, 4864, (NH, P))
        cPT = cut(R, 7424, (NH, P))
        aST = sb("attn_stats", [P, 3, 8])
        ROW = cut(R, 0, (8, D))
        hrow = cut(R, 8192, (2, D))
        tmix = cut(R, 10240, (2, D))
        rt = [cut(R, 10240 + 160 * i, (NT, NE)) for i in range(10)]
        WR = cut(G, 12288, (DK, NR))
        junk = cut(R, 12288, (D,))
        yg = [cut(R, 2 * D * i if i < 3 else 8192 + 2 * D * (i - 3), (2, D)) for i in range(NT)]
        xg = cut(HT, 0, (2, D))
        xT = cut(HT, 2048, (2, DK, BLK))
        GU = cut(HT, 3072, (2, FF))
        th = cut(HT, 3584, (2, BLK))
        hE = cut(HT, 3712, (2, 2, BLK))
        yb = cut(HT, 3968, (2, 512))
        RS = sb("router_small", [P, 8, NT])
        SLOT = sb("slots", [P, 2, NT], I32)
        TID = sb("assignment_ids", [P, 2, NT], I32)
        IDX = cut(G, 13000, (3, NE + 2)).bitcast(I32)
        RB = sb("router_bias", [P, NR])
        MOST = sb("largest_count", [P, 1], I32)
        HALF = sb("minus_half", [P, NHEADS])
        IDC = sb("row_ids_now", [P, 4], I32)
        EX = cut(R, 11840, (2, NT, 5))
        sg = cut(HT, 4992, (2, BLK))

        PS = ctx.enter_context(nc.psum_tensor("ps", [P, 8, 512], F32))

        def bank(b):
            return PS[:, b, :]

        def pair(p):
            return PS[:, 2 * p:2 * p + 2, :].rearrange("p b n -> p (b n)")

        S = {name: sem(name) for name in PER}
        per = dict(PER)
        per.update(CH)
        full = [sem(f"psum_full{p}") for p in range(4)]
        free = [sem(f"psum_free{p}") for p in range(4)]
        loaded = [sem(f"chunk_loaded{s}") for s in range(WSLOTS)]
        const_in, x_in = sem("const_in"), sem("x_in")
        aside = sem("aside")
        f_turn = sem("more_turns")
        silu_a, silu_b = sem("silu_tanh"), sem("silu_ready")
        setup = sem("setup_done")
        done = sem("outputs_stored")
        ex_loaded = [sem(f"expert_loaded{e}") for e in range(2)]
        dn_loaded = [sem(f"expert_down_loaded{e}") for e in range(2)]
        rows_in = [sem(f"expert_rows{e}") for e in range(2)]
        idc = [sem(f"gather_ids_copied{e}") for e in range(2)]
        idy = [sem(f"scatter_ids_copied{e}") for e in range(2)]
        yg_in = [sem(f"y_gathered{i}") for i in range(NT)]
        xT_full, xT_out = sem("ex_xT_full"), sem("ex_xT_out")
        gu_full, gu_out, gt_full = sem("ex_gu_full"), sem("ex_gu_out"), sem("ex_gt_full")
        th_out, sg_out, h_out = sem("ex_tanh"), sem("ex_silu"), sem("ex_h")
        dn_full, y_out = sem("ex_down_full"), sem("ex_y_out")
        y_sent = [sem(f"ex_y_sent{e}") for e in range(2)]
        f_ids, f_step, f_gathered, f_sent = sem("more_ids"), sem("more_ids_step"), sem("more_gathered"), sem("more_sent")
        f_rows, f_loaded, f_done = sem("more_rows_in"), sem("more_weights_in"), sem("more_block_done")
        f_xT, f_xo, f_gu, f_go, f_gt = sem("more_xT"), sem("more_xT_out"), sem("more_gu"), sem("more_gu_out"), sem("more_gt")
        f_th, f_sg, f_h, f_dn, f_y = sem("more_tanh"), sem("more_silu"), sem("more_h"), sem("more_down"), sem("more_y_out")
        count = {"dve_step": 0, "act_step": 0, "pool_step": 0}

        def upto(name, l, n):
            return l * per[name] + n

        chunk_dmas = [[0] for _ in range(WSLOTS)]
        nth_of_slot, last_of_slot = [], []
        for c, (_, _, n, s) in enumerate(CHUNKS):
            before = [b for b in range(c) if CHUNKS[b][3] == s]
            nth_of_slot.append(len(before))
            last_of_slot.append(before[-1] if before else None)
            chunk_dmas[s].append(chunk_dmas[s][-1] + 16 * n)

        def chunk(name, i=0):
            c = CHUNK_AT[name, i]
            s = CHUNKS[c][3]
            return s, chunk_dmas[s][nth_of_slot[c] + 1]

        def loaded_at(l, name, i=0):
            s, n = chunk(name, i)
            return loaded[s], l * chunk_dmas[s][-1] + n

        def used_at(l, c):
            name, i, _, _ = CHUNKS[c]
            return filled_at(l, *{"ada": ("ada", i), "q": ("qkv", NT - 1), "kvx": ("qkv", NT - 1), "xp": ("xp", 1),
                                  "cos": ("dft", 1), "sin": ("dft", 3), "gate": ("gate", 4 * i + 3),
                                  "ao": ("mattn", DK - 1), "pf": ("mfour", DK - 1), "wo": ("mix", NT - 1)}[name])

        def freed_at(l, name, i):
            p, _, n = PAIRS.at[name, i]
            return free[p], l * PAIRS.free[p] + n + 1

        def filled_at(l, name, i):
            p, n, _ = PAIRS.at[name, i]
            return full[p], l * PAIRS.full[p] + n + 1

        def drained_at(l, name, i):
            p, _, n = PAIRS.at[name, i]
            return free[p], l * PAIRS.free[p] + n + 2

        def pair_of(name, i):
            return PAIRS.at[name, i][0]

        def cols(base):
            return CON[:, base:base + P]

        ident, ones, tri = cols(C_ID), cols(C_ONE), cols(C_TRI)

        def stream(n):
            return slice(0, LAT) if n == 0 else slice(LAT, TOK)

        def further_blocks(eng, l, body, mine):
            eng.wait_ge(S["slots_ready"], upto("slots_ready", l, 1))
            eng.sem_inc(aside, 1)
            most = eng.value_load(MOST[0:1, 0:1], min_val=0, max_val=TOK)
            with eng.If(most > BLK):
                with eng.Fori(1, XBLK + 1) as b:
                    with eng.If(most > b * BLK):
                        with eng.Fori(0, NE) as e:
                            body(b, e, (l * XBLK + b - 1) * NE + e)
                    with eng.Else():
                        for s, n in mine:
                            eng.sem_inc(s, n * NE)
                    if eng.engine == nc.gpsimd.engine:
                        eng.sem_inc(f_turn, 1)
                    else:
                        eng.wait_ge(f_turn, l * XBLK + b)
                        eng.sem_inc(aside, 1)
            with eng.Else():
                for s, n in mine:
                    eng.sem_inc(s, n * NE * XBLK)
                if eng.engine == nc.gpsimd.engine:
                    eng.sem_inc(f_turn, XBLK)
            if eng.engine != nc.gpsimd.engine:
                eng.wait_ge(f_turn, l * XBLK + XBLK)
                eng.sem_inc(aside, 1)

        block = ctx.enter_context(nc.Block())

        @block.sync
        def _(sp):
            def small(dst, src):
                sp.dma_start(dst, src).then_inc(S["layer_in"], 16)

            def small_inputs(l):
                small(VEC[:, :], A["vecs"][bass.ds(l, 1)].rearrange("a p n -> p (a n)"))
                small(RB[:, :], A["router_b"][bass.ds(l, 1)].rearrange("a p n -> p (a n)"))
                small(GAIN, A["gains"][bass.ds(l, 1)].rearrange("a p n -> p (a n)"))
                small(ROPE.rearrange("p a b c -> p (a b c)"), A["rope"])
                small(kc, A["cache_k"][0, bass.ds(l, 1)].rearrange("a p h d -> p (a h d)"))
                sp.wait_ge(setup, l + 2)
                sp.sem_inc(aside, 1)
                for g in range(4):
                    h = g % 2
                    small(WPG[HD * h:HD * h + HD, g // 2, HD * h:HD * h + HD],
                          A["w_pool_group"][bass.ds(l, 1), g].rearrange("a c d -> c (a d)"))
                sp.dma_start(A["table"].rearrange("(p n) a -> p (n a)", p=P), A["table_init"])\
                    .then_inc(S["table_clear"], 16)

            sp.dma_start(SILU[:, :, 0:2], A["c_cols"]).then_inc(const_in, 16)
            sp.dma_start(CON[:, :], A["consts"]).then_inc(const_in, 16)
            with sp.Fori(0, DEPTH) as l:
                for c, (name, i, _, s) in enumerate(CHUNKS):
                    slot = W[:, s, :]
                    if c == WSLOTS:
                        small_inputs(l)
                    if (name, i) == ("cos", 0):
                        sp.wait_ge(S["x_end"], upto("x_end", l, NT))
                        sp.sem_inc(aside, 1)
                        small(V[:, 0, :], A["cache_v"][0, bass.ds(l, 1)].rearrange("a p h d -> p (a h d)"))
                    if last_of_slot[c] is not None:
                        sp.wait_ge(*used_at(l, last_of_slot[c]))
                    k8 = slot.rearrange("p (k n) -> p k n", k=DK)

                    def w_cols(w, a, b):
                        return w[bass.ds(l, 1), :, a:b].rearrange("a (k p) n -> p (a k) n", p=P)

                    if name == "ada":
                        sp.dma_start(k8, w_cols(A["w_ada"], 512 * i, 512 * i + 512)).then_inc(loaded[s], 16)
                    elif name == "q":
                        sp.dma_start(k8, w_cols(A["w_in"], 0, QW)).then_inc(loaded[s], 16)
                    elif name == "kvx":
                        sp.dma_start(k8[:, :, 0:256], w_cols(A["w_in"], QW, QW + 256)).then_inc(loaded[s], 16)
                        sp.dma_start(k8[:, :, 256:512], w_cols(A["w_in"], 1024, 1280)).then_inc(loaded[s], 16)
                    elif name == "xp":
                        sp.dma_start(slot[:, 0:2048].rearrange("p (k n) -> p k n", k=DK),
                                     w_cols(A["w_in"], 768, 1024)).then_inc(loaded[s], 16)
                    elif name in ("cos", "sin"):
                        src = A["dft"][0 if name == "cos" else 1].rearrange("(k p) n -> p k n", p=P)
                        sp.dma_start(slot[:, 0:2048].rearrange("p (k n) -> p k n", k=LT), src).then_inc(loaded[s], 16)
                    elif name == "gate":
                        sp.dma_start(k8, w_cols(A["w_in"], 1280 + 512 * i, 1792 + 512 * i)).then_inc(loaded[s], 16)
                    elif name == "ao":
                        v = A["w_attn_out"][bass.ds(l, 1)].rearrange("a (s j p) n -> s p (a j) n", s=2, p=HD)
                        for h in range(2):
                            sp.dma_start(slot[HD * h:HD * h + HD, :].rearrange("p (j n) -> p j n", j=4),
                                         v[h]).then_inc(loaded[s], 16)
                    elif name == "pf":
                        for h, w in enumerate(("w_pool_out", "w_fourier_out")):
                            sp.dma_start(slot[:, 2048 * h:2048 * h + 2048].rearrange("p (k n) -> p k n", k=2),
                                         w_cols(A[w], 0, D)).then_inc(loaded[s], 16)
                    else:
                        sp.dma_start(k8, w_cols(A["w_out"], 512 * i, 512 * i + 512)).then_inc(loaded[s], 16)
                sp.wait_ge(S["merged"], upto("merged", l, DK))
                sp.sem_inc(aside, 1)
                with sp.Fori(0, NE // 2) as it:
                    for e in range(2):
                        n = (l * (NE // 2) + it) * 2 + e
                        ex = bass.ds(it * 2 + e, 1)
                        sp.wait_ge(gu_full, n + 1)
                        sp.sem_inc(aside, 1)
                        for u, w in enumerate(("w_expert_gate", "w_expert_up")):
                            sp.dma_start(wgu[e][:, u], A[w][bass.ds(l, 1), ex].rearrange("a b (p k) f -> p (a b k) f", p=P))\
                              .then_inc(ex_loaded[e], 16)
                        sp.wait_ge(dn_full, n + 1)
                        sp.sem_inc(aside, 1)
                        sp.dma_start(wdn[e], A["w_expert_down"][bass.ds(l, 1), ex].rearrange("a b (p c) n -> p (a b c) n", p=P))\
                          .then_inc(dn_loaded[e], 16)

                def weights_again(b, e, n):
                    sp.wait_ge(f_rows, n + 1)
                    sp.sem_inc(aside, 1)
                    ex = bass.ds(e, 1)
                    for u, w in enumerate(("w_expert_gate", "w_expert_up")):
                        sp.dma_start(wgu[0][:, u], A[w][bass.ds(l, 1), ex].rearrange("a b (p k) f -> p (a b k) f", p=P))\
                          .then_inc(f_loaded, 16)
                    sp.dma_start(wdn[0], A["w_expert_down"][bass.ds(l, 1), ex].rearrange("a b (p c) n -> p (a b c) n", p=P))\
                      .then_inc(f_loaded, 16)
                    sp.wait_ge(f_loaded, 48 * n + 48)
                    sp.sem_inc(aside, 1)

                further_blocks(sp, l, weights_again, [(f_loaded, 48)])

        @block.gpsimd
        def _(pool):
            def hold(s, value):
                pool.wait_ge(s, value)
                pool.sem_inc(aside, 1)

            def link(l, ins):
                count["pool_step"] += 1
                ins.then_inc(S["pool_step"], 1)
                hold(S["pool_step"], upto("pool_step", l, count["pool_step"]))

            for k in range(2):
                pool.dma_start(TID[:, k, :], A["token_ids"][:, k, :]).then_inc(y_sent[k], 16)

            def rstd(l, wait, n, src, dst, inc):
                hold(S[wait], upto(wait, l, n))
                link(l, pool.tensor_scalar(dst, src, 1.0 / D, EPS, ALU.mult, ALU.add))
                w = dst.shape[1]
                pool.tensor_tensor(dst, dst, HALF[:, 0:w], ALU.pow).then_inc(S[inc], 1)

            for k in range(2):
                pool.wait_ge(y_sent[k], 16)
            pool.memset(HALF[:, :], -0.5).then_inc(setup, 1)
            pool.wait_ge(setup, 1)
            pool.memset(WPG, 0.0).then_inc(setup, 1)
            blocks16 = pool.alloc_register("blocks16")
            pool.reg_mov(blocks16, 0)
            with pool.Fori(0, DEPTH) as l:
                count["pool_step"] = 0
                rstd(l, "x_sumsq", NT, ST[:, 0, :], ST[:, 1, :], "rstd1")
                for i in range(NT):
                    hold(S["qk_sq"], upto("qk_sq", l, i + 1))
                    a, b = qst[:, (i % 2) * 2, :], qst[:, (i % 2) * 2 + 1, :]
                    link(l, pool.tensor_scalar(b, a, 1.0 / HD, EPS, ALU.mult, ALU.add))
                    pool.tensor_tensor(b, b, HALF[:, 0:NHEADS], ALU.pow).then_inc(S["qk_rstd"], 1)
                hold(S["merged"], upto("merged", l, DK))
                hold(*filled_at(l, "bc", 0))
                pool.dma_start(WR, A["w_router"][bass.ds(l, 1)].rearrange("a (k p) n -> p (a k) n", p=P))\
                    .then_inc(S["wr_in"], 16)
                for i in range(NT):
                    rstd(l, "mix_sq", i + 1, ST[:, 2, i:i + 1], ST[:, 3, i:i + 1], "mix_rstd")
                    rstd(l, "x2_sq", i + 1, ST[:, 4, i:i + 1], ST[:, 5, i:i + 1], "x2_rstd")
                    s = 0 if i < LT else 1
                    hold(S["h_a"], upto("h_a", l, i + 1))
                    pool.tensor_tensor(hrow[:, i % 2, :], hrow[:, i % 2, :], ROW[:, 4 + s, :], ALU.add)\
                        .then_inc(S["h_b"], 1)
                    hold(S["h_b"], upto("h_b", l, i + 1))
                    pool.dma_start(A["h_rows"][P * i:P * i + P, :], hrow[:, i % 2, :])\
                        .then_inc(S[f"h_sent{i % 2}"], 16)
                hold(S["slots_ready"], upto("slots_ready", l, 1))
                hold(S["table_clear"], upto("table_clear", l, 16))
                for k in range(2):
                    for i in range(NT):
                        pool.indirect_dma_start(
                            out=A["table"], out_offset=bass.IndirectOffsetOnAxis(ap=SLOT[:, k, i:i + 1], axis=0),
                            in_=TID[:, k, i:i + 1], in_offset=None).then_inc(S["table_set"], 16)
                hold(S["table_set"], upto("table_set", l, 16 * 2 * NT))
                pool.memset(IDX[:, 0, NE:NE + 2], 2 * TOK).then_inc(S["ids_step"], 1)
                for h in range(2):
                    pool.dma_start(IDX[BLK * h:BLK * h + BLK, 0, 0:NE],
                                   A["table"][0:BLK * NE].rearrange("(p e) a -> p (e a)", e=NE))\
                        .then_inc(S["table_read"], 16)
                hold(S["table_read"], upto("table_read", l, 32))
                hold(S["ids_step"], upto("ids_step", l, 1))
                pool.tensor_scalar(IDX[:, 1, :], IDX[:, 0, :], float(TOK), -float(TOK), ALU.is_ge, ALU.mult)\
                    .then_inc(S["ids_step"], 1)
                pool.tensor_scalar(IDX[:, 2, :], IDX[:, 0, :], 2.0, CON[:, C_HALF:C_HALF + 1], ALU.mult, ALU.add)\
                    .then_inc(S["ids_step"], 1)
                hold(S["ids_step"], upto("ids_step", l, 3))
                pool.tensor_tensor(IDX[:, 1, :], IDX[:, 1, :], IDX[:, 0, :], ALU.add).then_inc(S["ids_step"], 1)
                hold(S["ids_step"], upto("ids_step", l, 4))
                for e in range(2):
                    hold(S[f"h_sent{e}"], upto(f"h_sent{e}", l, per[f"h_sent{e}"]))
                hold(*filled_at(l, "pos", 0))
                pool.memset(HT[0:BLK, 0:2 * D], 0.0).then_inc(S["xg_zero"], 1)
                hold(S["xg_zero"], upto("xg_zero", l, 1))

                def gather(e, nth, col):
                    pool.tensor_copy(IDC[0:BLK, e:e + 1], IDX[0:BLK, 1, bass.ds(col, 1)]).then_inc(idc[e], 1)
                    hold(idc[e], nth)
                    pool.indirect_dma_start(
                        out=xg[0:BLK, e, :], out_offset=None, in_=A["h_rows"],
                        in_offset=bass.IndirectOffsetOnAxis(ap=IDC[0:BLK, e:e + 1], axis=0),
                        bounds_check=TOK - 1, oob_is_err=False).then_inc(rows_in[e], 16)

                for e in range(2):
                    gather(e, l * (NE // 2 + 1) + 1, e)
                with pool.Fori(0, NE // 2) as it:
                    q = l * (NE // 2) + it
                    for e in range(2):
                        hold(xT_full, q * 2 + e + 3)
                        hold(rows_in[e], (q + l) * 16 + 16)
                        gather(e, q + l + 2, it * 2 + 2 + e)
                    for e in range(2):
                        hold(y_out, q * 2 + e + 3)
                        pool.tensor_copy(IDC[:, 2 + e:3 + e], IDX[:, 2, bass.ds(it * 2 + e, 1)]).then_inc(idy[e], 1)
                        hold(idy[e], q + 1)
                        pool.indirect_dma_start(
                            out=A["y_half_rows"], out_offset=bass.IndirectOffsetOnAxis(ap=IDC[:, 2 + e:3 + e], axis=0),
                            in_=yb[:, e, :], in_offset=None,
                            bounds_check=4 * TOK - 1, oob_is_err=False).then_inc(y_sent[e], 16)
                for e in range(2):
                    hold(y_sent[e], (l + 1) * (NE // 2) * 16 + 16)

                def more_rows(b, e, n):
                    pool.reg_add(blocks16, blocks16, 16)
                    in_all = pool.snap(blocks16)
                    ids = A["table"].rearrange("(b p x) a -> b p (x a)", p=BLK, x=NE)[bass.ds(b, 1)]
                    for h in range(2):
                        pool.dma_start(IDX[BLK * h:BLK * h + BLK, 0, 0:NE], ids.rearrange("b p x -> p (b x)"))\
                            .then_inc(f_ids, 16)
                    hold(f_ids, in_all * 2)
                    now, token, half = IDC[:, 3:4], IDX[:, 1, 0:1], IDX[:, 2, 0:1]
                    pool.tensor_copy(now, IDX[:, 0, bass.ds(e, 1)]).then_inc(f_step, 1)
                    hold(f_step, 4 * n + 1)
                    pool.tensor_scalar(token, now, float(TOK), -float(TOK), ALU.is_ge, ALU.mult).then_inc(f_step, 1)
                    pool.tensor_scalar(half, now, 2.0, CON[:, C_HALF:C_HALF + 1], ALU.mult, ALU.add).then_inc(f_step, 1)
                    hold(f_step, 4 * n + 3)
                    pool.tensor_tensor(IDC[0:BLK, 0:1], token[0:BLK], now[0:BLK], ALU.add).then_inc(f_step, 1)
                    hold(f_step, 4 * n + 4)
                    pool.indirect_dma_start(
                        out=xg[0:BLK, 0, :], out_offset=None, in_=A["h_rows"],
                        in_offset=bass.IndirectOffsetOnAxis(ap=IDC[0:BLK, 0:1], axis=0),
                        bounds_check=TOK - 1, oob_is_err=False).then_inc(f_gathered, 16)
                    hold(f_gathered, in_all)
                    pool.sem_inc(f_rows, 1)
                    hold(f_y, n + 1)
                    pool.tensor_copy(IDC[:, 2:3], half).then_inc(f_done, 1)
                    hold(f_done, n + 1)
                    pool.indirect_dma_start(
                        out=A["y_half_rows"], out_offset=bass.IndirectOffsetOnAxis(ap=IDC[:, 2:3], axis=0),
                        in_=yb[:, 0, :], in_offset=None,
                        bounds_check=4 * TOK - 1, oob_is_err=False).then_inc(f_sent, 16)
                    hold(f_sent, in_all)

                for e in range(2):
                    hold(rows_in[e], (l + 1) * (NE // 2 + 1) * 16)
                further_blocks(pool, l, more_rows, [(f_step, 4), (f_rows, 1), (f_done, 1)])
                for i in range(NT):
                    pool.dma_start(yg[i].rearrange("p k (h n) -> p k h n", h=2),
                                   A["y_half_rows"].rearrange("(k t h) n -> t k h n", k=2, h=2)[P * i:P * i + P])\
                        .then_inc(yg_in[i], 16)
                pool.memset(WPG, 0.0).then_inc(setup, 1)
                for i in range(NT):
                    rstd(l, "y_sq", i + 1, ST[:, 2, i:i + 1], ST[:, 3, i:i + 1], "y_rstd")

        @block.scalar
        def _(act):
            def link(l, ins):
                count["act_step"] += 1
                ins.then_inc(S["act_step"], 1)
                act.wait_ge(S["act_step"], upto("act_step", l, count["act_step"]))

            act.dma_start(X[:, 0:LT, :], A["x_sample"][0].rearrange("(i p) n -> p i n", p=P)).then_inc(x_in, 16)
            act.dma_start(X[:, LT, :], A["x_prompt"][0]).then_inc(x_in, 16)
            act.wait_ge(const_in, 32)
            act.activation(SILU[:, :, 2:4], SILU[:, :, 0:2], ACT.Tanh, scale=0.5).then_inc(silu_a, 1)
            act.wait_ge(x_in, 32)
            with act.Fori(0, DEPTH) as l:
                count["act_step"] = 0
                for i in range(NT):
                    act.wait_ge(S["x_end"], upto("x_end", l, i + 1))
                    act.activation(junk, X[:, i, :], ACT.Square, accum_out=ST[:, 0, i:i + 1])\
                       .then_inc(S["x_sumsq"], 1)
                    act.wait_ge(S["x_sumsq"], upto("x_sumsq", l, i + 1))
                def partial_sums(c):
                    p = pair_of("ada", c)
                    act.wait_ge(*filled_at(l, "ada", c))
                    if c >= 2:
                        act.wait_ge(S["ada_cols"], upto("ada_cols", l, c - 1))
                    act.activation(part[:, c % 2, :], bank(2 * p), ACT.Copy).then_inc(free[p], 1)

                for c in range(EARLY):
                    partial_sums(c)
                act.wait_ge(S["affine_ready"], upto("affine_ready", l, 1))
                for k in range(0, DK, 2):
                    act.wait_ge(*filled_at(l, "hT", k))
                    for s in range(2):
                        ins = act.activation(hT[:, k, stream(s)], pair(pair_of("hT", k))[:, stream(s)], ACT.Identity,
                                             bias=MOD[:, 0, k, s:s + 1], scale=AFF[:, 0, k, s:s + 1])
                    ins.then_inc(free[pair_of("hT", k)], 1)
                def qkT(i):
                    act.wait_ge(*filled_at(l, "qkT", i))
                    p = pair_of("qkT", i)
                    to = slice(P * i, P * i + P)
                    if i < NT:
                        act.activation(qT[:, :, to], bank(2 * p).rearrange("p (j t) -> p j t", j=4), ACT.Copy)
                        to = slice(P + P * i, 2 * P + P * i)
                    else:
                        to = slice(0, P)
                    for s in range(2):
                        h = slice(HD * s, HD * s + HD)
                        ins = act.activation(kT[h, s, to], PS[h, 2 * p + 1, 0:P], ACT.Copy)
                    ins.then_inc(free[p], 1)

                for i in range(NT):
                    act.wait_ge(*filled_at(l, "qkv", i))
                    p = pair(pair_of("qkv", i))
                    if i >= 2:
                        act.wait_ge(S["qk_rot"], upto("qk_rot", l, i - 1))
                    act.activation(qraw[:, i % 2, :], p[:, 0:640], ACT.Copy).then_inc(S["qk_raw"], 1)
                    if i == NT - 1:
                        link(l, act.activation(V[:, 1 + i, :], p[:, 640:768], ACT.Copy))
                        act.dma_start(A["out_v"][0, bass.ds(l, 1)].rearrange("a p h d -> p (a h d)"), V[:, 1 + i, :])\
                           .then_inc(S["kv_out"], 16)
                    else:
                        act.activation(V[:, 1 + i, :], p[:, 640:768], ACT.Copy)
                    act.activation(XF[:, i, :], p[:, 768:1024], ACT.Copy).then_inc(free[pair_of("qkv", i)], 1)
                    if i:
                        qkT(i - 1)
                act.wait_ge(S["qk_rot"], upto("qk_rot", l, NT))
                act.dma_start(A["out_k"][0, bass.ds(l, 1)].rearrange("a p h d -> p (a h d)"),
                              qrot[:, (NT - 1) % 2, QW:640]).then_inc(S["kv_out"], 16)
                qkT(NT - 1)
                qkT(NT)
                for c in range(2):
                    act.wait_ge(*filled_at(l, "xp", c))
                    p = pair(c)
                    act.activation(xpT[:, c, POOL_PAD:POOL_PAD + LAT], p[:, 0:LAT], ACT.Copy)
                    act.activation(xpT[:, c, 3 * POOL_PAD + LAT:3 * POOL_PAD + TOK], p[:, LAT:TOK], ACT.Copy)\
                       .then_inc(free[c], 1)
                for j in range(4):
                    act.wait_ge(*filled_at(l, "dft", j))
                    act.activation(AB[:, j, :], pair(pair_of("dft", j))[:, 0:TOK], ACT.Copy)\
                       .then_inc(free[pair_of("dft", j)], 1)
                for c in range(2):
                    act.wait_ge(*filled_at(l, "plin", c))
                    act.activation(PM[:, c, :], pair(pair_of("plin", c))[:, 0:TOK], ACT.Copy,
                                   scale=VEC[:, V_PS + c:V_PS + c + 1]).then_inc(free[pair_of("plin", c)], 1)
                for c in range(2):
                    act.wait_ge(*filled_at(l, "four", c))
                    act.activation(FM[:, c, :], pair(pair_of("four", c))[:, 0:TOK], ACT.Copy)\
                       .then_inc(free[pair_of("four", c)], 1)
                act.wait_ge(S["kv_out"], upto("kv_out", l, 32))
                n_s = 0
                for what, x in STEPS:
                    if what == "ada":
                        partial_sums(x)
                    elif what == "ctxS":
                        act.wait_ge(*drained_at(l, "ctxS", 0))
                        act.activation(cP.rearrange("p h t -> p (h t)"), cP.rearrange("p h t -> p (h t)"), ACT.Exp,
                                       scale=SCALE).then_inc(S["cprob"], 1)
                    elif what == "ctxT":
                        act.wait_ge(*filled_at(l, "ctxT", 0))
                        act.activation(cPT.rearrange("p h t -> p (h t)"), pair(3), ACT.Copy).then_inc(free[3], 1)
                    elif what == "gates" and x[1]:
                        g, p = x[0], pair_of("gate", x[0])
                        act.wait_ge(*filled_at(l, "gate", g))
                        act.activation(TG[:, g // DK, g % DK, :], pair(p)[:, 0:TOK], ACT.Tanh, scale=0.5)\
                           .then_inc(free[p], 1)
                    elif what == "S":
                        h, t = x
                        n_s += 1
                        act.wait_ge(S["smax"], upto("smax", l, n_s))
                        if h:
                            act.wait_ge(S["tr_full"], upto("tr_full", l, 5 * h))
                        act.activation(PR[:, t, :], pair(2)[:, 0:KEYS], ACT.Exp, scale=SCALE,
                                       bias=aST[:, 0, t:t + 1], accum_out=aST[:, 1, t:t + 1]).then_inc(free[2], 1)
                    elif what == "PV":
                        for kt in range(5):
                            n = 5 * x + kt
                            if n % 2:
                                act.wait_ge(S["tr_full"], upto("tr_full", l, n + 1))
                                act.activation(PT[:, 1, :], bank((6, 4)[kt % 2]), ACT.Copy).then_inc(S[f"ptT{n % 2}"], 1)
                for v in range(8):
                    act.wait_ge(*filled_at(l, "bc", v))
                    act.activation(ROW[:, v, :], pair(v % 4), ACT.Copy).then_inc(free[v % 4], 1)
                for i in range(NT + 1):
                    if i < NT:
                        act.wait_ge(*filled_at(l, "mix", i))
                        act.activation(junk, pair(i % 2), ACT.Square, scale=0.5, accum_out=ST[:, 2, i:i + 1])\
                           .then_inc(S["mix_sq"], 1)
                        act.wait_ge(S["mix_sq"], upto("mix_sq", l, i + 1))
                    if i:
                        j = i - 1
                        act.wait_ge(*filled_at(l, "h2T", j))
                        p = pair_of("h2T", j)
                        act.activation(hT[:, :, P * j:P * j + P], pair(p).rearrange("p (k t) -> p k t", k=DK),
                                       ACT.Copy).then_inc(free[p], 1)
                    if i < NT:
                        act.wait_ge(S["x_mid"], upto("x_mid", l, i + 1))
                        act.activation(junk, X[:, i, :], ACT.Square, accum_out=ST[:, 4, i:i + 1])\
                           .then_inc(S["x2_sq"], 1)
                        act.wait_ge(S["x2_sq"], upto("x2_sq", l, i + 1))
                act.wait_ge(S["sel_in"], upto("sel_in", l, 1))
                act.activation(EX[:, 1], EX[:, 0], ACT.Exp).then_inc(S["sel_exp"], 1)
                with act.Fori(0, NE // 2) as it:
                    n = (l * (NE // 2) + it) * 2

                    def x_out(e):
                        act.wait_ge(xT_full, n + e + 3)
                        act.wait_ge(gu_full, n + e + 1)
                        act.activation(xT[:, e].rearrange("p k t -> p (k t)"), bank(e), ACT.Copy).then_inc(xT_out, 1)

                    def tanh(e):
                        act.wait_ge(gt_full, n + e + 3)
                        act.wait_ge(h_out, n + e + 2)
                        act.activation(th, bank(4 + e)[:, 0:256].rearrange("p (c t) -> p c t", c=2)[:, :, 0:BLK],
                                       ACT.Tanh, scale=0.5).then_inc(th_out, 1)

                    def y_rows(e):
                        act.wait_ge(dn_full, n + e + 3)
                        act.wait_ge(y_sent[e], (l * (NE // 2) + it) * 16 + 16)
                        act.activation(yb[:, e, :], bank(6 + e), ACT.Copy, scale=0.5).then_inc(y_out, 1)

                    x_out(0)
                    x_out(1)
                    tanh(0)
                    y_rows(0)
                    tanh(1)
                    y_rows(1)

                def more_act(b, e, n):
                    act.wait_ge(f_xT, n + 1)
                    act.activation(xT[:, 0].rearrange("p k t -> p (k t)"), bank(0), ACT.Copy).then_inc(f_xo, 1)
                    act.wait_ge(f_gt, n + 1)
                    act.activation(th, bank(4)[:, 0:256].rearrange("p (c t) -> p c t", c=2)[:, :, 0:BLK],
                                   ACT.Tanh, scale=0.5).then_inc(f_th, 1)
                    act.wait_ge(f_dn, n + 1)
                    act.activation(yb[:, 0, :], bank(6), ACT.Copy, scale=0.5).then_inc(f_y, 1)

                further_blocks(act, l, more_act, [(f_xo, 1), (f_th, 1), (f_y, 1)])
                for i in range(NT + 1):
                    if i < NT:
                        act.wait_ge(yg_in[i], l * 16 + 16)
                        act.activation(yg[i][:, 0, :], yg[i][:, 0, :], ACT.Copy, scale=RS[:, 5, i:i + 1])\
                           .then_inc(S["y_scaled"], 1)
                    if i:
                        j = i - 1
                        act.wait_ge(S["y_sum"], upto("y_sum", l, i))
                        act.activation(junk, yg[j][:, 0, :], ACT.Square, accum_out=ST[:, 2, j:j + 1])\
                           .then_inc(S["y_sq"], 1)
                        act.wait_ge(S["y_sq"], upto("y_sq", l, i))
            act.wait_ge(S["x_end"], (DEPTH + 1) * per["x_end"])
            act.dma_start(A["out_s"][0].rearrange("(i p) n -> p i n", p=P), X[:, 0:LT, :]).then_inc(done, 16)
            act.dma_start(A["out_p"][0], X[:, LT, :]).then_inc(done, 16)
            act.wait_ge(done, 32)
            act.wait_ge(S["kv_out"], DEPTH * 32)

        @block.vector
        def _(dve):
            def link(l, ins):
                count["dve_step"] += 1
                ins.then_inc(S["dve_step"], 1)
                dve.wait_ge(S["dve_step"], upto("dve_step", l, count["dve_step"]))

            def bc(ap, axis, shape):
                return ap.unsqueeze(axis).broadcast_to([P] + list(shape))

            for p in range(4):
                dve.sem_inc(free[p], 1)
            dve.sem_inc(S["x_end"], per["x_end"])
            for s in (xT_full, xT_out, gu_full, gu_out, gt_full, h_out, dn_full, y_out):
                dve.sem_inc(s, 2)
            dve.wait_ge(const_in, 32)
            dve.wait_ge(silu_a, 1)
            dve.scalar_tensor_tensor(SILU[:, :, 0:2], SILU[:, :, 2:4], 1.0, SILU[:, :, 0:2], ALU.add, ALU.mult)\
               .then_inc(silu_b, 1)
            dve.wait_ge(silu_b, 1)
            dve.tensor_scalar(SILU[:, :, 0:2], SILU[:, :, 0:2], 0.5, None, ALU.mult).then_inc(silu_b, 1)
            dve.memset(SILU[:, :, 2:32], 0.0).then_inc(silu_b, 1)

            with dve.Fori(0, DEPTH) as l:
                count["dve_step"] = 0
                dve.wait_ge(S["x_end"], upto("x_end", l, NT))
                dve.memset(kT[HD:P, 0, :], 0.0)
                dve.memset(kT[0:HD, 1, :], 0.0)
                for a, b in ((0, POOL_PAD), (POOL_PAD + LAT, 3 * POOL_PAD + LAT), (PL - POOL_PAD, PL)):
                    dve.memset(xpT[:, :, a:b], 0.0)
                dve.wait_ge(S["rstd1"], upto("rstd1", l, 1))
                for i in range(NT):
                    ins = dve.tensor_scalar(xn[:, i, :], X[:, i, :], ST[:, 1, i:i + 1], None, ALU.mult)
                ins.then_inc(S["xn_ready"], 1)
                dve.wait_ge(S["layer_in"], upto("layer_in", l, 16 * 9))

                def ada_columns(c):
                    dve.wait_ge(S["ada_cols"], upto("ada_cols", l, c + 1))
                    dve.tensor_tensor(MOD[:, c // 2, 4 * (c % 2):4 * (c % 2) + 4, :],
                                      PS[:, 2 * pair_of("ada", c) + 1, 0:8].rearrange("p (k t) -> p k t", t=2),
                                      bc(VEC[:, V_BADA + 4 * c:V_BADA + 4 * c + 4], 2, (4, 2)), ALU.add)\
                       .then_inc(free[pair_of("ada", c)], 1)

                def affine(n, sec, add, mul, gain):
                    return dve.scalar_tensor_tensor(AFF[:, n], MOD[:, sec], add if mul is None else mul,
                                                    bc(VEC[:, gain:gain + DK], 2, (DK, 2)),
                                                    ALU.add if mul is None else ALU.mult, ALU.mult)

                def columns_in(c):
                    p, _, n = PAIRS.at["ada", c]
                    dve.wait_ge(free[p], l * PAIRS.free[p] + n + 3)

                for c in range(EARLY):
                    ada_columns(c)
                for c in (2, 3):
                    columns_in(c)
                affine(0, 1, 1.0, None, V_MPRE).then_inc(S["affine_ready"], 1)
                for c in (0, 1):
                    columns_in(c)
                dve.wait_ge(S["affine_ready"], upto("affine_ready", l, 1))
                for k in range(1, DK, 2):
                    dve.wait_ge(*filled_at(l, "hT", k))
                    for s in range(2):
                        ins = dve.tensor_scalar(hT[:, k, stream(s)], pair(pair_of("hT", k))[:, stream(s)],
                                                AFF[:, 0, k, s:s + 1], MOD[:, 0, k, s:s + 1], ALU.mult, ALU.add)
                    ins.then_inc(free[pair_of("hT", k)], 1)
                for i in range(NT):
                    raw, st = qraw[:, i % 2, :], (i % 2) * 2
                    dve.wait_ge(S["qk_raw"], upto("qk_raw", l, i + 1))
                    if i:
                        dve.wait_ge(S["qk_rot"], upto("qk_rot", l, i))
                    link(l, dve.tensor_tensor(qsq, raw, raw, ALU.mult))
                    dve.tensor_reduce(qst[:, st, :], qsq.rearrange("p (h d) -> p h d", d=HD), AX.X, ALU.add)\
                       .then_inc(S["qk_sq"], 1)
                    dve.wait_ge(S["qk_rstd"], upto("qk_rstd", l, i + 1))
                    link(l, dve.tensor_tensor(qa.rearrange("p (h d) -> p h d", d=HD), raw.rearrange("p (h d) -> p h d", d=HD),
                                              bc(qst[:, st + 1, :], 2, (NHEADS, HD)), ALU.mult))
                    if i >= 2:
                        dve.wait_ge(*filled_at(l, "qkT", i - 2))
                    out_q = qrot[:, i % 2, 0:QW].rearrange("p (j s d) -> p s j d", j=4, s=2)
                    out_k = qrot[:, i % 2, QW:640]
                    if i < LT:
                        link(l, dve.tensor_tensor(qb, qa, GAIN, ALU.mult))
                        x5 = qb.rearrange("p (h a f c) -> p h a f c", a=2, f=2, c=16)
                        y5 = qsq.rearrange("p (h a f c) -> p h a f c", a=2, f=2, c=16)
                        r5 = ROPE[:, 1, i, :].rearrange("p (a f c) -> p a f c", a=2, f=2)
                        dve.tensor_tensor(qa.rearrange("p (h d) -> p h d", d=HD), qb.rearrange("p (h d) -> p h d", d=HD),
                                          bc(ROPE[:, 0, i, :], 1, (NHEADS, HD)), ALU.mult)
                        for f in range(2):
                            ins = dve.tensor_tensor(y5[:, :, :, f, :], x5[:, :, :, 1 - f, :],
                                                    bc(r5[:, :, f, :], 1, (NHEADS, 2, 16)), ALU.mult)
                        link(l, ins)
                        a, b, op = qa, qsq, ALU.add
                    else:
                        a, b, op = qa, GAIN, ALU.mult
                    dve.tensor_tensor(out_q, a[:, 0:QW].rearrange("p (s j d) -> p s j d", s=2, j=4),
                                      b[:, 0:QW].rearrange("p (s j d) -> p s j d", s=2, j=4), op)
                    dve.tensor_tensor(out_k, a[:, QW:640], b[:, QW:640], op).then_inc(S["qk_rot"], 1)
                for c in range(2):
                    dve.wait_ge(*drained_at(l, "xp", c))
                    x = xpT[:, c, :]

                    def double(to, of, half, lo, part=slice(0, P)):
                        a, b = lo, PL - lo
                        up = half if half else 0
                        dn = half if half else 1
                        link(l, dve.tensor_tensor(to[part, a:b], of[part, a - dn:b - dn], of[part, a + up:b + up], ALU.add))

                    double(pS[0], x, 0, 1)
                    if c == 0:
                        low, high, half, lo = pS[0], pS[1], 1, 2
                    else:
                        double(pS[1], pS[0], 1, 2)
                        double(pS[2], pS[1], 2, 4)
                        low, high, half, lo = pS[2], pS[0], 4, 8
                    dve.tensor_copy(high[0:HD, POOL_PAD:PL - POOL_PAD], low[0:HD, POOL_PAD:PL - POOL_PAD])
                    double(high, low, half, lo, slice(HD, P))
                    for side, at, step in ((0, POOL_PAD, LAT + 2 * POOL_PAD), (1, LAT, CTX + 2 * POOL_PAD)):
                        e = C_EDGE + (2 * side + c) * 8
                        for n in range(2):
                            v = high[:, at + n * step:at + n * step + 8]
                            ins = dve.tensor_tensor(v, v, CON[:, e:e + 8], ALU.mult)
                    link(l, ins)
                    for s, at in ((0, POOL_PAD), (1, 3 * POOL_PAD + LAT)):
                        n = LAT if s == 0 else CTX
                        ins = dve.scalar_tensor_tensor(pooled[:, c, stream(s)], high[:, at:at + n],
                                                       CON[:, C_WINV + c:C_WINV + c + 1], x[:, at:at + n],
                                                       ALU.mult, ALU.subtract)
                    ins.then_inc(S["pooled"], 1)
                    dve.wait_ge(S["pooled"], upto("pooled", l, c + 1))
                def normalise(h, t):
                    dve.wait_ge(*drained_at(l, "S", (h, t)))
                    link(l, dve.reciprocal(aST[:, 2, t:t + 1], aST[:, 1, t:t + 1]))
                    dve.tensor_scalar(PR[:, t, :], PR[:, t, :], aST[:, 2, t:t + 1], None, ALU.mult)\
                       .then_inc(S["pnorm"], 1)

                for what, x in STEPS:
                    if what == "adacol":
                        ada_columns(x)
                    elif what == "ctxS":
                        dve.wait_ge(*filled_at(l, "ctxS", 0))
                        sc = pair(2).rearrange("p (h t) -> p h t", h=NH)
                        link(l, dve.tensor_reduce(aST[:, 0, :], sc, AX.X, ALU.max))
                        dve.tensor_tensor(cP, sc, bc(aST[:, 0, :], 2, (NH, P)), ALU.subtract).then_inc(free[2], 1)
                        dve.wait_ge(S["cprob"], upto("cprob", l, 1))
                        link(l, dve.tensor_reduce(aST[:, 1, :], cP, AX.X, ALU.add))
                        link(l, dve.reciprocal(aST[:, 2, :], aST[:, 1, :]))
                        dve.tensor_tensor(cP, cP, bc(aST[:, 2, :], 2, (NH, P)), ALU.mult).then_inc(S["cpn"], 1)
                    elif what == "ctxO":
                        dve.wait_ge(*filled_at(l, "ctxO", 0))
                        dve.tensor_copy(OT[:, :, LAT:TOK], bank(4).rearrange("p (j t) -> p j t", j=4)).then_inc(free[2], 1)
                    elif what == "S":
                        h, t = x
                        dve.wait_ge(*filled_at(l, "S", (h, t)))
                        link(l, dve.tensor_reduce(aST[:, 0, t:t + 1], pair(2)[:, 0:KEYS], AX.X, ALU.max))
                        dve.tensor_scalar(aST[:, 0, t:t + 1], aST[:, 0, t:t + 1], -SCALE, None, ALU.mult)\
                           .then_inc(S["smax"], 1)
                        if t:
                            normalise(h, t - 1)
                    elif what == "PV":
                        h = x
                        normalise(h, LT - 1)
                        for kt in range(5):
                            n = 5 * h + kt
                            if n % 2 == 0:
                                dve.wait_ge(S["tr_full"], upto("tr_full", l, n + 1))
                                dve.tensor_copy(PT[:, 0, :], bank((6, 4)[kt % 2])).then_inc(S[f"ptT{n % 2}"], 1)
                        s, j = h // 4, h % 4
                        dve.wait_ge(S["pv_full"], upto("pv_full", l, h + 1))
                        dve.tensor_copy(OT[HD * s:HD * s + HD, j, 0:LAT], PS[HD * s:HD * s + HD, 7, :])\
                           .then_inc(S["o_ready"], 1)
                for c in range(EARLY, 12):
                    columns_in(c)
                affine(1, 2, None, 0.5, V_MPOST)
                affine(2, 4, 1.0, None, V_FPRE)
                affine(3, 5, None, 1.0, V_FPOST).then_inc(S["rows_ready"], 1)
                for d in range(DK):
                    for b, name in enumerate(("mattn", "mpool", "mfour")):
                        dve.wait_ge(*filled_at(l, name, d))
                        p = pair_of(name, d)
                        to = hT[:, d, :] if b == 0 else TG[:, b, d, :]
                        dve.scalar_tensor_tensor(to, TG[:, b, d, :], 1.0, pair(p)[:, 0:TOK], ALU.add, ALU.mult)\
                           .then_inc(free[p], 1)
                        if b:
                            dve.wait_ge(*drained_at(l, name, d))
                            ins = dve.tensor_tensor(hT[:, d, :], hT[:, d, :], TG[:, b, d, :], ALU.add)
                            if b == 1:
                                link(l, ins)
                    ins.then_inc(S["merged"], 1)

                def mixed(i):
                    s = 0 if i < LT else 1
                    dve.wait_ge(*filled_at(l, "mix", i))
                    dve.wait_ge(S["mix_rstd"], upto("mix_rstd", l, i + 1))
                    dve.scalar_tensor_tensor(tmix[:, i % 2, :], pair(i % 2), ST[:, 3, i:i + 1], ROW[:, s, :],
                                             ALU.mult, ALU.mult).then_inc(free[i % 2], 1)
                    dve.wait_ge(*drained_at(l, "mix", i))
                    dve.tensor_tensor(X[:, i, :], X[:, i, :], tmix[:, i % 2, :], ALU.add).then_inc(S["x_mid"], 1)

                def h_rows(i):
                    s = 0 if i < LT else 1
                    dve.wait_ge(S["x2_rstd"], upto("x2_rstd", l, i + 1))
                    if i >= 2:
                        dve.wait_ge(*filled_at(l, "h2T", i - 2))
                        dve.wait_ge(S[f"h_sent{i % 2}"], upto(f"h_sent{i % 2}", l, 16 * (i // 2)))
                    dve.scalar_tensor_tensor(hrow[:, i % 2, :], X[:, i, :], ST[:, 5, i:i + 1], ROW[:, 2 + s, :],
                                             ALU.mult, ALU.mult).then_inc(S["h_a"], 1)

                for v in range(4, 8):
                    dve.wait_ge(*drained_at(l, "bc", v))
                for i in range(NT):
                    mixed(i)
                    h_rows(i)
                L = cut(R, 10240, (NT, NR))
                sc1, mask, m1, m2, oh1, oh2 = rt[2], rt[3], rt[4], rt[5], rt[6], rt[7]
                CUM = cut(R, 10240 + 160 * 8, (NT + 1, NE))
                rev, eid = CON[:, C_REV:C_REV + NE], CON[:, C_EID:C_EID + NE]
                dve.wait_ge(*filled_at(l, "lg", 0))
                dve.tensor_tensor(L, PS[:, 6, 0:NT * NR].rearrange("p (t n) -> p t n", n=NR),
                                  bc(RB[:, :], 1, (NT, NR)), ALU.add).then_inc(free[3], 1)
                dve.wait_ge(*drained_at(l, "lg", 0))

                def first_best(vals, best, n, out, tmp):
                    link(l, dve.tensor_reduce(best, vals, AX.X, ALU.max))
                    link(l, dve.tensor_tensor(tmp, vals, bc(best, 2, (NT, n)), ALU.is_equal))
                    link(l, dve.tensor_tensor(tmp, tmp, bc(rev[:, 0:n], 1, (NT, n)), ALU.mult))
                    link(l, dve.tensor_reduce(RS[:, 7, :], tmp, AX.X, ALU.max))
                    link(l, dve.tensor_tensor(out, tmp, bc(RS[:, 7, :], 2, (NT, n)), ALU.is_equal))

                g_oh, g_tmp = mask[:, :, 0:NG], sc1[:, :, 0:NG]
                first_best(L[:, :, 0:NG], RS[:, 0, :], NG, g_oh, g_tmp)
                dve.tensor_tensor(EX[:, 0, :, 0:NG], L[:, :, 0:NG], bc(RS[:, 0, :], 2, (NT, NG)), ALU.subtract)
                link(l, dve.tensor_scalar(g_tmp, g_oh, 1.0, BIG, ALU.subtract, ALU.mult))
                for i in range(NT):
                    ins = dve.tensor_tensor(m1[:, i, :].rearrange("p (g e) -> p g e", g=NG),
                                            L[:, i, NG:NR].rearrange("p (g e) -> p g e", g=NG),
                                            bc(g_tmp[:, i, :], 2, (NG, EPG)), ALU.add)
                link(l, ins)
                first_best(m1, RS[:, 2, :], NE, oh1, sc1)
                link(l, dve.scalar_tensor_tensor(m2, oh1, -2 * BIG, m1, ALU.mult, ALU.add))
                first_best(m2, RS[:, 3, :], NE, oh2, sc1)
                dve.tensor_tensor(EX[:, 0, :, 4], RS[:, 3, :], RS[:, 2, :], ALU.subtract).then_inc(S["sel_in"], 1)
                dve.memset(CUM[:, 0, :], 0.0)
                link(l, dve.tensor_tensor(mask, oh1, oh2, ALU.add))
                for i in range(NT):
                    ins = dve.tensor_tensor(CUM[:, i + 1, :], CUM[:, i, :], mask[:, i, :], ALU.add)
                    if i < NT - 1:
                        link(l, ins)
                ins.then_inc(S["mask_ready"], 1)
                dve.wait_ge(S["sel_exp"], upto("sel_exp", l, 1))
                link(l, dve.tensor_reduce(RS[:, 1, :], EX[:, 1, :, 0:NG], AX.X, ALU.add))
                link(l, dve.scalar_tensor_tensor(RS[:, 4, :], EX[:, 1, :, 4], 1.0, RS[:, 1, :], ALU.add, ALU.mult))
                link(l, dve.reciprocal(RS[:, 5, :], RS[:, 4, :]))
                link(l, dve.tensor_tensor(RS[:, 6, :], RS[:, 5, :], EX[:, 1, :, 4], ALU.mult))
                dve.wait_ge(*filled_at(l, "pos", 0))
                link(l, dve.tensor_reduce(RS[:, 0, 0:1], PS[:, 1, 0:NE], AX.X, ALU.max))
                dve.tensor_copy(MOST[:, :], RS[:, 0, 0:1])
                dve.scalar_tensor_tensor(m1, PS[:, 0, 0:NT * NE].rearrange("p (t n) -> p t n", n=NE), float(NE),
                                         bc(eid, 1, (NT, NE)), ALU.mult, ALU.add).then_inc(free[0], 1)
                dve.wait_ge(*drained_at(l, "pos", 0))
                for k, oh in enumerate((oh1, oh2)):
                    link(l, dve.tensor_tensor(oh, oh, m1, ALU.mult))
                    link(l, dve.tensor_reduce(RS[:, 2 + k, :], oh, AX.X, ALU.add))
                    ins = dve.tensor_copy(SLOT[:, k, :], RS[:, 2 + k, :])
                ins.then_inc(S["slots_ready"], 1)
                with dve.Fori(0, NE // 2) as it:
                    n = (l * (NE // 2) + it) * 2
                    for e in range(2):
                        dve.wait_ge(gu_full, n + e + 3)
                        dve.wait_ge(gt_full, n + e + 1)
                        dve.tensor_copy(GU[:, e, :], PS[:, 2 + e, 0:FF]).then_inc(gu_out, 1)
                        dve.wait_ge(th_out, n + e + 1)
                        gt = bank(4 + e)[:, 0:256].rearrange("p (c t) -> p c t", c=2)
                        dve.scalar_tensor_tensor(sg, th, 1.0, gt[:, :, 0:BLK], ALU.add, ALU.mult).then_inc(sg_out, 1)
                        dve.wait_ge(sg_out, n + e + 1)
                        dve.wait_ge(dn_full, n + e + 1)
                        dve.tensor_tensor(hE[:, e], sg, gt[:, :, BLK:P], ALU.mult).then_inc(h_out, 1)

                def more_dve(b, e, n):
                    dve.wait_ge(f_gu, n + 1)
                    dve.tensor_copy(GU[:, 0, :], PS[:, 2, 0:FF]).then_inc(f_go, 1)
                    dve.wait_ge(f_th, n + 1)
                    gt = bank(4)[:, 0:256].rearrange("p (c t) -> p c t", c=2)
                    dve.scalar_tensor_tensor(sg, th, 1.0, gt[:, :, 0:BLK], ALU.add, ALU.mult).then_inc(f_sg, 1)
                    dve.wait_ge(f_sg, n + 1)
                    dve.tensor_tensor(hE[:, 0], sg, gt[:, :, BLK:P], ALU.mult).then_inc(f_h, 1)

                further_blocks(dve, l, more_dve, [(f_go, 1), (f_sg, 1), (f_h, 1)])
                for i in range(NT + 1):
                    if i < NT:
                        dve.wait_ge(S["y_scaled"], upto("y_scaled", l, i + 1))
                        y = yg[i]
                        dve.scalar_tensor_tensor(y[:, 0, :], y[:, 1, :], RS[:, 6, i:i + 1], y[:, 0, :], ALU.mult, ALU.add)\
                           .then_inc(S["y_sum"], 1)
                        dve.wait_ge(S["y_sum"], upto("y_sum", l, i + 1))
                    if i:
                        j = i - 1
                        s = 0 if j < LT else 1
                        y = yg[j]
                        dve.wait_ge(S["y_rstd"], upto("y_rstd", l, i))
                        link(l, dve.scalar_tensor_tensor(y[:, 1, :], y[:, 0, :], ST[:, 3, j:j + 1], ROW[:, 6 + s, :],
                                                         ALU.mult, ALU.mult))
                        dve.tensor_tensor(X[:, j, :], X[:, j, :], y[:, 1, :], ALU.add).then_inc(S["x_end"], 1)

        @block.tensor
        def _(pe):
            pe.wait_ge(const_in, 32)
            pe.wait_ge(silu_b, 3)
            mm, tp = nc.tensor.matmul, nc.tensor.transpose

            with pe.Fori(0, DEPTH) as l:

                def slot(name, i, k=DK):
                    s, _ = chunk(name, i)
                    return W[:, s, :].rearrange("p (k n) -> p k n", k=k)

                def both_streams(p, lhsT, rhs, start, stop):
                    mm(pair(p)[:, 0:LAT], lhsT, rhs[:, 0:LAT], start=start, stop=stop)
                    return mm(pair(p)[:, LAT:TOK], lhsT, rhs[:, LAT:TOK], start=start, stop=stop)

                def ada_products(c):
                    p = pair_of("ada", c)
                    pe.wait_ge(*freed_at(l, "ada", c))
                    pe.wait_ge(*loaded_at(l, "ada", c))
                    w = slot("ada", c)
                    for k in range(DK):
                        j = k % 4
                        ins = mm(PS[32 * j:32 * j + 32, 2 * p, :], SILU[:, k, :], w[:, k, :], start=k < 4, stop=k >= 4)
                    ins.then_inc(full[p], 1)

                def ada_cols(c):
                    pe.wait_ge(*drained_at(l, "ada", c))
                    for k in range(4):
                        ins = mm(PS[:, 2 * pair_of("ada", c) + 1, 2 * k:2 * k + 2], part[:, c % 2, P * k:P * k + P],
                                 CON[:, C_SEL:C_SEL + 2], start=True, stop=True)
                    ins.then_inc(S["ada_cols"], 1)

                for c in range(EARLY):
                    ada_products(c)
                    if c:
                        ada_cols(c - 1)
                ada_cols(EARLY - 1)
                pe.wait_ge(S["xn_ready"], upto("xn_ready", l, 1))
                for k in range(DK):
                    p = pair_of("hT", k)
                    pe.wait_ge(*freed_at(l, "hT", k))
                    for i in range(NT):
                        ins = tp(pair(p)[:, P * i:P * i + P], xn[:, i, P * k:P * k + P], ident)
                    ins.then_inc(full[p], 1)
                for k in range(4, DK):
                    pe.wait_ge(*drained_at(l, "hT", k))

                def qkT(i):
                    p = pair_of("qkT", i)
                    pe.wait_ge(*freed_at(l, "qkT", i))
                    if i < NT:
                        pe.wait_ge(S["qk_rot"], upto("qk_rot", l, i + 1))
                        for j in range(5):
                            ins = tp(pair(p)[:, P * j:P * j + P], qrot[:, i % 2, P * j:P * j + P], ident)
                    else:
                        pe.wait_ge(S["layer_in"], upto("layer_in", l, per["layer_in"]))
                        ins = tp(PS[:, 2 * p + 1, 0:P], kc, ident)
                    ins.then_inc(full[p], 1)

                for i in range(NT):
                    p = pair_of("qkv", i)
                    pe.wait_ge(*freed_at(l, "qkv", i))
                    for n, name in enumerate(("q", "kvx")):
                        pe.wait_ge(*loaded_at(l, name))
                        for k in range(DK):
                            ins = mm(bank(2 * p + n), hT[:, k, P * i:P * i + P], slot(name, 0)[:, k, :],
                                     start=k == 0, stop=k == DK - 1)
                    ins.then_inc(full[p], 1)
                    if i:
                        qkT(i - 1)
                for c in range(2):
                    pe.wait_ge(*freed_at(l, "xp", c))
                    pe.wait_ge(*loaded_at(l, "xp"))
                    w = W[:, chunk("xp")[0], 0:2048].rearrange("p (k n) -> p k n", k=DK)
                    for k in range(DK):
                        ins = both_streams(c, w[:, k, P * c:P * c + P], hT[:, k, :], k == 0, k == DK - 1)
                    ins.then_inc(full[c], 1)
                    if c == 0:
                        qkT(NT - 1)
                        qkT(NT)
                pe.wait_ge(*drained_at(l, "qkv", NT - 1))
                pe.wait_ge(*drained_at(l, "qkv", NT - 2))
                for j in range(4):
                    c, f = j % 2, j // 2
                    p = pair_of("dft", j)
                    pe.wait_ge(*freed_at(l, "dft", j))
                    name = ("cos", "sin")[f]
                    pe.wait_ge(*loaded_at(l, name))
                    w = W[:, chunk(name)[0], 0:2048].rearrange("p (k n) -> p k n", k=LT)
                    for k in range(LT):
                        ins = mm(bank(2 * p), XF[:, k, P * c:P * c + P], w[:, k, :], start=k == 0, stop=k == LT - 1)
                    mm(PS[:, 2 * p + 1, 0:P], XF[:, LT, P * c:P * c + P], cols(C_XC if f == 0 else C_XS),
                       start=True, stop=True).then_inc(full[p], 1)
                for c in range(2):
                    p = pair_of("plin", c)
                    pe.wait_ge(*freed_at(l, "plin", c))
                    pe.wait_ge(S["pooled"], upto("pooled", l, c + 1))
                    both_streams(p, WPG[:, c, :], pooled[:, c, :], True, True).then_inc(full[p], 1)
                for c in range(2):
                    p = pair_of("four", c)
                    pe.wait_ge(*freed_at(l, "four", c))
                    pe.wait_ge(*drained_at(l, "dft", c))
                    both_streams(p, cols(C_CC), AB[:, c, :], True, False)
                    pe.wait_ge(*drained_at(l, "dft", 2 + c))
                    both_streams(p, cols(C_CS), AB[:, 2 + c, :], False, True).then_inc(full[p], 1)

                pe.wait_ge(*drained_at(l, "qkT", NT - 1))
                pe.wait_ge(*drained_at(l, "qkT", NT))
                for what, x in STEPS:
                    if what == "ada":
                        ada_products(x)
                    elif what == "adacol":
                        ada_cols(x)
                    elif what == "gates":
                        g, half = x
                        p = pair_of("gate", g)
                        if half == 0:
                            pe.wait_ge(*freed_at(l, "gate", g))
                            pe.wait_ge(*loaded_at(l, "gate", g // 4))
                        w = slot("gate", g // 4)
                        for k in range(4 * half, 4 * half + 4):
                            ins = both_streams(p, w[:, k, P * (g % 4):P * (g % 4) + P], hT[:, k, :], k == 0, k == DK - 1)
                        if half:
                            ins.then_inc(full[p], 1)
                    elif what == "ctxS":
                        pe.wait_ge(*freed_at(l, "ctxS", 0))
                        for h in range(NH):
                            ins = mm(pair(2)[:, P * h:P * h + P], qT[:, h % 4, LAT:TOK], kT[:, h // 4, KEYS:KALL],
                                     start=True, stop=True)
                        ins.then_inc(full[2], 1)
                    elif what == "ctxT":
                        pe.wait_ge(*freed_at(l, "ctxT", 0))
                        pe.wait_ge(S["cpn"], upto("cpn", l, 1))
                        for h in range(NH):
                            ins = tp(pair(3)[:, P * h:P * h + P], cP[:, h, :], ident)
                        ins.then_inc(full[3], 1)
                    elif what == "ctxO":
                        pe.wait_ge(*freed_at(l, "ctxO", 0))
                        pe.wait_ge(*drained_at(l, "ctxT", 0))
                        for h in range(NH):
                            s, j = h // 4, h % 4
                            ins = mm(PS[HD * s:HD * s + HD, 4, P * j:P * j + P], V[:, NT, HD * s:HD * s + HD], cPT[:, h, :],
                                     start=True, stop=True)
                        ins.then_inc(full[2], 1)
                    elif what == "S":
                        h, t = x
                        pe.wait_ge(*freed_at(l, "S", x))
                        q = qT[:, h % 4, P * t:P * t + P]
                        mm(bank(4), q, kT[:, h // 4, 0:512], start=True, stop=True)
                        mm(PS[:, 5, 0:P], q, kT[:, h // 4, 512:KEYS], start=True, stop=True).then_inc(full[2], 1)
                    elif what == "PV":
                        s, j = x // 4, x % 4
                        pe.wait_ge(S["pnorm"], upto("pnorm", l, LT * (x + 1)))

                        def transposed(kt):
                            for t in range(LT):
                                ins = tp(bank((6, 4)[kt % 2])[:, P * t:P * t + P], PR[:, t, P * kt:P * kt + P], ident)
                            ins.then_inc(S["tr_full"], 1)

                        transposed(0)
                        if x:
                            pe.wait_ge(S["o_ready"], upto("o_ready", l, x))
                        for kt in range(5):
                            n = 5 * x + kt
                            if kt < 4:
                                transposed(kt + 1)
                            pe.wait_ge(S[f"ptT{n % 2}"], upto(f"ptT{n % 2}", l, n // 2 + 1))
                            ins = mm(PS[HD * s:HD * s + HD, 7, :], V[:, kt, HD * s:HD * s + HD], PT[:, n % 2, :],
                                     start=kt == 0, stop=kt == 4)
                        ins.then_inc(S["pv_full"], 1)
                pe.wait_ge(S["o_ready"], upto("o_ready", l, NH))
                pe.wait_ge(*drained_at(l, "plin", 1))
                pe.wait_ge(*drained_at(l, "four", 1))
                for d in range(DK):
                    at = slice(P * d, P * d + P)
                    pf = W[:, chunk("pf")[0], :].rearrange("p (w k n) -> p w k n", w=2, k=2)
                    for name, src, n in (("mattn", OT, 4), ("mpool", PM, 2), ("mfour", FM, 2)):
                        p = pair_of(name, d)
                        pe.wait_ge(*freed_at(l, name, d))
                        pe.wait_ge(*loaded_at(l, "ao" if n == 4 else "pf"))
                        w = slot("ao", 0, 4) if n == 4 else pf[:, 0 if name == "mpool" else 1]
                        for k in range(n):
                            ins = both_streams(p, w[:, k, at], src[:, k, :], k == 0, k == n - 1)
                        ins.then_inc(full[p], 1)
                pe.wait_ge(S["rows_ready"], upto("rows_ready", l, 1))
                for v in range(8):
                    p, s = v % 4, v % 2
                    pe.wait_ge(*freed_at(l, "bc", v))
                    vec = (AFF[:, 1], AFF[:, 2], MOD[:, 3], AFF[:, 3])[v // 2]
                    for k in range(DK):
                        ins = mm(pair(p)[:, P * k:P * k + P], vec[:, k, s:s + 1].broadcast_to([P, P]), ident,
                                 start=True, stop=True)
                    ins.then_inc(full[p], 1)

                def h2T(i):
                    p = pair_of("h2T", i)
                    pe.wait_ge(*freed_at(l, "h2T", i))
                    pe.wait_ge(S["h_b"], upto("h_b", l, i + 1))
                    for k in range(DK):
                        ins = tp(pair(p)[:, P * k:P * k + P], hrow[:, i % 2, P * k:P * k + P], ident)
                    ins.then_inc(full[p], 1)

                def logits(i):
                    if i == 0:
                        pe.wait_ge(*freed_at(l, "lg", 0))
                        pe.wait_ge(S["wr_in"], upto("wr_in", l, 16))
                    pe.wait_ge(*drained_at(l, "h2T", i))
                    for k in range(DK):
                        ins = mm(PS[:, 6, NR * i:NR * i + NR], hT[:, k, P * i:P * i + P], WR[:, k, :],
                                 start=k == 0, stop=k == DK - 1)
                    return ins

                pe.wait_ge(S["merged"], upto("merged", l, DK))
                for i in range(NT):
                    p = i % 2
                    pe.wait_ge(*freed_at(l, "mix", i))
                    for n in range(2):
                        pe.wait_ge(*loaded_at(l, "wo", n))
                        for k in range(DK):
                            ins = mm(bank(2 * p + n), hT[:, k, P * i:P * i + P], slot("wo", n)[:, k, :],
                                     start=k == 0, stop=k == DK - 1)
                    ins.then_inc(full[p], 1)
                    if i:
                        h2T(i - 1)
                    if i >= 2:
                        logits(i - 2)
                logits(NT - 2)
                h2T(NT - 1)
                logits(NT - 1).then_inc(full[3], 1)
                pe.wait_ge(*freed_at(l, "pos", 0))
                pe.wait_ge(S["mask_ready"], upto("mask_ready", l, 1))
                flat = slice(0, NT * NE)
                cum = cut(R, 10240 + 160 * 8, (NT * NE + NE,))
                mm(PS[:, 0, flat], tri, rt[3].rearrange("p t n -> p (t n)"), start=True, stop=False)
                mm(PS[:, 0, flat], ones, cum[:, flat], start=False, stop=True)
                mm(PS[:, 1, 0:NE], ones, cum[:, NT * NE:], start=True, stop=True).then_inc(full[0], 1)

                def transpose_rows(e):
                    rows = xg[0:BLK, e, :].rearrange("p (f k) -> p k f", k=DK)
                    for k in range(DK):
                        ins = tp(bank(e)[:, BLK * k:BLK * k + BLK], rows[:, k, :], ident[0:BLK, 0:BLK])
                    return ins

                def gate_up_products(e):
                    for k in range(DK):
                        for u in range(2):
                            ins = mm(PS[BLK * u:BLK * u + BLK, 2 + e, 0:FF], xT[:, e, k, :], wgu[e][:, u, k, :],
                                     start=k == 0, stop=k == DK - 1)
                    return ins

                def transpose_gate_up(e):
                    v = GU[:, e, :].rearrange("p (f c) -> p c f", c=2)
                    for c in range(2):
                        ins = tp(bank(4 + e)[:, P * c:P * c + P], v[:, c, :], ident)
                    return ins

                def down_products(e):
                    for c in range(2):
                        for h in range(2):
                            ins = mm(PS[BLK * h:BLK * h + BLK, 6 + e, :], hE[:, e, c, :],
                                     wdn[e][:, c, 512 * h:512 * h + 512], start=c == 0, stop=c == 1)
                    return ins

                for p in range(4):
                    pe.wait_ge(free[p], (l + 1) * PAIRS.free[p] + 1)
                pe.sem_inc(aside, 1)
                with pe.Fori(0, NE // 2) as it:
                    q = l * (NE // 2) + it
                    n = q * 2

                    def rows_T(e):
                        pe.wait_ge(rows_in[e], (q + l) * 16 + 16)
                        pe.wait_ge(xT_out, n + e + 1)
                        pe.sem_inc(aside, 1)
                        transpose_rows(e).then_inc(xT_full, 1)

                    def gate_up(e):
                        pe.wait_ge(xT_out, n + e + 3)
                        pe.wait_ge(ex_loaded[e], q * 32 + 32)
                        pe.wait_ge(gu_out, n + e + 1)
                        gate_up_products(e).then_inc(gu_full, 1)

                    def gu_T(e):
                        pe.wait_ge(gu_out, n + e + 3)
                        pe.wait_ge(h_out, n + e + 1)
                        transpose_gate_up(e).then_inc(gt_full, 1)

                    def down(e):
                        pe.wait_ge(h_out, n + e + 3)
                        pe.wait_ge(dn_loaded[e], q * 16 + 16)
                        pe.wait_ge(y_out, n + e + 1)
                        down_products(e).then_inc(dn_full, 1)

                    rows_T(0)
                    gate_up(0)
                    rows_T(1)
                    gu_T(0)
                    gate_up(1)
                    down(0)
                    gu_T(1)
                    down(1)
                for s in (xT_out, gu_out, h_out, y_out):
                    pe.wait_ge(s, (l + 1) * NE + 2)

                def more_pe(b, e, n):
                    pe.wait_ge(f_rows, n + 1)
                    pe.sem_inc(aside, 1)
                    transpose_rows(0).then_inc(f_xT, 1)
                    pe.wait_ge(f_xo, n + 1)
                    pe.wait_ge(f_loaded, 48 * n + 48)
                    gate_up_products(0).then_inc(f_gu, 1)
                    pe.wait_ge(f_go, n + 1)
                    transpose_gate_up(0).then_inc(f_gt, 1)
                    pe.wait_ge(f_h, n + 1)
                    down_products(0).then_inc(f_dn, 1)

                further_blocks(pe, l, more_pe, [(f_xT, 1), (f_gu, 1), (f_gt, 1), (f_dn, 1)])
                pe.wait_ge(f_y, (l + 1) * XBLK * NE)

        for name, n in count.items():
            assert n == per[name], (name, n)


STEPS_PER_LAYER = dict(dve_step=138, act_step=1, pool_step=21)


def host_constants(np):
    con = np.zeros((P, NCONST), np.float64)
    con[:, C_ID:C_ID + P] = np.eye(P)
    con[:, C_ONE:C_ONE + P] = 1
    con[:, C_TRI:C_TRI + P] = np.triu(np.ones((P, P)), 1)

    def dft(n):
        a = 2 * np.pi * (np.outer(np.arange(n), np.arange(n)) % n) / n
        return np.cos(a) / np.sqrt(n), np.sin(a) / np.sqrt(n)

    cc, cs = dft(HD)
    for h in range(2):
        at = slice(HD * h, HD * h + HD)
        con[at, C_CC + HD * h:C_CC + HD * h + HD] = cc
        con[at, C_CS + HD * h:C_CS + HD * h + HD] = -cs
    con[:, C_XC:C_XC + P], con[:, C_XS:C_XS + P] = dft(CTX)
    for c in range(2):
        for h in range(2):
            w = (2, 4, 8, 16)[2 * c + h]
            at = slice(HD * h, HD * h + HD)
            con[at, C_WINV + c] = 1 / w
            t = np.arange(8)
            con[at, C_EDGE + c * 8:C_EDGE + c * 8 + 8] = w / np.minimum(w, t + w // 2)
            con[at, C_EDGE + (2 + c) * 8:C_EDGE + (2 + c) * 8 + 8] = w / np.minimum(w, 8 - t + w // 2)
    con[:, C_EID:C_EID + NE] = np.arange(NE)
    con[BLK:, C_HALF] = 1
    con[:, C_REV:C_REV + NE] = NE - np.arange(NE)
    for j in range(4):
        for s in range(2):
            con[32 * j + s, C_SEL + s] = 1
    f = np.float32
    t = np.arange(LAT)
    inv = (f(10000.0) ** (-np.arange(16, dtype=f) * f(2.0) / f(32))).astype(f)
    rope = np.zeros((P, 2, LT, HD), f)
    for a, pos in enumerate((t // 64, t % 64)):
        ang = (pos.astype(f)[:, None] * inv).astype(f)
        c, s = (np.cos(ang.astype(np.float64)).reshape(LT, P, 16).transpose(1, 0, 2),
                np.sin(ang.astype(np.float64)).reshape(LT, P, 16).transpose(1, 0, 2))
        for h in range(2):
            rope[:, 0, :, 32 * a + 16 * h:32 * a + 16 * h + 16] = c
            rope[:, 1, :, 32 * a + 16 * h:32 * a + 16 * h + 16] = s if h else -s
    return {
        "consts": con.astype(f), "rope": rope.reshape(P, -1), "dft": np.stack(dft(LAT)).astype(f),
        "token_ids": np.arange(2 * TOK, dtype=np.int32).reshape(2, NT, P).transpose(2, 0, 1).copy(),
        "table_init": np.full((P, TOK * NE // P), 2 * TOK, np.int32),
    }


def kernel(**inputs):
    import numpy as np
    import concourse.bacc as _bacc
    from concourse.bass_utils import run_bass_kernel_spmd as _run

    x = {k: np.asarray(v) for k, v in inputs.items()}

    def columns(v):
        return v.reshape(DEPTH, -1, P).transpose(0, 2, 1)

    arrays = host_constants(np)
    for k in ("x_prompt", "x_sample", "cache_k", "cache_v", "w_ada", "w_in", "w_attn_out", "w_pool_group",
              "w_pool_out", "w_fourier_out", "w_out", "w_expert_gate", "w_expert_up", "w_expert_down"):
        arrays[k] = np.ascontiguousarray(x[k])
    arrays["vecs"] = np.ascontiguousarray(np.concatenate([columns(x[k]) for k in (
        "b_ada", "norm_mix_pre", "norm_mix_post", "norm_ffn_pre", "norm_ffn_post", "pool_scale")], axis=2))
    arrays["c_cols"] = np.ascontiguousarray(np.stack([x["c"][0].reshape(DK, P).T, x["c_ctx"].reshape(DK, P).T], axis=2))
    arrays["gains"] = np.ascontiguousarray(np.broadcast_to(np.concatenate(
        [x["q_norm"]] * NH + [x["k_norm"]] * NKV, axis=1)[:, None, :], (DEPTH, P, NHEADS * HD)))
    arrays["router_b"] = np.ascontiguousarray(np.broadcast_to(np.concatenate(
        [x["b_router_group"], x["b_router_expert"]], axis=1)[:, None, :], (DEPTH, P, NR)))
    arrays["w_router"] = np.ascontiguousarray(np.concatenate([x["w_router_group"], x["w_router_expert"]], axis=2))

    nc = _bacc.Bacc("TRN2", target_bir_lowering=False, num_devices=1)
    A = {}
    for k, v in arrays.items():
        A[k] = nc.dram_tensor("in_" + k, v.shape, mybir.dt.from_np(v.dtype), kind="ExternalInput").ap()
    outs = [("out_p", (1, CTX, D)), ("out_s", (1, LAT, D)), ("out_k", (1, DEPTH, CTX, NKV, HD)),
            ("out_v", (1, DEPTH, CTX, NKV, HD))]
    for k, shape in outs:
        A[k] = nc.dram_tensor(k, shape, F32, kind="ExternalOutput").ap()
    A["h_rows"] = nc.dram_tensor("h_rows", (TOK, D), F32, kind="Internal").ap()
    A["y_half_rows"] = nc.dram_tensor("y_half_rows", (4 * TOK, D // 2), F32, kind="Internal").ap()
    A["table"] = nc.dram_tensor("table", (TOK * NE, 1), I32, kind="Internal").ap()
    trunk_kernel(nc, A, STEPS_PER_LAYER)
    r = _run(nc, [{"in_" + k: v for k, v in arrays.items()}], core_ids=[0])
    return tuple(r.results[0][k] for k, _ in outs)
```

```python
import concourse.bass as bass
from concourse import mybir
from contextlib import ExitStack

F32 = mybir.dt.float32
I32 = mybir.dt.int32
ALU = mybir.AluOpType
ACT = mybir.ActivationFunctionType
AX = mybir.AxisListType

P = 128
D = 1024
DK = D // P
DEPTH = 2
CTX, LAT = 128, 512
TOK = CTX + LAT
NT = TOK // P
LT = LAT // P
NH, NKV, HD = 8, 2, 64
QW, KW = NH * HD, NKV * HD
NHEADS = NH + NKV
FOURW = 256
KEYS = P + LAT
KALL = KEYS + CTX
SCALE = float(HD) ** -0.5
NG, EPG = 4, 8
NE = NG * EPG
NR = NG + NE
FF = 256
BLK = 64
ESLOTS = 4
XBLK = TOK // BLK - 1
EPS = 1e-6
BIG = 1e30
POOL_PAD = 8

C_ID, C_ONE, C_TRI, C_CC, C_CS, C_XC, C_XS = (i * P for i in range(7))
C_EDGE = 7 * P
C_WINV = C_EDGE + 32
C_EID = C_WINV + 2
C_REV = C_EID + NE
C_SEL = C_REV + NE
C_HALF = C_SEL + 2
NCONST = C_HALF + 1
V_BADA, V_MPRE, V_MPOST, V_FPRE, V_FPOST, V_PS = 0, 48, 56, 64, 72, 80
NVEC = 82

CHUNKS = ([("ada", 0, 1, 0), ("ada", 1, 1, 1), ("ada", 2, 1, 2), ("ada", 3, 1, 0), ("q", 0, 1, 1), ("kvx", 0, 2, 2),
           ("xp", 0, 1, 0), ("cos", 0, 1, 1), ("sin", 0, 1, 2), ("gate", 0, 1, 1), ("ada", 4, 1, 0), ("gate", 1, 1, 2)] +
          [("ada", 5, 1, 0), ("ada", 6, 1, 0), ("gate", 2, 1, 1), ("ada", 7, 1, 0), ("ada", 8, 1, 0), ("gate", 3, 1, 2),
           ("ada", 9, 1, 0), ("ada", 10, 1, 0), ("gate", 4, 1, 1), ("ada", 11, 1, 0), ("gate", 5, 1, 2)] +
          [("ao", 0, 2, 0), ("pf", 0, 2, 1), ("wo", 0, 1, 2), ("wo", 1, 1, 0)])
WSLOTS = 3
CHUNK_AT = {(name, i): c for c, (name, i, _, _) in enumerate(CHUNKS)}
EARLY = 4

USES = [("ada", c, c % 4, 2) for c in range(EARLY)]
USES += [("hT", k, k % 4, 1) for k in range(DK)]
for _i in range(NT):
    USES.append(("qkv", _i, _i % 2, 1))
    if _i:
        USES.append(("qkT", _i - 1, 2 + (_i - 1) % 2, 1))
USES.append(("qkT", NT - 1, 2, 1))
USES.append(("qkT", NT, 3, 1))
USES += [("xp", c, c, 1) for c in range(2)]
USES += [("dft", j, (2 + j) % 4, 1) for j in range(4)]
USES += [("plin", c, 2 + c, 1) for c in range(2)]
USES += [("four", c, c, 1) for c in range(2)]
NGATE = 3 * DK
PARTS = 4


def attention_steps():
    after_gate = {2: 5, 4: 6, 6: 7, 8: 8, 10: 9, 12: 10, 14: 11}
    parts = iter([(x, part) for x in range(NGATE) for part in range(PARTS)])
    steps, due = [("ada", 4), ("ctxS", 0)], {}

    def gates(n):
        for _ in range(n):
            x = next(parts, None)
            if x is not None:
                add("gates", x)
                if x[1] == PARTS - 1 and x[0] in after_gate:
                    add("ada", after_gate[x[0]])
                    due[len(steps) + 2] = after_gate[x[0]]

    def add(name, x):
        if len(steps) in due:
            steps.append(("adacol", due[len(steps)]))
        steps.append((name, x))

    gates(PARTS)
    add("adacol", 4)
    add("ctxT", 0)
    gates(PARTS)
    add("ctxO", 0)
    for h in range(NH):
        for t in range(LT):
            add("S", (h, t))
            gates(2)
        add("T", (h, 0))
        for kt in range(KEYS // P):
            if kt + 1 < KEYS // P:
                add("T", (h, kt + 1))
            if kt % 2 == 0:
                gates(1)
            add("O", (h, kt))
    assert next(parts, None) is None
    return steps


STEPS = attention_steps()
_turn = 0
for _n, _x in STEPS:
    if _n == "ada":
        USES.append(("ada", _x, _turn, 2))
        _turn = 1 - _turn
    elif _n == "gates" and _x[1] == 0:
        USES.append(("gate", _x[0], _turn, 1))
        _turn = 1 - _turn
    elif _n == "S":
        USES.append(("S", _x, 2, 1))
    elif _n == "ctxS":
        USES.append(("ctxS", 0, 2, 1))
    elif _n == "ctxT":
        USES.append(("ctxT", 0, 3, 1))
    elif _n == "ctxO":
        USES.append(("ctxO", 0, 2, 1))
USES.append(("vecT", 0, 0, 1))
for _d in range(DK):
    USES += [(b, _d, (3 * _d + j) % 4, 1) for j, b in enumerate(("mattn", "mpool", "mfour"))]
USES += [("mix", i, i % 2, 1) for i in range(NT)]
USES += [("h2T", i, 2, 1) for i in range(NT)]
USES += [("lg", 0, 3, 1), ("pos", 0, 0, 1), ("ids", 0, 1, 1)]


class Pairs:

    def __init__(self):
        self.at, self.full, self.free = {}, [0] * 4, [0] * 4
        for name, i, p, drains in USES:
            self.at[name, i] = (p, self.full[p], self.free[p])
            self.full[p] += 1
            self.free[p] += drains


PAIRS = Pairs()

PER = dict(
    dve_step=0, act_step=0, pool_step=0, ada_cols=12, affine_ready=1, vecs_ready=1, rows_in_dram=16, rows_ready=16, x_sumsq=NT, x_ms=NT,
    rstd1=NT, xn_ready=NT, qk_raw=NT, qk_sq=NT, qk_rstd=NT, qk_rot=NT, pooled=2, cprob=1, cpn=1,
    smax=LT * NH, pnorm=LT * NH, tr_full=5 * NH, ptT0=5 * NH // 2, ptT1=5 * NH // 2, pv_full=NH, o_ready=NH, merged=DK,
    mix_sq=NT, mix_rstd=NT, x_mid=NT, x2_sq=NT, x2_rstd=NT, h_scaled=NT, h_ready=NT, h_sent0=48, h_sent1=32, wr_in=16,
    sel_in=1, sel_exp=1, mask_ready=1, slots_ready=1, table_clear=16, onehots=1, ids_ready=1, no_rows=1,
    y_scaled=NT, y_sum=NT, y_sq=NT, y_rstd=NT, x_end=NT, vec_in=16, layer_in=144, kv_out=32,
    xg_zero=1,
)


def trunk_kernel(nc, A, CH):
    ctx = ExitStack()
    with ctx:
        def sb(name, shape, dt=F32):
            return ctx.enter_context(nc.sbuf_tensor(name, shape, dt))

        def sem(name):
            return ctx.enter_context(nc.semaphore(name))

        X = sb("x_rows", [P, NT, D])
        HT = sb("h_T", [P, DK * TOK])
        G = sb("gates_mem", [P, NGATE * TOK])
        W = sb("w_ring", [P, WSLOTS, 4096])
        R = sb("attn_mem", [P, 13568])
        CON = sb("consts", [P, NCONST])
        VEC = sb("vectors", [P, NVEC])
        SILU = sb("silu_c", [P, DK, 32])
        MOD = sb("mod", [P, 6, DK, 2])
        AFF = sb("affine", [P, 4, DK, 2])
        ST = sb("stats", [P, 6, NT])

        hT = HT[:, :].rearrange("p (k t) -> p k t", k=DK)

        def cut(t, at, shape):
            n = 1
            for s in shape:
                n *= s
            v = t[:, at:at + n]
            if len(shape) == 1:
                return v
            names = "abcd"[:len(shape)]
            spec = " ".join(names)
            return v.rearrange(f"p ({spec}) -> p {spec}", **{c: s for c, s in zip(names[1:], shape[1:])})

        xn = cut(G, 0, (NT, D))
        AB = cut(G, 0, (4, TOK))
        PL = LAT + CTX + 4 * POOL_PAD
        pS = [cut(G, 4 * TOK + i * PL, (PL,)) for i in range(3)]
        XF = cut(G, 5120, (NT, FOURW))
        xpT = cut(G, 6400, (2, PL))
        qraw = cut(G, 7744, (2, 640))
        qsq = cut(G, 9024, (640,))
        qa = cut(G, 9664, (640,))
        qb = cut(G, 10304, (640,))
        qrot = cut(G, 10944, (2, 640))
        ROPE = cut(G, 12224, (2, LT, HD))
        GAIN = cut(G, 12736, (640,))
        pooled = cut(G, 9664, (2, TOK))
        qst = cut(G, 13376, (4, NHEADS))
        kc = cut(G, 13416, (KW,))
        WPG = cut(G, 13544, (2, P))
        TG = cut(G, 0, (3, DK, TOK))
        w_flat = W[:, :, :].rearrange("p s n -> p (s n)")
        EW = [cut(G, e * 6144, (6144,)) for e in range(2)] + [w_flat[:, e * 6144:e * 6144 + 6144] for e in range(2)]
        EW = [(w[:, 0:4096], w[:, 4096:6144]) for w in EW]
        EW += [(cut(R, 0, (4096,)), cut(R, 4096, (2048,))), (cut(R, 8192, (4096,)), cut(G, 13312, (2048,)))]
        wgu = [w.rearrange("p (u k f) -> p u k f", u=2, k=DK) for w, _ in EW]
        wdn = [w.rearrange("p (c n) -> p c n", c=2) for _, w in EW]
        qT = cut(R, 0, (4, TOK))
        kT = cut(R, 2560, (2, KALL))
        V = cut(R, 4096, (NT + 1, KW))
        PR = cut(R, 4864, (LT, KEYS))
        PT = cut(R, 7424, (2, 512))
        OT = cut(R, 8448, (4, TOK))
        PM = cut(R, 11008, (2, TOK))
        FM = cut(R, 12288, (2, TOK))
        part = cut(G, 14080, (2, 512))
        part = [part[:, 0], part[:, 1], cut(HT, 0, (512,)), cut(HT, 512, (512,))]
        cP = cut(R, 4864, (NH, P))
        cPT = cut(R, 7424, (NH, P))
        aST = sb("attn_stats", [P, 3, 8])
        ROW = cut(R, 0, (8, D))
        VCOL = cut(R, 4864, (4, 2, DK))
        VROW = cut(R, 5120, (P,))
        hrow = cut(R, 8192, (2, D))
        tmix = cut(R, 10240, (2, D))
        rt = [cut(R, 10240 + 160 * i, (NT, NE)) for i in range(10)]
        WR = cut(G, 12288, (DK, NR))
        junk = cut(R, 12288, (D,))
        yg = [cut(R, 2 * D * i if i < 3 else 8192 + 2 * D * (i - 3), (2, D)) for i in range(NT)]
        xg = cut(HT, 0, (2, D))
        xT = cut(HT, 2048, (2, DK, BLK))
        GU = cut(HT, 3072, (2, FF))
        th = cut(HT, 3584, (2, BLK))
        hE = cut(HT, 3712, (2, 2, BLK))
        yb = cut(HT, 3968, (2, 512))
        RS = sb("router_small", [P, 8, NT])
        SLOT = sb("slots", [P, 2, NT], I32)
        TID = sb("assignment_ids", [P, 2, NT], I32)
        IDX = cut(G, 13000, (3, NE + 2)).bitcast(I32)
        RB = sb("router_bias", [P, NR])
        MOST = sb("largest_count", [P, 1], I32)
        HALF = sb("minus_half", [P, NHEADS])
        IDC = sb("row_ids_now", [P, 4], I32)
        EX = cut(R, 11840, (2, NT, 5))
        OHP = cut(R, 11904, (2, NT, BLK))
        OHE = cut(R, 11904 + 2 * NT * BLK, (2, NT, NE))
        AIDS = cut(R, 11904 + 2 * NT * (BLK + NE), (3, NE))
        IOTA = cut(R, 13312, (BLK,))
        ID1 = cut(R, 13312 + BLK, (2, NT))
        sg = cut(HT, 4992, (2, BLK))

        PS = ctx.enter_context(nc.psum_tensor("ps", [P, 8, 512], F32))

        def bank(b):
            return PS[:, b, :]

        def pair(p):
            return PS[:, 2 * p:2 * p + 2, :].rearrange("p b n -> p (b n)")

        S = {name: sem(name) for name in PER}
        per = dict(PER)
        per.update(CH)
        full = [sem(f"psum_full{p}") for p in range(4)]
        free = [sem(f"psum_free{p}") for p in range(4)]
        loaded = [sem(f"chunk_loaded{s}") for s in range(WSLOTS)]
        const_in, x_in = sem("const_in"), sem("x_in")
        aside = sem("aside")
        f_turn = sem("more_turns")
        silu_a, silu_b = sem("silu_tanh"), sem("silu_ready")
        setup, table_set = sem("setup_done"), sem("table_set")
        done = sem("outputs_stored")
        ex_loaded = [sem(f"expert_loaded{e}") for e in range(ESLOTS + 2)]
        dn_loaded = [sem(f"expert_down_loaded{e}") for e in range(ESLOTS + 2)]
        rows_in = [sem(f"expert_rows{e}") for e in range(2)]
        idc = [sem(f"gather_ids_copied{e}") for e in range(2)]
        idy = [sem(f"scatter_ids_copied{e}") for e in range(2)]
        yg_in = [sem(f"y_gathered{i}") for i in range(NT)]
        xT_full, xT_out = sem("ex_xT_full"), sem("ex_xT_out")
        gu_full, gu_out, gt_full = sem("ex_gu_full"), sem("ex_gu_out"), sem("ex_gt_full")
        th_out, sg_out, h_out = sem("ex_tanh"), sem("ex_silu"), sem("ex_h")
        dn_full, y_out = sem("ex_down_full"), sem("ex_y_out")
        y_sent = [sem(f"ex_y_sent{e}") for e in range(2)]
        f_ids, f_step, f_gathered, f_sent = sem("more_ids"), sem("more_ids_step"), sem("more_gathered"), sem("more_sent")
        f_rows, f_loaded, f_done = sem("more_rows_in"), sem("more_weights_in"), sem("more_block_done")
        f_xT, f_xo, f_gu, f_go, f_gt = sem("more_xT"), sem("more_xT_out"), sem("more_gu"), sem("more_gu_out"), sem("more_gt")
        f_th, f_sg, f_h, f_dn, f_y = sem("more_tanh"), sem("more_silu"), sem("more_h"), sem("more_down"), sem("more_y_out")
        count = {"dve_step": 0, "act_step": 0, "pool_step": 0}

        def upto(name, l, n):
            return l * per[name] + n

        chunk_dmas = [[0] for _ in range(WSLOTS)]
        nth_of_slot, last_of_slot = [], []
        for c, (_, _, n, s) in enumerate(CHUNKS):
            before = [b for b in range(c) if CHUNKS[b][3] == s]
            nth_of_slot.append(len(before))
            last_of_slot.append(before[-1] if before else None)
            chunk_dmas[s].append(chunk_dmas[s][-1] + 16 * n)

        def chunk(name, i=0):
            c = CHUNK_AT[name, i]
            s = CHUNKS[c][3]
            return s, chunk_dmas[s][nth_of_slot[c] + 1]

        def loaded_at(l, name, i=0):
            s, n = chunk(name, i)
            return loaded[s], l * chunk_dmas[s][-1] + n

        def used_at(l, c):
            name, i, _, _ = CHUNKS[c]
            return filled_at(l, *{"ada": ("ada", i), "q": ("qkv", NT - 1), "kvx": ("qkv", NT - 1), "xp": ("xp", 1),
                                  "cos": ("dft", 1), "sin": ("dft", 3), "gate": ("gate", 4 * i + 3),
                                  "ao": ("mattn", DK - 1), "pf": ("mfour", DK - 1), "wo": ("mix", NT - 1)}[name])

        def freed_at(l, name, i):
            p, _, n = PAIRS.at[name, i]
            return free[p], l * PAIRS.free[p] + n + 1

        def filled_at(l, name, i):
            p, n, _ = PAIRS.at[name, i]
            return full[p], l * PAIRS.full[p] + n + 1

        def drained_at(l, name, i):
            p, _, n = PAIRS.at[name, i]
            return free[p], l * PAIRS.free[p] + n + 2

        def pair_of(name, i):
            return PAIRS.at[name, i][0]

        def part_of(c):
            return c if c < EARLY else c % 2

        def weights_of(l, it, c):
            if isinstance(it, int) and it == 0 and c < ESLOTS + 2:
                return c, l * (NE // ESLOTS - (1 if c >= 2 else 0)) + 1 if c < ESLOTS else l + 1
            c -= ESLOTS + 2
            fills = NE // ESLOTS - (1 if c % ESLOTS >= 2 else 0)
            return c % ESLOTS, l * fills + it + c // ESLOTS + 2

        def cols(base):
            return CON[:, base:base + P]

        ident, ones, tri = cols(C_ID), cols(C_ONE), cols(C_TRI)

        def stream(n):
            return slice(0, LAT) if n == 0 else slice(LAT, TOK)

        def further_blocks(eng, l, body, mine, first=None):
            eng.wait_ge(S["slots_ready"], upto("slots_ready", l, 1))
            eng.sem_inc(aside, 1)
            most = eng.value_load(MOST[0:1, 0:1], min_val=0, max_val=TOK)
            with eng.If(most > BLK):
                if first:
                    first()
                with eng.Fori(1, XBLK + 1) as b:
                    with eng.If(most > b * BLK):
                        with eng.Fori(0, NE) as e:
                            body(b, e, (l * XBLK + b - 1) * NE + e)
                    with eng.Else():
                        for s, n in mine:
                            eng.sem_inc(s, n * NE)
                    if eng.engine == nc.gpsimd.engine:
                        eng.sem_inc(f_turn, 1)
                    else:
                        eng.wait_ge(f_turn, l * XBLK + b)
                        eng.sem_inc(aside, 1)
            with eng.Else():
                for s, n in mine:
                    eng.sem_inc(s, n * NE * XBLK)
                if eng.engine == nc.gpsimd.engine:
                    eng.sem_inc(f_turn, XBLK)
            if eng.engine != nc.gpsimd.engine:
                eng.wait_ge(f_turn, l * XBLK + XBLK)
                eng.sem_inc(aside, 1)

        block = ctx.enter_context(nc.Block())

        @block.sync
        def _(sp):
            def small(dst, src):
                sp.dma_start(dst, src).then_inc(S["layer_in"], 16)

            def small_inputs(l):
                small(RB[:, :], A["router_b"][bass.ds(l, 1)].rearrange("a p n -> p (a n)"))
                small(GAIN, A["gains"][bass.ds(l, 1)].rearrange("a p n -> p (a n)"))
                small(ROPE.rearrange("p a b c -> p (a b c)"), A["rope"])
                small(kc, A["cache_k"][0, bass.ds(l, 1)].rearrange("a p h d -> p (a h d)"))
                sp.wait_ge(setup, l + 2)
                sp.sem_inc(aside, 1)
                for g in range(4):
                    h = g % 2
                    small(WPG[HD * h:HD * h + HD, g // 2, HD * h:HD * h + HD],
                          A["w_pool_group"][bass.ds(l, 1), g].rearrange("a c d -> c (a d)"))
                sp.dma_start(A["table"].rearrange("(p n) a -> p (n a)", p=P), A["table_init"])\
                    .then_inc(S["table_clear"], 16)

            sp.dma_start(SILU[:, :, 0:2], A["c_cols"]).then_inc(const_in, 16)
            sp.dma_start(CON[:, :], A["consts"]).then_inc(const_in, 16)

            def first_chunk(layer, c):
                _, i, _, s = CHUNKS[c]
                src = A["w_ada"][layer, :, 512 * i:512 * i + 512].rearrange("a (k p) n -> p (a k) n", p=P)
                sp.dma_start(W[:, s, :].rearrange("p (k n) -> p k n", k=DK), src).then_inc(loaded[s], 16)

            for c in range(WSLOTS):
                first_chunk(slice(0, 1), c)
            with sp.Fori(0, DEPTH) as l:
                sp.dma_start(VEC[:, :], A["vecs"][bass.ds(l, 1)].rearrange("a p n -> p (a n)")).then_inc(S["vec_in"], 16)
                for c, (name, i, _, s) in enumerate(CHUNKS):
                    slot = W[:, s, :]
                    if c < WSLOTS:
                        continue
                    if c == WSLOTS + 1:
                        small_inputs(l)
                    if name == "xp":
                        sp.wait_ge(S["x_end"], upto("x_end", l, NT))
                        sp.sem_inc(aside, 1)
                        small(V[:, 0, :], A["cache_v"][0, bass.ds(l, 1)].rearrange("a p h d -> p (a h d)"))
                    if last_of_slot[c] is not None:
                        sp.wait_ge(*used_at(l, last_of_slot[c]))
                    k8 = slot.rearrange("p (k n) -> p k n", k=DK)

                    def w_cols(w, a, b):
                        return w[bass.ds(l, 1), :, a:b].rearrange("a (k p) n -> p (a k) n", p=P)

                    if name == "ada":
                        sp.dma_start(k8, w_cols(A["w_ada"], 512 * i, 512 * i + 512)).then_inc(loaded[s], 16)
                    elif name == "q":
                        sp.dma_start(k8, w_cols(A["w_in"], 0, QW)).then_inc(loaded[s], 16)
                    elif name == "kvx":
                        sp.dma_start(k8[:, :, 0:256], w_cols(A["w_in"], QW, QW + 256)).then_inc(loaded[s], 16)
                        sp.dma_start(k8[:, :, 256:512], w_cols(A["w_in"], 1024, 1280)).then_inc(loaded[s], 16)
                    elif name == "xp":
                        sp.dma_start(slot[:, 0:2048].rearrange("p (k n) -> p k n", k=DK),
                                     w_cols(A["w_in"], 768, 1024)).then_inc(loaded[s], 16)
                    elif name in ("cos", "sin"):
                        src = A["dft"][0 if name == "cos" else 1].rearrange("(k p) n -> p k n", p=P)
                        sp.dma_start(slot[:, 0:2048].rearrange("p (k n) -> p k n", k=LT), src).then_inc(loaded[s], 16)
                    elif name == "gate":
                        sp.dma_start(k8, w_cols(A["w_in"], 1280 + 512 * i, 1792 + 512 * i)).then_inc(loaded[s], 16)
                    elif name == "ao":
                        v = A["w_attn_out"][bass.ds(l, 1)].rearrange("a (s j p) n -> s p (a j) n", s=2, p=HD)
                        for h in range(2):
                            sp.dma_start(slot[HD * h:HD * h + HD, :].rearrange("p (j n) -> p j n", j=4),
                                         v[h]).then_inc(loaded[s], 16)
                    elif name == "pf":
                        for h, w in enumerate(("w_pool_out", "w_fourier_out")):
                            sp.dma_start(slot[:, 2048 * h:2048 * h + 2048].rearrange("p (k n) -> p k n", k=2),
                                         w_cols(A[w], 0, D)).then_inc(loaded[s], 16)
                    else:
                        sp.dma_start(k8, w_cols(A["w_out"], 512 * i, 512 * i + 512)).then_inc(loaded[s], 16)
                def gate_up_weights(e, ex):
                    for u, w in enumerate(("w_expert_gate", "w_expert_up")):
                        sp.dma_start(wgu[e][:, u], A[w][bass.ds(l, 1), ex].rearrange("a b (p k) f -> p (a b k) f", p=P))\
                          .then_inc(ex_loaded[e], 16)

                def down_weights(e, ex):
                    sp.dma_start(wdn[e], A["w_expert_down"][bass.ds(l, 1), ex].rearrange("a b (p c) n -> p (a b c) n", p=P))\
                      .then_inc(dn_loaded[e], 16)

                sp.wait_ge(S["merged"], upto("merged", l, DK))
                sp.sem_inc(aside, 1)
                for e in range(ESLOTS):
                    if e == 2:
                        sp.wait_ge(*filled_at(l, "mix", NT - 1))
                        sp.sem_inc(aside, 1)
                    gate_up_weights(e, slice(e, e + 1))
                    down_weights(e, slice(e, e + 1))
                sp.wait_ge(S["h_ready"], upto("h_ready", l, NT))
                sp.sem_inc(aside, 1)
                gate_up_weights(ESLOTS, slice(ESLOTS, ESLOTS + 1))
                down_weights(ESLOTS, slice(ESLOTS, ESLOTS + 1))
                down_weights(ESLOTS + 1, slice(ESLOTS + 1, ESLOTS + 2))
                for e in range(2):
                    sp.wait_ge(rows_in[e], l * (NE // 2 + 1) * 16 + 16)
                    sp.sem_inc(aside, 1)
                gate_up_weights(ESLOTS + 1, slice(ESLOTS + 1, ESLOTS + 2))

                def next_weights(s, i, before):
                    n = l * NE + before
                    ex = slice(i, i + 1) if isinstance(i, int) else bass.ds(i, 1)
                    sp.wait_ge(gu_full, n + 3)
                    sp.sem_inc(aside, 1)
                    gate_up_weights(s, ex)
                    sp.wait_ge(dn_full, n + 3)
                    sp.sem_inc(aside, 1)
                    down_weights(s, ex)

                for s in range(ESLOTS):
                    next_weights(s, ESLOTS + 2 + s, s)
                with sp.Fori(1, NE // ESLOTS - 2) as it:
                    for s in range(ESLOTS):
                        next_weights(s, it * ESLOTS + ESLOTS + 2 + s, it * ESLOTS + 2 + s)
                for s in range(2):
                    next_weights(s, NE - 2 + s, NE - 2 - ESLOTS + s)
                def next_layer(c):
                    with sp.If(l < DEPTH - 1):
                        first_chunk(bass.ds(nc.s_assert_within(
                            l + 1, 1, DEPTH - 1, skip_runtime_bounds_check_because="l < DEPTH - 1 here"), 1), c)

                sp.wait_ge(dn_full, l * NE + NE - ESLOTS + 3)
                sp.sem_inc(aside, 1)
                sp.wait_ge(rows_in[1], (l * (NE // 2 + 1) + NE // 2) * 16)
                sp.sem_inc(aside, 1)
                next_layer(0)
                sp.wait_ge(dn_full, l * NE + NE - 2 + 3)
                sp.sem_inc(aside, 1)
                next_layer(1)

                def weights_again(b, e, n):
                    sp.wait_ge(f_rows, n + 1)
                    sp.sem_inc(aside, 1)
                    ex = bass.ds(e, 1)
                    for u, w in enumerate(("w_expert_gate", "w_expert_up")):
                        sp.dma_start(wgu[0][:, u], A[w][bass.ds(l, 1), ex].rearrange("a b (p k) f -> p (a b k) f", p=P))\
                          .then_inc(f_loaded, 16)
                    sp.dma_start(wdn[0], A["w_expert_down"][bass.ds(l, 1), ex].rearrange("a b (p c) n -> p (a b c) n", p=P))\
                      .then_inc(f_loaded, 16)
                    sp.wait_ge(f_loaded, 48 * n + 48)
                    sp.sem_inc(aside, 1)

                further_blocks(sp, l, weights_again, [(f_loaded, 48)])
                sp.wait_ge(yg_in[0], l * 16 + 16)
                sp.sem_inc(aside, 1)
                next_layer(2)

            for i in range(NT):
                sp.wait_ge(S["x_end"], DEPTH * per["x_end"] + i + 1)
                to = A["out_s"][0, P * i:P * i + P, :] if i < LT else A["out_p"][0]
                sp.dma_start(to, X[:, i, :]).then_inc(done, 16)
            sp.wait_ge(done, 16 * NT)

        @block.gpsimd
        def _(pool):
            def hold(s, value):
                pool.wait_ge(s, value)
                pool.sem_inc(aside, 1)

            def link(l, ins):
                count["pool_step"] += 1
                ins.then_inc(S["pool_step"], 1)
                hold(S["pool_step"], upto("pool_step", l, count["pool_step"]))

            for k in range(2):
                pool.dma_start(TID[:, k, :], A["token_ids"][:, k, :]).then_inc(y_sent[k], 16)

            def rstd(l, wait, n, src, dst, inc):
                hold(S[wait], upto(wait, l, n))
                link(l, pool.tensor_scalar(dst, src, 1.0 / D, EPS, ALU.mult, ALU.add))
                w = dst.shape[1]
                pool.tensor_tensor(dst, dst, HALF[:, 0:w], ALU.pow).then_inc(S[inc], 1)

            for k in range(2):
                pool.wait_ge(y_sent[k], 16)
            pool.memset(HALF[:, :], -0.5).then_inc(setup, 1)
            pool.wait_ge(setup, 1)
            pool.memset(WPG, 0.0).then_inc(setup, 1)
            blocks16 = pool.alloc_register("blocks16")
            pool.reg_mov(blocks16, 0)
            in_table = pool.alloc_register("in_table")
            pool.reg_mov(in_table, 0)

            def x_rstd(l, i):
                hold(S["x_sumsq"], upto("x_sumsq", l, i + 1))
                pool.tensor_scalar(ST[:, 1, i:i + 1], ST[:, 0, i:i + 1], 1.0 / D, EPS, ALU.mult, ALU.add)\
                    .then_inc(S["x_ms"], 1)
                hold(S["x_ms"], upto("x_ms", l, i + 1))
                pool.tensor_tensor(ST[:, 1, i:i + 1], ST[:, 1, i:i + 1], HALF[:, 0:1], ALU.pow).then_inc(S["rstd1"], 1)

            for i in range(NT - 1):
                x_rstd(0, i)
            with pool.Fori(0, DEPTH) as l:
                count["pool_step"] = 0
                x_rstd(l, NT - 1)
                for i in range(NT):
                    hold(S["qk_sq"], upto("qk_sq", l, i + 1))
                    a, b = qst[:, (i % 2) * 2, :], qst[:, (i % 2) * 2 + 1, :]
                    link(l, pool.tensor_scalar(b, a, 1.0 / HD, EPS, ALU.mult, ALU.add))
                    pool.tensor_tensor(b, b, HALF[:, 0:NHEADS], ALU.pow).then_inc(S["qk_rstd"], 1)
                hold(S["merged"], upto("merged", l, DK))
                hold(*filled_at(l, "mfour", DK - 1))
                pool.dma_start(WR, A["w_router"][bass.ds(l, 1)].rearrange("a (k p) n -> p (a k) n", p=P))\
                    .then_inc(S["wr_in"], 16)
                for i in range(NT):
                    rstd(l, "mix_sq", i + 1, ST[:, 2, i:i + 1], ST[:, 3, i:i + 1], "mix_rstd")
                    rstd(l, "x2_sq", i + 1, ST[:, 4, i:i + 1], ST[:, 5, i:i + 1], "x2_rstd")
                    hold(S["h_ready"], upto("h_ready", l, i + 1))
                    pool.dma_start(A["h_rows"][P * i:P * i + P, :], hrow[:, i % 2, :])\
                        .then_inc(S[f"h_sent{i % 2}"], 16)
                pool.memset(IDX[:, 1, NE:NE + 2], 2 * TOK).then_inc(S["no_rows"], 1)
                hold(*filled_at(l, "pos", 0))
                pool.memset(HT[0:BLK, 0:2 * D], 0.0).then_inc(S["xg_zero"], 1)
                hold(S["no_rows"], upto("no_rows", l, 1))
                hold(S["xg_zero"], upto("xg_zero", l, 1))
                for e in range(2):
                    hold(S[f"h_sent{e}"], upto(f"h_sent{e}", l, per[f"h_sent{e}"]))
                hold(S["ids_ready"], upto("ids_ready", l, 1))

                def gather(e, nth, col):
                    pool.tensor_copy(IDC[0:BLK, e:e + 1], IDX[0:BLK, 1, slice(col, col + 1) if isinstance(col, int) else bass.ds(col, 1)])\
                        .then_inc(idc[e], 1)
                    hold(idc[e], nth)
                    pool.indirect_dma_start(
                        out=xg[0:BLK, e, :], out_offset=None, in_=A["h_rows"],
                        in_offset=bass.IndirectOffsetOnAxis(ap=IDC[0:BLK, e:e + 1], axis=0),
                        bounds_check=TOK - 1, oob_is_err=False).then_inc(rows_in[e], 16)

                for e in range(2):
                    gather(e, l * (NE // 2 + 1) + 1, e)

                def next_gather(it, e):
                    q = l * (NE // 2) + it
                    hold(xT_full, q * 2 + e + 3)
                    hold(rows_in[e], (q + l) * 16 + 16)
                    gather(e, q + l + 2, it * 2 + 2 + e)

                def scatter(it, e):
                    q = l * (NE // 2) + it
                    col = it * 2 + e
                    hold(y_out, q * 2 + e + 3)
                    at = slice(col, col + 1) if isinstance(col, int) else bass.ds(col, 1)
                    pool.tensor_copy(IDC[:, 2 + e:3 + e], IDX[:, 2, at]).then_inc(idy[e], 1)
                    hold(idy[e], q + 1)
                    pool.indirect_dma_start(
                        out=A["y_half_rows"], out_offset=bass.IndirectOffsetOnAxis(ap=IDC[:, 2 + e:3 + e], axis=0),
                        in_=yb[:, e, :], in_offset=None,
                        bounds_check=4 * TOK - 1, oob_is_err=False).then_inc(y_sent[e], 16)

                for e in range(2):
                    next_gather(0, e)
                with pool.Fori(1, NE // 2) as it:
                    for e in range(2):
                        next_gather(it, e)
                        scatter(it - 1, e)
                for e in range(2):
                    scatter(NE // 2 - 1, e)
                for e in range(2):
                    hold(y_sent[e], (l + 1) * (NE // 2) * 16 + 16)

                def more_rows(b, e, n):
                    pool.reg_add(blocks16, blocks16, 16)
                    in_all = pool.snap(blocks16)
                    ids = A["table"].rearrange("(b p x) a -> b p (x a)", p=BLK, x=NE)[bass.ds(b, 1)]
                    for h in range(2):
                        pool.dma_start(IDX[BLK * h:BLK * h + BLK, 0, 0:NE], ids.rearrange("b p x -> p (b x)"))\
                            .then_inc(f_ids, 16)
                    hold(f_ids, in_all * 2)
                    now, token, half = IDC[:, 3:4], IDX[:, 1, 0:1], IDX[:, 2, 0:1]
                    pool.tensor_copy(now, IDX[:, 0, bass.ds(e, 1)]).then_inc(f_step, 1)
                    hold(f_step, 4 * n + 1)
                    pool.tensor_scalar(token, now, float(TOK), -float(TOK), ALU.is_ge, ALU.mult).then_inc(f_step, 1)
                    pool.tensor_scalar(half, now, 2.0, CON[:, C_HALF:C_HALF + 1], ALU.mult, ALU.add).then_inc(f_step, 1)
                    hold(f_step, 4 * n + 3)
                    pool.tensor_tensor(IDC[0:BLK, 0:1], token[0:BLK], now[0:BLK], ALU.add).then_inc(f_step, 1)
                    hold(f_step, 4 * n + 4)
                    pool.indirect_dma_start(
                        out=xg[0:BLK, 0, :], out_offset=None, in_=A["h_rows"],
                        in_offset=bass.IndirectOffsetOnAxis(ap=IDC[0:BLK, 0:1], axis=0),
                        bounds_check=TOK - 1, oob_is_err=False).then_inc(f_gathered, 16)
                    hold(f_gathered, in_all)
                    pool.sem_inc(f_rows, 1)
                    hold(f_y, n + 1)
                    pool.tensor_copy(IDC[:, 2:3], half).then_inc(f_done, 1)
                    hold(f_done, n + 1)
                    pool.indirect_dma_start(
                        out=A["y_half_rows"], out_offset=bass.IndirectOffsetOnAxis(ap=IDC[:, 2:3], axis=0),
                        in_=yb[:, 0, :], in_offset=None,
                        bounds_check=4 * TOK - 1, oob_is_err=False).then_inc(f_sent, 16)
                    hold(f_sent, in_all)

                for e in range(2):
                    hold(rows_in[e], (l + 1) * (NE // 2 + 1) * 16)

                def set_table():
                    pool.reg_add(in_table, in_table, 16 * 2 * NT)
                    hold(S["table_clear"], upto("table_clear", l, 16))
                    for k in range(2):
                        for i in range(NT):
                            pool.indirect_dma_start(
                                out=A["table"], out_offset=bass.IndirectOffsetOnAxis(ap=SLOT[:, k, i:i + 1], axis=0),
                                in_=TID[:, k, i:i + 1], in_offset=None).then_inc(table_set, 16)
                    hold(table_set, pool.snap(in_table))

                further_blocks(pool, l, more_rows, [(f_step, 4), (f_rows, 1), (f_done, 1)], set_table)
                for i in range(NT):
                    pool.dma_start(yg[i].rearrange("p k (h n) -> p k h n", h=2),
                                   A["y_half_rows"].rearrange("(k t h) n -> t k h n", k=2, h=2)[P * i:P * i + P])\
                        .then_inc(yg_in[i], 16)
                pool.memset(WPG, 0.0).then_inc(setup, 1)
                for i in range(NT):
                    rstd(l, "y_sq", i + 1, ST[:, 2, i:i + 1], ST[:, 3, i:i + 1], "y_rstd")
                    if i:
                        x_rstd(l + 1, i - 1)

        @block.scalar
        def _(act):
            def link(l, ins):
                count["act_step"] += 1
                ins.then_inc(S["act_step"], 1)
                act.wait_ge(S["act_step"], upto("act_step", l, count["act_step"]))

            act.dma_start(X[:, 0:LT, :], A["x_sample"][0].rearrange("(i p) n -> p i n", p=P)).then_inc(x_in, 16)
            act.dma_start(X[:, LT, :], A["x_prompt"][0]).then_inc(x_in, 16)
            act.wait_ge(const_in, 32)
            act.activation(SILU[:, :, 2:4], SILU[:, :, 0:2], ACT.Tanh, scale=0.5).then_inc(silu_a, 1)
            act.wait_ge(x_in, 32)

            def x_squares(l, i):
                act.wait_ge(S["x_end"], upto("x_end", l, i + 1))
                act.activation(junk, X[:, i, :], ACT.Square, accum_out=ST[:, 0, i:i + 1]).then_inc(S["x_sumsq"], 1)
                act.wait_ge(S["x_sumsq"], upto("x_sumsq", l, i + 1))

            for i in range(NT - 1):
                x_squares(0, i)
            with act.Fori(0, DEPTH) as l:
                count["act_step"] = 0
                def partial_sums(c):
                    p = pair_of("ada", c)
                    act.wait_ge(*filled_at(l, "ada", c))
                    if c >= EARLY:
                        act.wait_ge(S["ada_cols"], upto("ada_cols", l, c - 1))
                    act.activation(part[part_of(c)], bank(2 * p), ACT.Copy).then_inc(free[p], 1)

                for c in range(EARLY):
                    if c == EARLY - 1:
                        x_squares(l, NT - 1)
                    partial_sums(c)
                act.wait_ge(S["affine_ready"], upto("affine_ready", l, 1))
                for k in range(0, DK, 2):
                    act.wait_ge(*filled_at(l, "hT", k))
                    for s in range(2):
                        ins = act.activation(hT[:, k, stream(s)], pair(pair_of("hT", k))[:, stream(s)], ACT.Identity,
                                             bias=MOD[:, 0, k, s:s + 1], scale=AFF[:, 0, k, s:s + 1])
                    ins.then_inc(free[pair_of("hT", k)], 1)
                def qkT(i):
                    act.wait_ge(*filled_at(l, "qkT", i))
                    p = pair_of("qkT", i)
                    to = slice(P * i, P * i + P)
                    if i < NT:
                        act.activation(qT[:, :, to], bank(2 * p).rearrange("p (j t) -> p j t", j=4), ACT.Copy)
                        to = slice(P + P * i, 2 * P + P * i)
                    else:
                        to = slice(0, P)
                    for s in range(2):
                        h = slice(HD * s, HD * s + HD)
                        ins = act.activation(kT[h, s, to], PS[h, 2 * p + 1, 0:P], ACT.Copy)
                    ins.then_inc(free[p], 1)

                for i in range(NT):
                    act.wait_ge(*filled_at(l, "qkv", i))
                    p = pair(pair_of("qkv", i))
                    if i >= 2:
                        act.wait_ge(S["qk_rot"], upto("qk_rot", l, i - 1))
                    act.activation(qraw[:, i % 2, :], p[:, 0:640], ACT.Copy).then_inc(S["qk_raw"], 1)
                    if i == NT - 1:
                        link(l, act.activation(V[:, 1 + i, :], p[:, 640:768], ACT.Copy))
                        act.dma_start(A["out_v"][0, bass.ds(l, 1)].rearrange("a p h d -> p (a h d)"), V[:, 1 + i, :])\
                           .then_inc(S["kv_out"], 16)
                    else:
                        act.activation(V[:, 1 + i, :], p[:, 640:768], ACT.Copy)
                    act.activation(XF[:, i, :], p[:, 768:1024], ACT.Copy).then_inc(free[pair_of("qkv", i)], 1)
                    if i:
                        qkT(i - 1)
                act.wait_ge(S["qk_rot"], upto("qk_rot", l, NT))
                act.dma_start(A["out_k"][0, bass.ds(l, 1)].rearrange("a p h d -> p (a h d)"),
                              qrot[:, (NT - 1) % 2, QW:640]).then_inc(S["kv_out"], 16)
                qkT(NT - 1)
                qkT(NT)
                for c in range(2):
                    act.wait_ge(*filled_at(l, "xp", c))
                    p = pair(c)
                    act.activation(xpT[:, c, POOL_PAD:POOL_PAD + LAT], p[:, 0:LAT], ACT.Copy)
                    act.activation(xpT[:, c, 3 * POOL_PAD + LAT:3 * POOL_PAD + TOK], p[:, LAT:TOK], ACT.Copy)\
                       .then_inc(free[c], 1)
                for j in range(4):
                    act.wait_ge(*filled_at(l, "dft", j))
                    act.activation(AB[:, j, :], pair(pair_of("dft", j))[:, 0:TOK], ACT.Copy)\
                       .then_inc(free[pair_of("dft", j)], 1)
                for c in range(2):
                    act.wait_ge(*filled_at(l, "plin", c))
                    act.activation(PM[:, c, :], pair(pair_of("plin", c))[:, 0:TOK], ACT.Copy,
                                   scale=VEC[:, V_PS + c:V_PS + c + 1]).then_inc(free[pair_of("plin", c)], 1)
                for c in range(2):
                    act.wait_ge(*filled_at(l, "four", c))
                    act.activation(FM[:, c, :], pair(pair_of("four", c))[:, 0:TOK], ACT.Copy)\
                       .then_inc(free[pair_of("four", c)], 1)
                act.wait_ge(S["kv_out"], upto("kv_out", l, 32))
                n_s = 0
                for what, x in STEPS:
                    if what == "ada":
                        partial_sums(x)
                    elif what == "ctxS":
                        act.wait_ge(*drained_at(l, "ctxS", 0))
                        act.activation(cP.rearrange("p h t -> p (h t)"), cP.rearrange("p h t -> p (h t)"), ACT.Exp,
                                       scale=SCALE).then_inc(S["cprob"], 1)
                    elif what == "ctxT":
                        act.wait_ge(*filled_at(l, "ctxT", 0))
                        act.activation(cPT.rearrange("p h t -> p (h t)"), pair(3), ACT.Copy).then_inc(free[3], 1)
                    elif what == "gates" and x[1] == PARTS - 1:
                        g, p = x[0], pair_of("gate", x[0])
                        act.wait_ge(*filled_at(l, "gate", g))
                        act.activation(TG[:, g // DK, g % DK, :], pair(p)[:, 0:TOK], ACT.Tanh, scale=0.5)\
                           .then_inc(free[p], 1)
                    elif what == "S":
                        h, t = x
                        n_s += 1
                        act.wait_ge(S["smax"], upto("smax", l, n_s))
                        if h:
                            act.wait_ge(S["tr_full"], upto("tr_full", l, 5 * h))
                        act.activation(PR[:, t, :], pair(2)[:, 0:KEYS], ACT.Exp, scale=SCALE,
                                       bias=aST[:, 0, t:t + 1], accum_out=aST[:, 1, t:t + 1]).then_inc(free[2], 1)
                    elif what == "T":
                        n = 5 * x[0] + x[1]
                        if n % 2:
                            act.wait_ge(S["tr_full"], upto("tr_full", l, n + 1))
                            act.activation(PT[:, 1, :], bank((6, 4)[x[1] % 2]), ACT.Copy).then_inc(S["ptT1"], 1)
                act.wait_ge(*filled_at(l, "vecT", 0))
                act.activation(VROW[0:64], PS[0:64, 0, 0:P], ACT.Copy).then_inc(free[0], 1)
                act.wait_ge(*drained_at(l, "vecT", 0))
                act.dma_start(A["vec_rows"].rearrange("v (k n) -> (v k) n", n=P), VROW[0:64]).then_inc(S["rows_in_dram"], 16)
                act.wait_ge(S["rows_in_dram"], upto("rows_in_dram", l, 16))
                act.sem_inc(aside, 1)
                act.dma_start(ROW, A["vec_rows"].unsqueeze(0).broadcast_to([P, 8, D])).then_inc(S["rows_ready"], 16)
                for i in range(NT + 1):
                    if i < NT:
                        act.wait_ge(*filled_at(l, "mix", i))
                        act.activation(junk, pair(i % 2), ACT.Square, scale=0.5, accum_out=ST[:, 2, i:i + 1])\
                           .then_inc(S["mix_sq"], 1)
                        act.wait_ge(S["mix_sq"], upto("mix_sq", l, i + 1))
                    if i:
                        j = i - 1
                        act.wait_ge(*filled_at(l, "h2T", j))
                        p = pair_of("h2T", j)
                        act.activation(hT[:, :, P * j:P * j + P], pair(p).rearrange("p (k t) -> p k t", k=DK),
                                       ACT.Copy).then_inc(free[p], 1)
                    if i < NT:
                        act.wait_ge(S["x_mid"], upto("x_mid", l, i + 1))
                        act.activation(junk, X[:, i, :], ACT.Square, accum_out=ST[:, 4, i:i + 1])\
                           .then_inc(S["x2_sq"], 1)
                        act.wait_ge(S["x2_sq"], upto("x2_sq", l, i + 1))
                act.wait_ge(S["sel_in"], upto("sel_in", l, 1))
                act.activation(EX[:, 1], EX[:, 0], ACT.Exp).then_inc(S["sel_exp"], 1)
                def x_out(m, e):
                    act.wait_ge(xT_full, m + 3)
                    act.wait_ge(gu_full, m + 1)
                    act.activation(xT[:, e].rearrange("p k t -> p (k t)"), bank(e), ACT.Copy).then_inc(xT_out, 1)

                def tanh(m, e):
                    act.wait_ge(gt_full, m + 3)
                    act.wait_ge(h_out, m + 2)
                    act.activation(th, bank(4 + e)[:, 0:256].rearrange("p (c t) -> p c t", c=2)[:, :, 0:BLK],
                                   ACT.Tanh, scale=0.5).then_inc(th_out, 1)

                def y_rows(m, q, e):
                    act.wait_ge(dn_full, m + 3)
                    act.wait_ge(y_sent[e], q * 16 + 16)
                    act.activation(yb[:, e, :], bank(6 + e), ACT.Copy, scale=0.5).then_inc(y_out, 1)

                m0, q0 = l * NE, l * (NE // 2)
                x_out(m0, 0)
                x_out(m0 + 1, 1)
                tanh(m0, 0)
                with act.Fori(0, NE // 2 - 1) as it:
                    m, q = l * NE + it * 2, l * (NE // 2) + it
                    x_out(m + 2, 0)
                    y_rows(m, q, 0)
                    tanh(m + 1, 1)
                    x_out(m + 3, 1)
                    y_rows(m + 1, q, 1)
                    tanh(m + 2, 0)
                y_rows(m0 + NE - 2, q0 + NE // 2 - 1, 0)
                tanh(m0 + NE - 1, 1)
                y_rows(m0 + NE - 1, q0 + NE // 2 - 1, 1)

                def more_act(b, e, n):
                    act.wait_ge(f_xT, n + 1)
                    act.activation(xT[:, 0].rearrange("p k t -> p (k t)"), bank(0), ACT.Copy).then_inc(f_xo, 1)
                    act.wait_ge(f_gt, n + 1)
                    act.activation(th, bank(4)[:, 0:256].rearrange("p (c t) -> p c t", c=2)[:, :, 0:BLK],
                                   ACT.Tanh, scale=0.5).then_inc(f_th, 1)
                    act.wait_ge(f_dn, n + 1)
                    act.activation(yb[:, 0, :], bank(6), ACT.Copy, scale=0.5).then_inc(f_y, 1)

                further_blocks(act, l, more_act, [(f_xo, 1), (f_th, 1), (f_y, 1)])
                for i in range(NT + 1):
                    if i < NT:
                        act.wait_ge(yg_in[i], l * 16 + 16)
                        act.activation(yg[i][:, 0, :], yg[i][:, 0, :], ACT.Copy, scale=RS[:, 5, i:i + 1])\
                           .then_inc(S["y_scaled"], 1)
                    if 1 <= i <= NT:
                        j = i - 1
                        act.wait_ge(S["y_sum"], upto("y_sum", l, i))
                        act.activation(junk, yg[j][:, 0, :], ACT.Square, accum_out=ST[:, 2, j:j + 1])\
                           .then_inc(S["y_sq"], 1)
                        act.wait_ge(S["y_sq"], upto("y_sq", l, i))
                    if i >= 2:
                        x_squares(l + 1, i - 2)
            act.wait_ge(S["kv_out"], DEPTH * 32)

        @block.vector
        def _(dve):
            def link(l, ins):
                count["dve_step"] += 1
                ins.then_inc(S["dve_step"], 1)
                dve.wait_ge(S["dve_step"], upto("dve_step", l, count["dve_step"]))

            def bc(ap, axis, shape):
                return ap.unsqueeze(axis).broadcast_to([P] + list(shape))

            for p in range(4):
                dve.sem_inc(free[p], 1)
            dve.sem_inc(S["x_end"], per["x_end"])
            for s in (xT_full, xT_out, gu_full, gu_out, gt_full, h_out, dn_full, y_out):
                dve.sem_inc(s, 2)
            dve.wait_ge(const_in, 32)
            dve.wait_ge(silu_a, 1)
            dve.scalar_tensor_tensor(SILU[:, :, 0:2], SILU[:, :, 2:4], 1.0, SILU[:, :, 0:2], ALU.add, ALU.mult)\
               .then_inc(silu_b, 1)
            dve.wait_ge(silu_b, 1)
            dve.tensor_scalar(SILU[:, :, 0:2], SILU[:, :, 0:2], 0.5, None, ALU.mult).then_inc(silu_b, 1)
            dve.memset(SILU[:, :, 2:32], 0.0).then_inc(silu_b, 1)

            with dve.Fori(0, DEPTH) as l:
                count["dve_step"] = 0
                dve.wait_ge(S["x_end"], upto("x_end", l, NT))
                for i in range(NT):
                    dve.wait_ge(S["rstd1"], upto("rstd1", l, i + 1))
                    dve.tensor_scalar(xn[:, i, :], X[:, i, :], ST[:, 1, i:i + 1], None, ALU.mult).then_inc(S["xn_ready"], 1)
                dve.memset(kT[HD:P, 0, :], 0.0)
                dve.memset(kT[0:HD, 1, :], 0.0)
                for a, b in ((0, POOL_PAD), (POOL_PAD + LAT, 3 * POOL_PAD + LAT), (PL - POOL_PAD, PL)):
                    dve.memset(xpT[:, :, a:b], 0.0)
                dve.wait_ge(S["vec_in"], upto("vec_in", l, 16))

                def ada_columns(c):
                    dve.wait_ge(S["ada_cols"], upto("ada_cols", l, c + 1))
                    dve.tensor_tensor(MOD[:, c // 2, 4 * (c % 2):4 * (c % 2) + 4, :],
                                      PS[:, 2 * pair_of("ada", c) + 1, 0:8].rearrange("p (k t) -> p k t", t=2),
                                      bc(VEC[:, V_BADA + 4 * c:V_BADA + 4 * c + 4], 2, (4, 2)), ALU.add)\
                       .then_inc(free[pair_of("ada", c)], 1)

                def affine(n, sec, add, mul, gain):
                    return dve.scalar_tensor_tensor(AFF[:, n], MOD[:, sec], add if mul is None else mul,
                                                    bc(VEC[:, gain:gain + DK], 2, (DK, 2)),
                                                    ALU.add if mul is None else ALU.mult, ALU.mult)

                def columns_in(c):
                    p, _, n = PAIRS.at["ada", c]
                    dve.wait_ge(free[p], l * PAIRS.free[p] + n + 3)

                for c in range(EARLY):
                    ada_columns(c)
                for c in (2, 3):
                    columns_in(c)
                affine(0, 1, 1.0, None, V_MPRE).then_inc(S["affine_ready"], 1)
                for c in (0, 1):
                    columns_in(c)
                dve.wait_ge(S["affine_ready"], upto("affine_ready", l, 1))
                for k in range(1, DK, 2):
                    dve.wait_ge(*filled_at(l, "hT", k))
                    for s in range(2):
                        ins = dve.tensor_scalar(hT[:, k, stream(s)], pair(pair_of("hT", k))[:, stream(s)],
                                                AFF[:, 0, k, s:s + 1], MOD[:, 0, k, s:s + 1], ALU.mult, ALU.add)
                    ins.then_inc(free[pair_of("hT", k)], 1)
                dve.wait_ge(S["layer_in"], upto("layer_in", l, per["layer_in"]))
                for i in range(NT):
                    raw, st = qraw[:, i % 2, :], (i % 2) * 2
                    dve.wait_ge(S["qk_raw"], upto("qk_raw", l, i + 1))
                    if i:
                        dve.wait_ge(S["qk_rot"], upto("qk_rot", l, i))
                    link(l, dve.tensor_tensor(qsq, raw, raw, ALU.mult))
                    dve.tensor_reduce(qst[:, st, :], qsq.rearrange("p (h d) -> p h d", d=HD), AX.X, ALU.add)\
                       .then_inc(S["qk_sq"], 1)
                    dve.wait_ge(S["qk_rstd"], upto("qk_rstd", l, i + 1))
                    link(l, dve.tensor_tensor(qa.rearrange("p (h d) -> p h d", d=HD), raw.rearrange("p (h d) -> p h d", d=HD),
                                              bc(qst[:, st + 1, :], 2, (NHEADS, HD)), ALU.mult))
                    if i >= 2:
                        dve.wait_ge(*filled_at(l, "qkT", i - 2))
                    out_q = qrot[:, i % 2, 0:QW].rearrange("p (j s d) -> p s j d", j=4, s=2)
                    out_k = qrot[:, i % 2, QW:640]
                    if i < LT:
                        link(l, dve.tensor_tensor(qb, qa, GAIN, ALU.mult))
                        x5 = qb.rearrange("p (h a f c) -> p h a f c", a=2, f=2, c=16)
                        y5 = qsq.rearrange("p (h a f c) -> p h a f c", a=2, f=2, c=16)
                        r5 = ROPE[:, 1, i, :].rearrange("p (a f c) -> p a f c", a=2, f=2)
                        dve.tensor_tensor(qa.rearrange("p (h d) -> p h d", d=HD), qb.rearrange("p (h d) -> p h d", d=HD),
                                          bc(ROPE[:, 0, i, :], 1, (NHEADS, HD)), ALU.mult)
                        for f in range(2):
                            ins = dve.tensor_tensor(y5[:, :, :, f, :], x5[:, :, :, 1 - f, :],
                                                    bc(r5[:, :, f, :], 1, (NHEADS, 2, 16)), ALU.mult)
                        link(l, ins)
                        a, b, op = qa, qsq, ALU.add
                    else:
                        a, b, op = qa, GAIN, ALU.mult
                    dve.tensor_tensor(out_q, a[:, 0:QW].rearrange("p (s j d) -> p s j d", s=2, j=4),
                                      b[:, 0:QW].rearrange("p (s j d) -> p s j d", s=2, j=4), op)
                    dve.tensor_tensor(out_k, a[:, QW:640], b[:, QW:640], op).then_inc(S["qk_rot"], 1)
                for c in range(2):
                    dve.wait_ge(*drained_at(l, "xp", c))
                    x = xpT[:, c, :]

                    def double(to, of, half, lo, part=slice(0, P)):
                        a, b = lo, PL - lo
                        up = half if half else 0
                        dn = half if half else 1
                        link(l, dve.tensor_tensor(to[part, a:b], of[part, a - dn:b - dn], of[part, a + up:b + up], ALU.add))

                    double(pS[0], x, 0, 1)
                    if c == 0:
                        low, high, half, lo = pS[0], pS[1], 1, 2
                    else:
                        double(pS[1], pS[0], 1, 2)
                        double(pS[2], pS[1], 2, 4)
                        low, high, half, lo = pS[2], pS[0], 4, 8
                    dve.tensor_copy(high[0:HD, POOL_PAD:PL - POOL_PAD], low[0:HD, POOL_PAD:PL - POOL_PAD])
                    double(high, low, half, lo, slice(HD, P))
                    for side, at, step in ((0, POOL_PAD, LAT + 2 * POOL_PAD), (1, LAT, CTX + 2 * POOL_PAD)):
                        e = C_EDGE + (2 * side + c) * 8
                        for n in range(2):
                            v = high[:, at + n * step:at + n * step + 8]
                            ins = dve.tensor_tensor(v, v, CON[:, e:e + 8], ALU.mult)
                    link(l, ins)
                    for s, at in ((0, POOL_PAD), (1, 3 * POOL_PAD + LAT)):
                        n = LAT if s == 0 else CTX
                        ins = dve.scalar_tensor_tensor(pooled[:, c, stream(s)], high[:, at:at + n],
                                                       CON[:, C_WINV + c:C_WINV + c + 1], x[:, at:at + n],
                                                       ALU.mult, ALU.subtract)
                    ins.then_inc(S["pooled"], 1)
                    dve.wait_ge(S["pooled"], upto("pooled", l, c + 1))
                def normalise(h, t):
                    dve.wait_ge(*drained_at(l, "S", (h, t)))
                    link(l, dve.reciprocal(aST[:, 2, t:t + 1], aST[:, 1, t:t + 1]))
                    dve.tensor_scalar(PR[:, t, :], PR[:, t, :], aST[:, 2, t:t + 1], None, ALU.mult)\
                       .then_inc(S["pnorm"], 1)

                for what, x in STEPS:
                    if what == "adacol":
                        ada_columns(x)
                    elif what == "ctxS":
                        dve.wait_ge(*filled_at(l, "ctxS", 0))
                        sc = pair(2).rearrange("p (h t) -> p h t", h=NH)
                        link(l, dve.tensor_reduce(aST[:, 0, :], sc, AX.X, ALU.max))
                        dve.tensor_tensor(cP, sc, bc(aST[:, 0, :], 2, (NH, P)), ALU.subtract).then_inc(free[2], 1)
                        dve.wait_ge(S["cprob"], upto("cprob", l, 1))
                        link(l, dve.tensor_reduce(aST[:, 1, :], cP, AX.X, ALU.add))
                        link(l, dve.reciprocal(aST[:, 2, :], aST[:, 1, :]))
                        dve.tensor_tensor(cP, cP, bc(aST[:, 2, :], 2, (NH, P)), ALU.mult).then_inc(S["cpn"], 1)
                    elif what == "ctxO":
                        dve.wait_ge(*filled_at(l, "ctxO", 0))
                        dve.tensor_copy(OT[:, :, LAT:TOK], bank(4).rearrange("p (j t) -> p j t", j=4)).then_inc(free[2], 1)
                    elif what == "S":
                        h, t = x
                        dve.wait_ge(*filled_at(l, "S", (h, t)))
                        link(l, dve.tensor_reduce(aST[:, 0, t:t + 1], pair(2)[:, 0:KEYS], AX.X, ALU.max))
                        dve.tensor_scalar(aST[:, 0, t:t + 1], aST[:, 0, t:t + 1], -SCALE, None, ALU.mult)\
                           .then_inc(S["smax"], 1)
                        if t:
                            normalise(h, t - 1)
                    elif what == "T":
                        h, kt = x
                        n = 5 * h + kt
                        if kt == 0:
                            normalise(h, LT - 1)
                        if n % 2 == 0:
                            dve.wait_ge(S["tr_full"], upto("tr_full", l, n + 1))
                            dve.tensor_copy(PT[:, 0, :], bank((6, 4)[kt % 2])).then_inc(S["ptT0"], 1)
                    elif what == "O" and x[1] == 4:
                        h = x[0]
                        s, j = h // 4, h % 4
                        dve.wait_ge(S["pv_full"], upto("pv_full", l, h + 1))
                        dve.tensor_copy(OT[HD * s:HD * s + HD, j, 0:LAT], PS[HD * s:HD * s + HD, 7, :])\
                           .then_inc(S["o_ready"], 1)
                for c in range(EARLY, 12):
                    columns_in(c)
                affine(1, 2, None, 0.5, V_MPOST)
                affine(2, 4, 1.0, None, V_FPRE)
                link(l, affine(3, 5, None, 1.0, V_FPOST))
                for n, vec in enumerate((AFF[:, 1], AFF[:, 2], MOD[:, 3], AFF[:, 3])):
                    ins = dve.tensor_copy(VCOL[:, n], vec.rearrange("p k s -> p s k"))
                ins.then_inc(S["vecs_ready"], 1)
                for d in range(DK):
                    for b, name in enumerate(("mattn", "mpool", "mfour")):
                        dve.wait_ge(*filled_at(l, name, d))
                        p = pair_of(name, d)
                        to = hT[:, d, :] if b == 0 else TG[:, b, d, :]
                        dve.scalar_tensor_tensor(to, TG[:, b, d, :], 1.0, pair(p)[:, 0:TOK], ALU.add, ALU.mult)\
                           .then_inc(free[p], 1)
                        if b:
                            dve.wait_ge(*drained_at(l, name, d))
                            ins = dve.tensor_tensor(hT[:, d, :], hT[:, d, :], TG[:, b, d, :], ALU.add)
                            if b == 1:
                                link(l, ins)
                    ins.then_inc(S["merged"], 1)

                def mixed(i):
                    s = 0 if i < LT else 1
                    dve.wait_ge(*filled_at(l, "mix", i))
                    dve.wait_ge(S["mix_rstd"], upto("mix_rstd", l, i + 1))
                    dve.scalar_tensor_tensor(tmix[:, i % 2, :], pair(i % 2), ST[:, 3, i:i + 1], ROW[:, s, :],
                                             ALU.mult, ALU.mult).then_inc(free[i % 2], 1)
                    dve.wait_ge(*drained_at(l, "mix", i))
                    dve.tensor_tensor(X[:, i, :], X[:, i, :], tmix[:, i % 2, :], ALU.add).then_inc(S["x_mid"], 1)

                def h_rows(i):
                    s = 0 if i < LT else 1
                    dve.wait_ge(S["x2_rstd"], upto("x2_rstd", l, i + 1))
                    if i >= 2:
                        dve.wait_ge(*filled_at(l, "h2T", i - 2))
                        dve.wait_ge(S[f"h_sent{i % 2}"], upto(f"h_sent{i % 2}", l, 16 * (i // 2)))
                    dve.scalar_tensor_tensor(hrow[:, i % 2, :], X[:, i, :], ST[:, 5, i:i + 1], ROW[:, 2 + s, :],
                                             ALU.mult, ALU.mult).then_inc(S["h_scaled"], 1)
                    dve.wait_ge(S["h_scaled"], upto("h_scaled", l, i + 1))
                    dve.tensor_tensor(hrow[:, i % 2, :], hrow[:, i % 2, :], ROW[:, 4 + s, :], ALU.add)\
                       .then_inc(S["h_ready"], 1)

                dve.wait_ge(S["rows_ready"], upto("rows_ready", l, 16))
                for i in range(NT):
                    mixed(i)
                    h_rows(i)
                L = cut(R, 10240, (NT, NR))
                sc1, mask, m1, m2, oh1, oh2 = rt[2], rt[3], rt[4], rt[5], rt[6], rt[7]
                dve.tensor_copy(IOTA[:, 0:NE], CON[:, C_EID:C_EID + NE])
                dve.tensor_scalar(IOTA[:, NE:BLK], CON[:, C_EID:C_EID + NE], float(NE), None, ALU.add)
                link(l, dve.tensor_scalar(ID1, TID[:, :, :], 1.0, None, ALU.add))
                CUM = cut(R, 10240 + 160 * 8, (NT + 1, NE))
                rev, eid = CON[:, C_REV:C_REV + NE], CON[:, C_EID:C_EID + NE]
                dve.wait_ge(*filled_at(l, "lg", 0))
                dve.tensor_tensor(L, PS[:, 6, 0:NT * NR].rearrange("p (t n) -> p t n", n=NR),
                                  bc(RB[:, :], 1, (NT, NR)), ALU.add).then_inc(free[3], 1)
                dve.wait_ge(*drained_at(l, "lg", 0))

                def first_best(vals, best, n, out, tmp):
                    link(l, dve.tensor_reduce(best, vals, AX.X, ALU.max))
                    link(l, dve.tensor_tensor(tmp, vals, bc(best, 2, (NT, n)), ALU.is_equal))
                    link(l, dve.tensor_tensor(tmp, tmp, bc(rev[:, 0:n], 1, (NT, n)), ALU.mult))
                    link(l, dve.tensor_reduce(RS[:, 7, :], tmp, AX.X, ALU.max))
                    link(l, dve.tensor_tensor(out, tmp, bc(RS[:, 7, :], 2, (NT, n)), ALU.is_equal))

                g_oh, g_tmp = mask[:, :, 0:NG], sc1[:, :, 0:NG]
                first_best(L[:, :, 0:NG], RS[:, 0, :], NG, g_oh, g_tmp)
                dve.tensor_tensor(EX[:, 0, :, 0:NG], L[:, :, 0:NG], bc(RS[:, 0, :], 2, (NT, NG)), ALU.subtract)
                link(l, dve.tensor_scalar(g_tmp, g_oh, 1.0, BIG, ALU.subtract, ALU.mult))
                for i in range(NT):
                    ins = dve.tensor_tensor(m1[:, i, :].rearrange("p (g e) -> p g e", g=NG),
                                            L[:, i, NG:NR].rearrange("p (g e) -> p g e", g=NG),
                                            bc(g_tmp[:, i, :], 2, (NG, EPG)), ALU.add)
                link(l, ins)
                first_best(m1, RS[:, 2, :], NE, oh1, sc1)
                link(l, dve.scalar_tensor_tensor(m2, oh1, -2 * BIG, m1, ALU.mult, ALU.add))
                first_best(m2, RS[:, 3, :], NE, oh2, sc1)
                dve.tensor_tensor(EX[:, 0, :, 4], RS[:, 3, :], RS[:, 2, :], ALU.subtract).then_inc(S["sel_in"], 1)
                dve.memset(CUM[:, 0, :], 0.0)
                link(l, dve.tensor_tensor(mask, oh1, oh2, ALU.add))
                for i in range(NT):
                    ins = dve.tensor_tensor(CUM[:, i + 1, :], CUM[:, i, :], mask[:, i, :], ALU.add)
                    if i < NT - 1:
                        link(l, ins)
                ins.then_inc(S["mask_ready"], 1)
                dve.wait_ge(S["sel_exp"], upto("sel_exp", l, 1))
                link(l, dve.tensor_reduce(RS[:, 1, :], EX[:, 1, :, 0:NG], AX.X, ALU.add))
                link(l, dve.scalar_tensor_tensor(RS[:, 4, :], EX[:, 1, :, 4], 1.0, RS[:, 1, :], ALU.add, ALU.mult))
                link(l, dve.reciprocal(RS[:, 5, :], RS[:, 4, :]))
                link(l, dve.tensor_tensor(RS[:, 6, :], RS[:, 5, :], EX[:, 1, :, 4], ALU.mult))
                dve.wait_ge(*filled_at(l, "pos", 0))
                link(l, dve.tensor_copy(m1, PS[:, 0, 0:NT * NE].rearrange("p (t n) -> p t n", n=NE)))
                for k, oh in enumerate((oh1, oh2)):
                    at = (sc1, m2)[k]
                    link(l, dve.tensor_tensor(at, oh, m1, ALU.mult))
                    link(l, dve.tensor_reduce(RS[:, 2 + k, :], at, AX.X, ALU.add))
                    dve.tensor_tensor(OHP[:, k], bc(IOTA, 1, (NT, BLK)), bc(RS[:, 2 + k, :], 2, (NT, BLK)), ALU.is_equal)
                    ins = dve.tensor_tensor(OHE[:, k], oh, bc(ID1[:, k], 2, (NT, NE)), ALU.mult)
                ins.then_inc(S["onehots"], 1)
                link(l, dve.tensor_reduce(RS[:, 0, 0:1], PS[:, 1, 0:NE], AX.X, ALU.max))
                dve.tensor_copy(MOST[:, :], RS[:, 0, 0:1]).then_inc(free[0], 1)
                for k, oh in enumerate((oh1, oh2)):
                    link(l, dve.tensor_tensor(oh, oh, bc(eid, 1, (NT, NE)), ALU.mult))
                    link(l, dve.tensor_reduce(RS[:, 7, :], oh, AX.X, ALU.add))
                    ins = dve.scalar_tensor_tensor(SLOT[:, k, :], RS[:, 2 + k, :], float(NE), RS[:, 7, :], ALU.mult, ALU.add)
                    if k == 0:
                        link(l, ins)
                ins.then_inc(S["slots_ready"], 1)
                dve.wait_ge(*filled_at(l, "ids", 0))
                ids = PS[:, 2, 0:NE]
                link(l, dve.tensor_scalar(AIDS[:, 0, :], ids, 0.0, 2.0 * TOK + 1.0, ALU.is_equal, ALU.mult))
                link(l, dve.scalar_tensor_tensor(AIDS[:, 1, :], ids, -1.0, AIDS[:, 0, :], ALU.add, ALU.add))
                dve.sem_inc(free[1], 1)
                dve.tensor_scalar(IDX[:, 2, 0:NE], AIDS[:, 1, :], 2.0, CON[:, C_HALF:C_HALF + 1], ALU.mult, ALU.add)
                link(l, dve.tensor_scalar(AIDS[:, 2, :], AIDS[:, 1, :], float(TOK), -float(TOK), ALU.is_ge, ALU.mult))
                dve.tensor_tensor(IDX[:, 1, 0:NE], AIDS[:, 2, :], AIDS[:, 1, :], ALU.add).then_inc(S["ids_ready"], 1)
                with dve.Fori(0, NE // 2) as it:
                    n = (l * (NE // 2) + it) * 2
                    for e in range(2):
                        dve.wait_ge(gu_full, n + e + 3)
                        dve.wait_ge(gt_full, n + e + 1)
                        dve.tensor_copy(GU[:, e, :], PS[:, 2 + e, 0:FF]).then_inc(gu_out, 1)
                        dve.wait_ge(th_out, n + e + 1)
                        gt = bank(4 + e)[:, 0:256].rearrange("p (c t) -> p c t", c=2)
                        dve.scalar_tensor_tensor(sg, th, 1.0, gt[:, :, 0:BLK], ALU.add, ALU.mult).then_inc(sg_out, 1)
                        dve.wait_ge(sg_out, n + e + 1)
                        dve.wait_ge(dn_full, n + e + 1)
                        dve.tensor_tensor(hE[:, e], sg, gt[:, :, BLK:P], ALU.mult).then_inc(h_out, 1)

                def more_dve(b, e, n):
                    dve.wait_ge(f_gu, n + 1)
                    dve.tensor_copy(GU[:, 0, :], PS[:, 2, 0:FF]).then_inc(f_go, 1)
                    dve.wait_ge(f_th, n + 1)
                    gt = bank(4)[:, 0:256].rearrange("p (c t) -> p c t", c=2)
                    dve.scalar_tensor_tensor(sg, th, 1.0, gt[:, :, 0:BLK], ALU.add, ALU.mult).then_inc(f_sg, 1)
                    dve.wait_ge(f_sg, n + 1)
                    dve.tensor_tensor(hE[:, 0], sg, gt[:, :, BLK:P], ALU.mult).then_inc(f_h, 1)

                further_blocks(dve, l, more_dve, [(f_go, 1), (f_sg, 1), (f_h, 1)])
                for i in range(NT + 1):
                    if i < NT:
                        dve.wait_ge(S["y_scaled"], upto("y_scaled", l, i + 1))
                        y = yg[i]
                        dve.scalar_tensor_tensor(y[:, 0, :], y[:, 1, :], RS[:, 6, i:i + 1], y[:, 0, :], ALU.mult, ALU.add)\
                           .then_inc(S["y_sum"], 1)
                        dve.wait_ge(S["y_sum"], upto("y_sum", l, i + 1))
                    if i:
                        j = i - 1
                        s = 0 if j < LT else 1
                        y = yg[j]
                        dve.wait_ge(S["y_rstd"], upto("y_rstd", l, i))
                        link(l, dve.scalar_tensor_tensor(y[:, 1, :], y[:, 0, :], ST[:, 3, j:j + 1], ROW[:, 6 + s, :],
                                                         ALU.mult, ALU.mult))
                        dve.tensor_tensor(X[:, j, :], X[:, j, :], y[:, 1, :], ALU.add).then_inc(S["x_end"], 1)

        @block.tensor
        def _(pe):
            pe.wait_ge(const_in, 32)
            pe.wait_ge(silu_b, 3)
            mm, tp = nc.tensor.matmul, nc.tensor.transpose

            with pe.Fori(0, DEPTH) as l:

                def slot(name, i, k=DK):
                    s, _ = chunk(name, i)
                    return W[:, s, :].rearrange("p (k n) -> p k n", k=k)

                def both_streams(p, lhsT, rhs, start, stop):
                    mm(pair(p)[:, 0:LAT], lhsT, rhs[:, 0:LAT], start=start, stop=stop)
                    return mm(pair(p)[:, LAT:TOK], lhsT, rhs[:, LAT:TOK], start=start, stop=stop)

                def ada_products(c):
                    p = pair_of("ada", c)
                    pe.wait_ge(*freed_at(l, "ada", c))
                    pe.wait_ge(*loaded_at(l, "ada", c))
                    w = slot("ada", c)
                    for k in range(DK):
                        j = k % 4
                        ins = mm(PS[32 * j:32 * j + 32, 2 * p, :], SILU[:, k, :], w[:, k, :], start=k < 4, stop=k >= 4)
                    ins.then_inc(full[p], 1)

                def ada_cols(c):
                    pe.wait_ge(*drained_at(l, "ada", c))
                    for k in range(4):
                        ins = mm(PS[:, 2 * pair_of("ada", c) + 1, 2 * k:2 * k + 2], part[part_of(c)][:, P * k:P * k + P],
                                 CON[:, C_SEL:C_SEL + 2], start=True, stop=True)
                    ins.then_inc(S["ada_cols"], 1)

                for c in range(EARLY - 1):
                    ada_products(c)
                for c in range(EARLY - 1):
                    ada_cols(c)
                ada_products(EARLY - 1)
                ada_cols(EARLY - 1)
                pe.wait_ge(S["xn_ready"], upto("xn_ready", l, NT))
                for k in range(DK):
                    p = pair_of("hT", k)
                    pe.wait_ge(*freed_at(l, "hT", k))
                    for i in range(NT):
                        ins = tp(pair(p)[:, P * i:P * i + P], xn[:, i, P * k:P * k + P], ident)
                    ins.then_inc(full[p], 1)
                for k in range(4, DK):
                    pe.wait_ge(*drained_at(l, "hT", k))

                def qkT(i):
                    p = pair_of("qkT", i)
                    pe.wait_ge(*freed_at(l, "qkT", i))
                    if i < NT:
                        pe.wait_ge(S["qk_rot"], upto("qk_rot", l, i + 1))
                        for j in range(5):
                            ins = tp(pair(p)[:, P * j:P * j + P], qrot[:, i % 2, P * j:P * j + P], ident)
                    else:
                        pe.wait_ge(S["layer_in"], upto("layer_in", l, per["layer_in"]))
                        ins = tp(PS[:, 2 * p + 1, 0:P], kc, ident)
                    ins.then_inc(full[p], 1)

                for i in range(NT):
                    p = pair_of("qkv", i)
                    pe.wait_ge(*freed_at(l, "qkv", i))
                    for n, name in enumerate(("q", "kvx")):
                        pe.wait_ge(*loaded_at(l, name))
                        for k in range(DK):
                            ins = mm(bank(2 * p + n), hT[:, k, P * i:P * i + P], slot(name, 0)[:, k, :],
                                     start=k == 0, stop=k == DK - 1)
                    ins.then_inc(full[p], 1)
                    if i:
                        qkT(i - 1)
                for c in range(2):
                    pe.wait_ge(*freed_at(l, "xp", c))
                    pe.wait_ge(*loaded_at(l, "xp"))
                    w = W[:, chunk("xp")[0], 0:2048].rearrange("p (k n) -> p k n", k=DK)
                    for k in range(DK):
                        ins = both_streams(c, w[:, k, P * c:P * c + P], hT[:, k, :], k == 0, k == DK - 1)
                    ins.then_inc(full[c], 1)
                    if c == 0:
                        qkT(NT - 1)
                        qkT(NT)
                pe.wait_ge(*drained_at(l, "qkv", NT - 1))
                pe.wait_ge(*drained_at(l, "qkv", NT - 2))
                for j in range(4):
                    c, f = j % 2, j // 2
                    p = pair_of("dft", j)
                    pe.wait_ge(*freed_at(l, "dft", j))
                    name = ("cos", "sin")[f]
                    pe.wait_ge(*loaded_at(l, name))
                    w = W[:, chunk(name)[0], 0:2048].rearrange("p (k n) -> p k n", k=LT)
                    for k in range(LT):
                        ins = mm(bank(2 * p), XF[:, k, P * c:P * c + P], w[:, k, :], start=k == 0, stop=k == LT - 1)
                    mm(PS[:, 2 * p + 1, 0:P], XF[:, LT, P * c:P * c + P], cols(C_XC if f == 0 else C_XS),
                       start=True, stop=True).then_inc(full[p], 1)
                for c in range(2):
                    p = pair_of("plin", c)
                    pe.wait_ge(*freed_at(l, "plin", c))
                    pe.wait_ge(S["pooled"], upto("pooled", l, c + 1))
                    both_streams(p, WPG[:, c, :], pooled[:, c, :], True, True).then_inc(full[p], 1)
                for c in range(2):
                    p = pair_of("four", c)
                    pe.wait_ge(*freed_at(l, "four", c))
                    pe.wait_ge(*drained_at(l, "dft", c))
                    both_streams(p, cols(C_CC), AB[:, c, :], True, False)
                    pe.wait_ge(*drained_at(l, "dft", 2 + c))
                    both_streams(p, cols(C_CS), AB[:, 2 + c, :], False, True).then_inc(full[p], 1)

                pe.wait_ge(*drained_at(l, "qkT", NT - 1))
                pe.wait_ge(*drained_at(l, "qkT", NT))
                for what, x in STEPS:
                    if what == "ada":
                        ada_products(x)
                    elif what == "adacol":
                        ada_cols(x)
                    elif what == "gates":
                        g, nth = x
                        p = pair_of("gate", g)
                        if nth == 0:
                            pe.wait_ge(*freed_at(l, "gate", g))
                            pe.wait_ge(*loaded_at(l, "gate", g // 4))
                        w = slot("gate", g // 4)
                        for k in range(DK // PARTS * nth, DK // PARTS * (nth + 1)):
                            ins = both_streams(p, w[:, k, P * (g % 4):P * (g % 4) + P], hT[:, k, :], k == 0, k == DK - 1)
                        if nth == PARTS - 1:
                            ins.then_inc(full[p], 1)
                    elif what == "ctxS":
                        pe.wait_ge(*freed_at(l, "ctxS", 0))
                        for h in range(NH):
                            ins = mm(pair(2)[:, P * h:P * h + P], qT[:, h % 4, LAT:TOK], kT[:, h // 4, KEYS:KALL],
                                     start=True, stop=True)
                        ins.then_inc(full[2], 1)
                    elif what == "ctxT":
                        pe.wait_ge(*freed_at(l, "ctxT", 0))
                        pe.wait_ge(S["cpn"], upto("cpn", l, 1))
                        for h in range(NH):
                            ins = tp(pair(3)[:, P * h:P * h + P], cP[:, h, :], ident)
                        ins.then_inc(full[3], 1)
                    elif what == "ctxO":
                        pe.wait_ge(*freed_at(l, "ctxO", 0))
                        pe.wait_ge(*drained_at(l, "ctxT", 0))
                        for h in range(NH):
                            s, j = h // 4, h % 4
                            ins = mm(PS[HD * s:HD * s + HD, 4, P * j:P * j + P], V[:, NT, HD * s:HD * s + HD], cPT[:, h, :],
                                     start=True, stop=True)
                        ins.then_inc(full[2], 1)
                    elif what == "S":
                        h, t = x
                        pe.wait_ge(*freed_at(l, "S", x))
                        q = qT[:, h % 4, P * t:P * t + P]
                        mm(bank(4), q, kT[:, h // 4, 0:512], start=True, stop=True)
                        mm(PS[:, 5, 0:P], q, kT[:, h // 4, 512:KEYS], start=True, stop=True).then_inc(full[2], 1)
                    elif what == "T":
                        h, kt = x
                        if kt == 0:
                            pe.wait_ge(S["pnorm"], upto("pnorm", l, LT * (h + 1)))
                        for t in range(LT):
                            ins = tp(bank((6, 4)[kt % 2])[:, P * t:P * t + P], PR[:, t, P * kt:P * kt + P], ident)
                        ins.then_inc(S["tr_full"], 1)
                    elif what == "O":
                        h, kt = x
                        s, n = h // 4, 5 * h + kt
                        if kt == 0 and h:
                            pe.wait_ge(S["o_ready"], upto("o_ready", l, h))
                        pe.wait_ge(S[f"ptT{n % 2}"], upto(f"ptT{n % 2}", l, n // 2 + 1))
                        ins = mm(PS[HD * s:HD * s + HD, 7, :], V[:, kt, HD * s:HD * s + HD], PT[:, n % 2, :],
                                 start=kt == 0, stop=kt == 4)
                        if kt == 4:
                            ins.then_inc(S["pv_full"], 1)
                pe.wait_ge(S["o_ready"], upto("o_ready", l, NH))
                pe.wait_ge(*drained_at(l, "plin", 1))
                pe.wait_ge(*drained_at(l, "four", 1))
                pe.wait_ge(*freed_at(l, "vecT", 0))
                pe.wait_ge(S["vecs_ready"], upto("vecs_ready", l, 1))
                pe.sem_inc(aside, 1)
                tp(PS[0:64, 0, 0:P], VCOL.rearrange("p n s k -> p (n s k)"), ident).then_inc(full[0], 1)
                for d in range(DK):
                    at = slice(P * d, P * d + P)
                    pf = W[:, chunk("pf")[0], :].rearrange("p (w k n) -> p w k n", w=2, k=2)
                    for name, src, n in (("mattn", OT, 4), ("mpool", PM, 2), ("mfour", FM, 2)):
                        p = pair_of(name, d)
                        pe.wait_ge(*freed_at(l, name, d))
                        pe.wait_ge(*loaded_at(l, "ao" if n == 4 else "pf"))
                        w = slot("ao", 0, 4) if n == 4 else pf[:, 0 if name == "mpool" else 1]
                        for k in range(n):
                            ins = both_streams(p, w[:, k, at], src[:, k, :], k == 0, k == n - 1)
                        ins.then_inc(full[p], 1)
                def h2T(i):
                    p = pair_of("h2T", i)
                    pe.wait_ge(*freed_at(l, "h2T", i))
                    pe.wait_ge(S["h_ready"], upto("h_ready", l, i + 1))
                    for k in range(DK):
                        ins = tp(pair(p)[:, P * k:P * k + P], hrow[:, i % 2, P * k:P * k + P], ident)
                    ins.then_inc(full[p], 1)

                def logits(i):
                    if i == 0:
                        pe.wait_ge(*freed_at(l, "lg", 0))
                        pe.wait_ge(S["wr_in"], upto("wr_in", l, 16))
                    pe.wait_ge(*drained_at(l, "h2T", i))
                    for k in range(DK):
                        ins = mm(PS[:, 6, NR * i:NR * i + NR], hT[:, k, P * i:P * i + P], WR[:, k, :],
                                 start=k == 0, stop=k == DK - 1)
                    return ins

                pe.wait_ge(S["merged"], upto("merged", l, DK))
                for i in range(NT):
                    p = i % 2
                    pe.wait_ge(*freed_at(l, "mix", i))
                    for n in range(2):
                        pe.wait_ge(*loaded_at(l, "wo", n))
                        for k in range(DK):
                            ins = mm(bank(2 * p + n), hT[:, k, P * i:P * i + P], slot("wo", n)[:, k, :],
                                     start=k == 0, stop=k == DK - 1)
                    ins.then_inc(full[p], 1)
                    if i:
                        h2T(i - 1)
                    if i >= 2:
                        logits(i - 2)
                logits(NT - 2)
                h2T(NT - 1)
                logits(NT - 1).then_inc(full[3], 1)
                pe.wait_ge(*freed_at(l, "pos", 0))
                pe.wait_ge(S["mask_ready"], upto("mask_ready", l, 1))
                flat = slice(0, NT * NE)
                cum = cut(R, 10240 + 160 * 8, (NT * NE + NE,))
                mm(PS[:, 0, flat], tri, rt[3].rearrange("p t n -> p (t n)"), start=True, stop=False)
                mm(PS[:, 0, flat], ones, cum[:, flat], start=False, stop=True)
                mm(PS[:, 1, 0:NE], ones, cum[:, NT * NE:], start=True, stop=True).then_inc(full[0], 1)

                pe.wait_ge(*freed_at(l, "ids", 0))
                pe.wait_ge(S["onehots"], upto("onehots", l, 1))
                for half in range(2):
                    for j in range(2 * NT):
                        ins = mm(PS[BLK * half:BLK * half + BLK, 2, 0:NE], OHP[:, j // NT, j % NT, :],
                                 OHE[:, j // NT, j % NT, :], start=j == 0, stop=j == 2 * NT - 1)
                ins.then_inc(full[1], 1)

                def transpose_rows(e):
                    rows = xg[0:BLK, e, :].rearrange("p (f k) -> p k f", k=DK)
                    for k in range(DK):
                        ins = tp(bank(e)[:, BLK * k:BLK * k + BLK], rows[:, k, :], ident[0:BLK, 0:BLK])
                    return ins

                def gate_up_products(e, ws):
                    for k in range(DK):
                        for u in range(2):
                            ins = mm(PS[BLK * u:BLK * u + BLK, 2 + e, 0:FF], xT[:, e, k, :], wgu[ws][:, u, k, :],
                                     start=k == 0, stop=k == DK - 1)
                    return ins

                def transpose_gate_up(e):
                    v = GU[:, e, :].rearrange("p (f c) -> p c f", c=2)
                    for c in range(2):
                        ins = tp(bank(4 + e)[:, P * c:P * c + P], v[:, c, :], ident)
                    return ins

                def down_products(e, ws):
                    for c in range(2):
                        for h in range(2):
                            ins = mm(PS[BLK * h:BLK * h + BLK, 6 + e, :], hE[:, e, c, :],
                                     wdn[ws][:, c, 512 * h:512 * h + 512], start=c == 0, stop=c == 1)
                    return ins

                for p in range(4):
                    pe.wait_ge(free[p], (l + 1) * PAIRS.free[p] + 1)
                pe.sem_inc(aside, 1)
                def rows_T(it, c):
                    m, e = l * NE + it * ESLOTS + c, c % 2
                    pe.wait_ge(rows_in[e], (l * (NE // 2 + 1) + it * (ESLOTS // 2) + c // 2 + 1) * 16)
                    pe.wait_ge(xT_out, m + 1)
                    pe.sem_inc(aside, 1)
                    transpose_rows(e).then_inc(xT_full, 1)

                def gate_up(it, c):
                    m, e = l * NE + it * ESLOTS + c, c % 2
                    ws, turn = weights_of(l, it, c)
                    pe.wait_ge(xT_out, m + 3)
                    pe.wait_ge(ex_loaded[ws], turn * 32)
                    pe.wait_ge(gu_out, m + 1)
                    gate_up_products(e, ws).then_inc(gu_full, 1)

                def gu_T(it, c):
                    m, e = l * NE + it * ESLOTS + c, c % 2
                    pe.wait_ge(gu_out, m + 3)
                    pe.wait_ge(h_out, m + 1)
                    transpose_gate_up(e).then_inc(gt_full, 1)

                def down(it, c):
                    m, e = l * NE + it * ESLOTS + c, c % 2
                    ws, turn = weights_of(l, it, c)
                    pe.wait_ge(h_out, m + 3)
                    pe.wait_ge(dn_loaded[ws], turn * 16)
                    pe.wait_ge(y_out, m + 1)
                    down_products(e, ws).then_inc(dn_full, 1)

                def steps(it, c):
                    gate_up(it, c)
                    if not (isinstance(it, int) and c == NE - 1):
                        rows_T(it, c + 1)
                    if not (isinstance(it, int) and c == 0):
                        down(it, c - 1)
                    gu_T(it, c)

                first = ESLOTS + 3
                rows_T(0, 0)
                for c in range(first):
                    steps(0, c)
                with pe.Fori(0, (NE - 1 - first) // ESLOTS) as it:
                    for c in range(first, first + ESLOTS):
                        steps(it, c)
                steps(0, NE - 1)
                down(0, NE - 1)
                for s in (xT_out, gu_out, h_out, y_out):
                    pe.wait_ge(s, (l + 1) * NE + 2)

                def more_pe(b, e, n):
                    pe.wait_ge(f_rows, n + 1)
                    pe.sem_inc(aside, 1)
                    transpose_rows(0).then_inc(f_xT, 1)
                    pe.wait_ge(f_xo, n + 1)
                    pe.wait_ge(f_loaded, 48 * n + 48)
                    gate_up_products(0, 0).then_inc(f_gu, 1)
                    pe.wait_ge(f_go, n + 1)
                    transpose_gate_up(0).then_inc(f_gt, 1)
                    pe.wait_ge(f_h, n + 1)
                    down_products(0, 0).then_inc(f_dn, 1)

                further_blocks(pe, l, more_pe, [(f_xT, 1), (f_gu, 1), (f_gt, 1), (f_dn, 1)])
                pe.wait_ge(f_y, (l + 1) * XBLK * NE)

        for name, n in count.items():
            assert n == per[name], (name, n)


STEPS_PER_LAYER = dict(dve_step=149, act_step=1, pool_step=20)


def host_constants(np):
    con = np.zeros((P, NCONST), np.float64)
    con[:, C_ID:C_ID + P] = np.eye(P)
    con[:, C_ONE:C_ONE + P] = 1
    con[:, C_TRI:C_TRI + P] = np.triu(np.ones((P, P)), 1)

    def dft(n):
        a = 2 * np.pi * (np.outer(np.arange(n), np.arange(n)) % n) / n
        return np.cos(a) / np.sqrt(n), np.sin(a) / np.sqrt(n)

    cc, cs = dft(HD)
    for h in range(2):
        at = slice(HD * h, HD * h + HD)
        con[at, C_CC + HD * h:C_CC + HD * h + HD] = cc
        con[at, C_CS + HD * h:C_CS + HD * h + HD] = -cs
    con[:, C_XC:C_XC + P], con[:, C_XS:C_XS + P] = dft(CTX)
    for c in range(2):
        for h in range(2):
            w = (2, 4, 8, 16)[2 * c + h]
            at = slice(HD * h, HD * h + HD)
            con[at, C_WINV + c] = 1 / w
            t = np.arange(8)
            con[at, C_EDGE + c * 8:C_EDGE + c * 8 + 8] = w / np.minimum(w, t + w // 2)
            con[at, C_EDGE + (2 + c) * 8:C_EDGE + (2 + c) * 8 + 8] = w / np.minimum(w, 8 - t + w // 2)
    con[:, C_EID:C_EID + NE] = np.arange(NE)
    con[BLK:, C_HALF] = 1
    con[:, C_REV:C_REV + NE] = NE - np.arange(NE)
    for j in range(4):
        for s in range(2):
            con[32 * j + s, C_SEL + s] = 1
    f = np.float32
    t = np.arange(LAT)
    inv = (f(10000.0) ** (-np.arange(16, dtype=f) * f(2.0) / f(32))).astype(f)
    rope = np.zeros((P, 2, LT, HD), f)
    for a, pos in enumerate((t // 64, t % 64)):
        ang = (pos.astype(f)[:, None] * inv).astype(f)
        c, s = (np.cos(ang.astype(np.float64)).reshape(LT, P, 16).transpose(1, 0, 2),
                np.sin(ang.astype(np.float64)).reshape(LT, P, 16).transpose(1, 0, 2))
        for h in range(2):
            rope[:, 0, :, 32 * a + 16 * h:32 * a + 16 * h + 16] = c
            rope[:, 1, :, 32 * a + 16 * h:32 * a + 16 * h + 16] = s if h else -s
    return {
        "consts": con.astype(f), "rope": rope.reshape(P, -1), "dft": np.stack(dft(LAT)).astype(f),
        "token_ids": np.arange(2 * TOK, dtype=np.int32).reshape(2, NT, P).transpose(2, 0, 1).copy(),
        "table_init": np.full((P, TOK * NE // P), 2 * TOK, np.int32),
    }


def kernel(**inputs):
    import numpy as np
    import concourse.bacc as _bacc
    from concourse.bass_utils import run_bass_kernel_spmd as _run

    x = {k: np.asarray(v) for k, v in inputs.items()}

    def columns(v):
        return v.reshape(DEPTH, -1, P).transpose(0, 2, 1)

    arrays = host_constants(np)
    for k in ("x_prompt", "x_sample", "cache_k", "cache_v", "w_ada", "w_in", "w_attn_out", "w_pool_group",
              "w_pool_out", "w_fourier_out", "w_out", "w_expert_gate", "w_expert_up", "w_expert_down"):
        arrays[k] = np.ascontiguousarray(x[k])
    arrays["vecs"] = np.ascontiguousarray(np.concatenate([columns(x[k]) for k in (
        "b_ada", "norm_mix_pre", "norm_mix_post", "norm_ffn_pre", "norm_ffn_post", "pool_scale")], axis=2))
    arrays["c_cols"] = np.ascontiguousarray(np.stack([x["c"][0].reshape(DK, P).T, x["c_ctx"].reshape(DK, P).T], axis=2))
    arrays["gains"] = np.ascontiguousarray(np.broadcast_to(np.concatenate(
        [x["q_norm"]] * NH + [x["k_norm"]] * NKV, axis=1)[:, None, :], (DEPTH, P, NHEADS * HD)))
    arrays["router_b"] = np.ascontiguousarray(np.broadcast_to(np.concatenate(
        [x["b_router_group"], x["b_router_expert"]], axis=1)[:, None, :], (DEPTH, P, NR)))
    arrays["w_router"] = np.ascontiguousarray(np.concatenate([x["w_router_group"], x["w_router_expert"]], axis=2))

    nc = _bacc.Bacc("TRN2", target_bir_lowering=False, num_devices=1)
    A = {}
    for k, v in arrays.items():
        A[k] = nc.dram_tensor("in_" + k, v.shape, mybir.dt.from_np(v.dtype), kind="ExternalInput").ap()
    outs = [("out_p", (1, CTX, D)), ("out_s", (1, LAT, D)), ("out_k", (1, DEPTH, CTX, NKV, HD)),
            ("out_v", (1, DEPTH, CTX, NKV, HD))]
    for k, shape in outs:
        A[k] = nc.dram_tensor(k, shape, F32, kind="ExternalOutput").ap()
    A["h_rows"] = nc.dram_tensor("h_rows", (TOK, D), F32, kind="Internal").ap()
    A["vec_rows"] = nc.dram_tensor("vec_rows", (8, D), F32, kind="Internal").ap()
    A["y_half_rows"] = nc.dram_tensor("y_half_rows", (4 * TOK, D // 2), F32, kind="Internal").ap()
    A["table"] = nc.dram_tensor("table", (TOK * NE, 1), I32, kind="Internal").ap()
    trunk_kernel(nc, A, STEPS_PER_LAYER)
    r = _run(nc, [{"in_" + k: v for k, v in arrays.items()}], core_ids=[0])
    return tuple(r.results[0][k] for k, _ in outs)
```
